# Optimizing a Trainium2 kernel written in Bass

```python
import math
import jax, jax.numpy as jnp
from jax import lax
import numpy as np

D_MODEL = 1024
BATCH = 1
SEQ = 128
DEPTH = 2
DEC_BATCH = 1
DEC_SEQ = 512
PAST_LEN = 128

GRID_W = 64
D_MIX = D_MODEL
D_ATTN = D_MIX // 2
D_CONV = D_MIX - D_ATTN
N_HEADS = 4
HEAD_DIM = D_ATTN // (2 * N_HEADS)
V_DIM = 2 * HEAD_DIM
CONV_W = 3
D_FF = 2816
ROPE_BASE = 10000.0
EPS = 1e-6
Q_BLOCK = 128
N_MOD = 6
D_IN = 3 * D_ATTN + 3 * D_CONV
SPLITS = (D_ATTN, 2 * D_ATTN, 3 * D_ATTN, 3 * D_ATTN + D_CONV, 3 * D_ATTN + 2 * D_CONV)

kernel_name = 'hybrid_diffattn_shortconv_dit_step'

def _rmsnorm(x, g):
    xf = x.astype(jnp.float32)
    r = lax.rsqrt(jnp.mean(xf * xf, axis=-1, keepdims=True) + EPS)
    return (xf * r).astype(x.dtype) * g

def _dwconv3(u, w):
    up = jnp.pad(u, ((0, 0), (1, 1), (0, 0)))
    return up[:, :-2] * w[0] + up[:, 1:-1] * w[1] + up[:, 2:] * w[2]

def _grid_angles(n_tok):
    rows = n_tok // GRID_W
    row = jnp.repeat(jnp.arange(rows, dtype=jnp.float32), GRID_W)
    col = jnp.tile(jnp.arange(GRID_W, dtype=jnp.float32), rows)
    n_freq = HEAD_DIM // 4
    inv = ROPE_BASE ** (-jnp.arange(n_freq, dtype=jnp.float32) / n_freq)
    return row[:, None] * inv[None], col[:, None] * inv[None]

def _rot_axis(x, ang):
    half = x.shape[-1] // 2
    cos = jnp.cos(ang)[None, :, None, None, :].astype(x.dtype)
    sin = jnp.sin(ang)[None, :, None, None, :].astype(x.dtype)
    x1, x2 = x[..., :half], x[..., half:]
    return jnp.concatenate([x1 * cos - x2 * sin, x2 * cos + x1 * sin], axis=-1)

def _rope_2d(x, ang_row, ang_col):
    h = HEAD_DIM // 2
    return jnp.concatenate([_rot_axis(x[..., :h], ang_row), _rot_axis(x[..., h:], ang_col)], axis=-1)

def _diff_attention(q, k, v, lam):
    bsz, lq = q.shape[:2]
    nb = lq // Q_BLOCK
    qb = q.reshape(bsz, nb, Q_BLOCK, N_HEADS, 2, HEAD_DIM).transpose(1, 0, 2, 3, 4, 5)
    scale = HEAD_DIM ** -0.5

    def block(qblk):
        s = jnp.einsum('bqhsd,bkhsd->bhsqk', qblk, k).astype(jnp.float32) * scale
        p = jax.nn.softmax(s, axis=-1)
        a = p[:, :, 0] - lam * p[:, :, 1]
        return jnp.einsum('bhqk,bkhe->bqhe', a.astype(v.dtype), v)

    o = lax.map(block, qb)
    return o.transpose(1, 0, 2, 3, 4).reshape(bsz, lq, N_HEADS, V_DIM)

def setup_inputs(seed: int = 0) -> dict:
    key = jax.random.key(seed)
    ks = jax.random.split(key, 24)
    f32 = jnp.float32
    nrm = lambda k, shape, s: jax.random.normal(k, shape, f32) * s
    return {
        'x_prompt': nrm(ks[0], (BATCH, SEQ, D_MODEL), 1.0),
        'x_sample': nrm(ks[1], (DEC_BATCH, DEC_SEQ, D_MODEL), 1.0),
        'cache_k': nrm(ks[2], (DEC_BATCH, DEPTH, PAST_LEN, N_HEADS, 2, HEAD_DIM), 1.0),
        'cache_v': nrm(ks[3], (DEC_BATCH, DEPTH, PAST_LEN, N_HEADS, V_DIM), 1.0),
        'c': nrm(ks[4], (DEC_BATCH, D_MODEL), 1.0),
        'c_ctx': nrm(ks[5], (D_MODEL,), 1.0),
        'w_mod': nrm(ks[6], (DEPTH, D_MODEL, N_MOD * D_MODEL), D_MODEL ** -0.5),
        'b_mod': nrm(ks[7], (DEPTH, N_MOD * D_MODEL), 0.02),
        'norm1_g': 1.0 + nrm(ks[8], (DEPTH, D_MODEL), 0.02),
        'w_in': nrm(ks[9], (DEPTH, D_MODEL, D_IN), D_MODEL ** -0.5),
        'q_norm_g': 1.0 + nrm(ks[10], (DEPTH, HEAD_DIM), 0.02),
        'k_norm_g': 1.0 + nrm(ks[11], (DEPTH, HEAD_DIM), 0.02),
        'lambda_q1': nrm(ks[12], (DEPTH, HEAD_DIM), 0.1),
        'lambda_k1': nrm(ks[13], (DEPTH, HEAD_DIM), 0.1),
        'lambda_q2': nrm(ks[14], (DEPTH, HEAD_DIM), 0.1),
        'lambda_k2': nrm(ks[15], (DEPTH, HEAD_DIM), 0.1),
        'subln_g': 1.0 + nrm(ks[16], (DEPTH, V_DIM), 0.02),
        'conv_w': nrm(ks[17], (DEPTH, CONV_W, D_CONV), CONV_W ** -0.5),
        'conv_norm_g': 1.0 + nrm(ks[18], (DEPTH, D_CONV), 0.02),
        'w_out': nrm(ks[19], (DEPTH, D_MIX, D_MODEL), D_MIX ** -0.5),
        'norm2_g': 1.0 + nrm(ks[20], (DEPTH, D_MODEL), 0.02),
        'w_up': nrm(ks[21], (DEPTH, D_MODEL, 2 * D_FF), D_MODEL ** -0.5),
        'ffn_conv_w': nrm(ks[22], (DEPTH, CONV_W, 2 * D_FF), CONV_W ** -0.5),
        'w_down': nrm(ks[23], (DEPTH, D_FF, D_MODEL), D_FF ** -0.5),
    }

def reference(x_prompt, x_sample, cache_k, cache_v, c, c_ctx, w_mod, b_mod, norm1_g, w_in,
              q_norm_g, k_norm_g, lambda_q1, lambda_k1, lambda_q2, lambda_k2, subln_g,
              conv_w, conv_norm_g, w_out, norm2_g, w_up, ffn_conv_w, w_down):

    def layer(l, x, cvec, ctx_kv, ang):
        m = (jax.nn.silu(cvec) @ w_mod[l] + b_mod[l])[..., None, :]
        sh1, sc1, g1, sh2, sc2, g2 = jnp.split(m, N_MOD, axis=-1)
        h = _rmsnorm(x, norm1_g[l]) * (1 + sc1) + sh1
        bsz, n = x.shape[:2]
        q, k, v, bg, cg, xc = jnp.split(h @ w_in[l], SPLITS, axis=-1)
        q = _rmsnorm(q.reshape(bsz, n, N_HEADS, 2, HEAD_DIM), q_norm_g[l])
        k = _rmsnorm(k.reshape(bsz, n, N_HEADS, 2, HEAD_DIM), k_norm_g[l])
        v = v.reshape(bsz, n, N_HEADS, V_DIM)
        if ang is None:
            k_all, v_all = k, v
        else:
            q = _rope_2d(q, *ang)
            k = _rope_2d(k, *ang)
            k_all = jnp.concatenate([ctx_kv[0], k], axis=1)
            v_all = jnp.concatenate([ctx_kv[1], v], axis=1)
        lam_init = 0.8 - 0.6 * math.exp(-0.3 * l)
        f = lambda a: a.astype(jnp.float32)
        lam = (jnp.exp(jnp.sum(f(lambda_q1[l]) * f(lambda_k1[l])))
               - jnp.exp(jnp.sum(f(lambda_q2[l]) * f(lambda_k2[l]))) + lam_init)
        o = _diff_attention(q, k_all, v_all, lam)
        o = (_rmsnorm(o, subln_g[l]) * (1.0 - lam_init)).reshape(bsz, n, D_ATTN)
        y = _rmsnorm(bg * _dwconv3(cg * xc, conv_w[l]), conv_norm_g[l])
        x = x + g1 * (jnp.concatenate([o, y], axis=-1) @ w_out[l])
        h2 = _rmsnorm(x, norm2_g[l]) * (1 + sc2) + sh2
        a, b = jnp.split(_dwconv3(h2 @ w_up[l], ffn_conv_w[l]), 2, axis=-1)
        x = x + g2 * ((jax.nn.silu(a) * b) @ w_down[l])
        return x, k, v

    xp = x_prompt
    ks_new, vs_new = [], []
    for l in range(DEPTH):
        xp, k_l, v_l = layer(l, xp, c_ctx, None, None)
        ks_new.append(k_l)
        vs_new.append(v_l)
    y_prompt = xp
    new_k = jnp.stack(ks_new, axis=1)
    new_v = jnp.stack(vs_new, axis=1)

    ang = _grid_angles(x_sample.shape[1])
    xs = x_sample
    for l in range(DEPTH):
        xs, _, _ = layer(l, xs, c, (cache_k[:, l], cache_v[:, l]), ang)
    y_sample = xs

    return (y_prompt, y_sample, new_k, new_v)


_drawn_inputs = setup_inputs


def setup_inputs(seed=0):
    import zlib

    import numpy as np

    out = dict(_drawn_inputs(seed))
    spreads = {}
    factors = {'norm1_g': 2.932,
     'q_norm_g': 8.0,
     'lambda_q1': 3.171,
     'lambda_q2': 4.166,
     'lambda_k2': 5.615,
     'subln_g': 6.35,
     'conv_norm_g': 5.401,
     'norm2_g': 3.163}
    for name, (base, spread) in spreads.items():
        noise = np.random.default_rng([zlib.crc32(name.encode()), seed]).standard_normal(out[name].shape)
        drawn = base * np.exp(spread * noise) if base else spread * noise
        out[name] = __import__('jax').numpy.asarray(drawn.astype(out[name].dtype))
    for name, factor in factors.items():
        out[name] = (out[name] * factor).astype(out[name].dtype)
    return out
```

```python
import math
from contextlib import ExitStack

import concourse.bass as bass
import numpy as np
from concourse import mybir

F32 = mybir.dt.float32
F32R = mybir.dt.float32r
ALU = mybir.AluOpType
ACT = mybir.ActivationFunctionType
AX = mybir.AxisListType
ds = bass.ds

P = 128
D = 1024
KT = D // P
DEPTH = 2
SEQ, DEC, PAST = 128, 512, 128
NH, HD, VD = 4, 64, 128
D_ATTN = D_CONV = 512
D_IN = 3 * D_ATTN + 3 * D_CONV
FF = 2816
NMOD = 6
GRID_W = 64
EPS = 1e-6
SCALE = HD ** -0.5

T = 644
HALF = T // 2
C_PROMPT, C_SAMPLE = 1, 130
TOK_TILES = [C_PROMPT] + [C_SAMPLE + P * i for i in range(DEC // P)]
NT = len(TOK_TILES)
SEQS = [(C_PROMPT, SEQ, 0), (C_SAMPLE, DEC, 1)]
PIECES = [(C_PROMPT, SEQ, 0, C_PROMPT, 0), (C_SAMPLE, HALF - C_SAMPLE, 0, C_SAMPLE, 1),
          (HALF, C_SAMPLE + DEC - HALF, 1, 0, 1)]
N_KEY = PAST + DEC
K_PROMPT, K_PAST, K_SAMPLE = 0, SEQ, SEQ + PAST

UC = 256
SLOT = KT * UC
CHUNKS = [12, 10]
CH0 = [0, 12]
Q_U, C_U, O_U = 0, 6, 12
UP_U = [16, 36]
DN_U = [28, 46]
N_SPLIT = 54
SPLIT_SLOT = N_SPLIT // 2
MOD_PRE = 8
MOD_LAYER = 24
RAW_SLOT = (N_SPLIT + MOD_LAYER) // 2
RAW_PRE = MOD_PRE // 2
M1_RAW, M2_RAW, M3_RAW = 2, 22, 34


def raw_of(n):
    return n if n < 2 else n + 8 if n < 14 else n + 16 if n < 18 else n + 24


V_BMOD, V_N1, V_N2, V_CONV, V_CNG, V_SUB, V_FFN = 0, 48, 56, 64, 76, 80, 128
V_ROWS0 = 81
V_FT = 2 * FF // P
V_N = V_FFN + 3 * V_FT
ROUNDS = NH * NT
HALVES = 24
N_SMALL = 16
LAM_INIT = [0.8 - 0.6 * math.exp(-0.3 * i) for i in range(DEPTH)]


def hybrid_step(nc, x_prompt, x_sample, cache_k, cache_v, c_sample, c_ctx, w_mod, b_mod, norm1_g, w_in, q_norm_g,
                k_norm_g, lambda_q1, lambda_k1, lambda_q2, lambda_k2, subln_g, conv_w, conv_norm_g, w_out,
                norm2_g, w_up, ffn_conv_w, w_down, ident_in, rope_in, y_prompt, y_sample, new_k, new_v):
    ctx = ExitStack()
    with ctx:
        def sb(name, shape, dt=F32, scope=None):
            return (scope or ctx).enter_context(nc.sbuf_tensor(name, shape, dt))

        def sem(name):
            return ctx.enter_context(nc.semaphore(name))

        x = sb("x", [P, KT, T])
        h_hi = sb("h_hi", [P, KT, T], F32R)
        h_lo = sb("h_lo", [P, KT, T], F32R)
        raw = sb("raw", [P, 2, SLOT])
        w_hi = sb("w_hi", [P, 2, SLOT], F32R)
        w_lo = sb("w_lo", [P, 2, SLOT], F32R)
        rb = sb("rb", [P, T])
        ssq = sb("ssq", [P, T])
        sq = sb("sq", [P, T])
        tmp = sb("tmp", [P, 2, T])
        ident = sb("ident", [P, P])
        ones = sb("ones", [P, P])
        junk = sb("junk", [P, VD])
        rope = sb("rope", [P, 2, 4, HD])
        rope_q = sb("rope_q", [P, 2, 2, 4, HD])
        vecs = sb("vecs", [P, DEPTH, V_N])
        vl = sb("vl", [P, V_N])
        modv = sb("modv", [P, NMOD, KT, 2])
        gain = sb("gain", [P, KT, 2])
        cT = sb("cT", [P, KT, 2])
        mod_row = sb("mod_row", [2, D])
        qkg = sb("qkg", [P, 2, DEPTH, HD])
        qkg_l = sb("qkg_l", [P, 2, HD])
        neglam = sb("neglam", [P, DEPTH])
        neglam_l = sb("neglam_l", [P, 1])
        lam_s = sb("lam_s", [P, 4])
        eps = sb("eps", [P, 1])
        st8 = sb("st8", [P, 2, 8])
        mx = sb("mx", [P, 2, 2])
        nbias = sb("nbias", [P, 2, 2])
        sums = sb("sums", [P, 2, 2])
        rec = sb("rec", [P, 2, 2])
        ssq_o = sb("ssq_o", [P, ROUNDS])

        mix = ExitStack()
        qT = sb("qT", [P, NH, NT * P], scope=mix)
        kT = sb("kT", [P, NH, K_SAMPLE + DEC], scope=mix)
        v = sb("v", [P, 6, D_ATTN], scope=mix)
        cgb = sb("cgb", [P, 2, T], scope=mix)
        tap = tmp
        y = sb("y", [P, 4, T], scope=mix)
        prep = ExitStack()
        qraw = sb("qraw", [P, 2, D_ATTN], scope=prep)
        qn = sb("qn", [P, NT, D_ATTN], scope=prep)
        rt = sb("rt", [P, 2, D_ATTN], scope=prep)
        kc = sb("kc", [P, D_ATTN], scope=prep)
        prep.close()
        stage = ExitStack()
        xin = sb("xin", [P, NT, D], scope=stage)
        stage.close()
        setup = ExitStack()
        att = ExitStack()
        probs = sb("probs", [P, 2, 2, N_KEY], scope=att)
        aT = rb
        o = sb("o", [P, ROUNDS, VD], scope=att)
        att.close()
        mix.close()
        mlp = ExitStack()
        g_hi = sb("g_hi", [P, CHUNKS[0] * T], F32R, scope=mlp)
        g_lo = sb("g_lo", [P, CHUNKS[0] * T], F32R, scope=mlp)
        ub = sb("ub", [P, 2, T], scope=mlp)
        cen = tmp
        gt = sb("gt", [P, T], scope=mlp)
        mlp.close()
        vrow = sb("vrow", [P, DEPTH, 3, P], scope=setup)
        crow = sb("crow", [P, P], scope=setup)
        brow = sb("brow", [1, 768], scope=setup)
        lamb = sb("lamb", [P, 4, DEPTH, HD], scope=setup)
        lamp = sb("lamp", [P, 2, DEPTH, HD], scope=setup)
        setup.close()

        ps = ctx.enter_context(nc.psum_tensor("ps", [P, 8, 512], F32))
        scores = ps[:, 2:5, :].rearrange("p b n -> p (b n)")
        probsT = ps[:, 5:7, :].rearrange("p b n -> p (b n)")

        xf = x[:, :, :].rearrange("p t n -> p (t n)")
        mf = modv[:, :, :, :].rearrange("p v t s -> p (v t s)")

        raw_full = [sem("raw_full0"), sem("raw_full1")]
        hi_done = [sem("hi_done0"), sem("hi_done1")]
        split_full = [sem("split_full0"), sem("split_full1")]
        unit_done = [sem("unit_done0"), sem("unit_done1")]
        mod_used = sem("mod_used")
        row_read, modT_full, mod_ready = sem("row_read"), sem("modT_full"), sem("mod_ready")
        c_in, small_in, ffn_in, x_in, kv_in, out_done = (
            sem(s) for s in ("c_in", "small_in", "ffn_in", "x_in", "kv_in", "out_done"))
        bank3_first = sem("bank3_first")
        spacer = sem("spacer")
        sq_added, y_out = sem("sq_added"), sem("y_out")
        const_ready, silu_c, setup_full, setup_read = (sem("const_ready"), sem("silu_c"), sem("setup_full"),
                                                       sem("setup_read"))
        lam_ready, lam_exp, cT_ready = sem("lam_ready"), sem("lam_exp"), sem("cT_ready")
        xT_full, xT_read = sem("xT_full"), sem("xT_read")
        x_ready, sq_ready, ssq_ready = sem("x_ready"), sem("sq_ready"), sem("ssq_ready")
        stat_full, rms_ready = sem("stat_full"), sem("rms_ready")
        tmp_ready, hh_ready, h_ready = sem("tmp_ready"), sem("hh_ready"), sem("h_ready")
        qkv_full, qkv_read, qsq_ready, qsum_ready, qrms_ready, qk_ready, qkT_full, qkT_read, v_ready = (
            sem(s) for s in ("qkv_full", "qkv_read", "qsq_ready", "qsum_ready", "qrms_ready", "qk_ready",
                             "qkT_full", "qkT_read", "v_ready"))
        nk_out = sem("nk_out")
        conv_full, cg_read, xb_read = sem("conv_full"), sem("cg_read"), sem("xb_read")
        qk_full, max_ready, exp_done, a_ready, aT_full, aT_ready, pv_full, o_read = (
            sem(s) for s in ("qk_full", "max_ready", "exp_done", "a_ready", "aT_full", "aT_ready", "pv_full",
                             "o_read"))
        orms_ready, on_ready, oT_full, oT_hi, oT_read, mix_ready = (
            sem(s) for s in ("orms_ready", "on_ready", "oT_full", "oT_hi", "oT_read", "mix_ready"))
        out_full = sem("out_full")
        up_read, taps_ready, silu_ready, gm_ready, gh_ready, g_ready = (
            sem(s) for s in ("up_read", "taps_ready", "silu_ready", "gm_ready", "gh_ready", "g_ready"))
        dn_read = sem("dn_read")
        yT_full, yT_read = sem("yT_full"), sem("yT_read")

        block = ctx.enter_context(nc.Block())

        def done(l, n):
            return 1 + l * SPLIT_SLOT + n // 2 + 1

        def usable(l, n):
            return l * SPLIT_SLOT + n // 2 + 2

        def landed(l, r):
            return 32 * (RAW_PRE + 1) + l * (32 * RAW_SLOT) + 32 * (r // 2)

        def apart(eng):
            eng.sem_inc(spacer, 1)

        w_in_v = w_in.rearrange("l (t p) n -> p (l t) n", p=P)
        w_out_v = w_out.rearrange("l (t p) n -> p (l t) n", p=P)
        w_up_v = w_up.rearrange("l (t p) n -> p (l t) n", p=P)
        w_down_v = w_down.rearrange("l (t p) n -> p (l t) n", p=P)
        w_mod_v = w_mod.rearrange("l (t p) n -> p (l t) n", p=P)

        @block.sync
        def _(sp):
            def load(b, src, t0, tiles, cols, width):
                hf = tiles // 2
                dst = raw[:, b, 0:tiles * width].rearrange("p (t n) -> p t n", n=width)
                for s in range(2):
                    sp.dma_start(dst[:, s * hf:(s + 1) * hf, :],
                                 src[:, ds(t0 + s * hf, hf), ds(cols, width)]).then_inc(raw_full[b], 16)

            for u in range(MOD_PRE):
                if u >= 2:
                    sp.wait_ge(mod_used, u - 1)
                load(u % 2, w_mod_v, 0, KT, u * UC, UC)

            with sp.Fori(0, DEPTH) as l:
                def free_of_split(n):
                    sp.wait_ge(split_full[n % 2], usable(l, n))

                def free_of_mod(k):
                    sp.wait_ge(mod_used, l * MOD_LAYER + (MOD_PRE + k))

                def split_unit(n):
                    if n < C_U + 6:
                        if n < C_U:
                            col = n * UC
                        else:
                            pair, kind = divmod(n - C_U, 3)
                            col = 3 * D_ATTN + D_CONV * (1, 2, 0)[kind] + pair * UC
                        load(n % 2, w_in_v, l * KT, KT, col, UC)
                    else:
                        load(n % 2, w_out_v, l * KT, KT, (n - O_U) * UC, UC)

                def up_unit(b, j):
                    dst = raw[:, b, :].rearrange("p (s t n) -> p s t n", s=2, n=P)
                    for s in range(2):
                        sp.dma_start(dst[:, s, :, :], w_up_v[:, ds(l * KT, KT), ds(s * FF + j * P, P)]
                                     ).then_inc(raw_full[b], 16)

                def mod_units(layer, first_vec, k0, n_before):
                    for u in range(8):
                        if u < 2:
                            free_of_split(n_before + u)
                            apart(sp)
                        else:
                            free_of_mod(k0 + u - 1)
                        load(u % 2, w_mod_v, layer * KT, KT, first_vec * D + u * UC, UC)

                for n in range(2):
                    sp.wait_ge(mod_used, l * MOD_LAYER + MOD_PRE)
                    sp.wait_ge(split_full[n], l * SPLIT_SLOT + 1)
                    split_unit(n)
                mod_units(l, 2, 0, 0)
                for n in range(2, 14):
                    free_of_mod(8 - 1 + n - 2) if n < 4 else free_of_split(n - 2)
                    split_unit(n)
                mod_units(l, 4, 8, 12)
                for n in range(14, 16):
                    free_of_mod(16 - 1 + n - 14)
                    split_unit(n)
                for b in range(2):
                    free_of_split(14 + b)
                    up_unit(b, b)
                nxt = (DEPTH - 1) - l
                mod_units(nxt, 0, 16, 16)
                for b in range(2):
                    free_of_mod(24 - 1 + b)
                    up_unit(b, 2 + b)
                with sp.Fori(0, CHUNKS[0] // 2 - 2) as i:
                    for b in range(2):
                        sp.wait_ge(split_full[b], l * SPLIT_SLOT + ((UP_U[0] + 2) // 2 + 2) + i)
                        up_unit(b, 2 * i + (4 + b))
                for c in range(2):
                    if c == 1:
                        with sp.Fori(0, CHUNKS[1] // 2) as i:
                            for b in range(2):
                                sp.wait_ge(split_full[b], l * SPLIT_SLOT + (UP_U[1] // 2 + 1) + i)
                                up_unit(b, 2 * i + (CH0[1] + b))
                    with sp.Fori(0, 4) as i:
                        for b in range(2):
                            sp.wait_ge(split_full[b], l * SPLIT_SLOT + (DN_U[c] // 2 + 1) + i)
                            load(b, w_down_v, l * (FF // P) + CH0[c], CHUNKS[c], (2 * i + b) * P, P)

            for t in range(NT):
                sp.wait_ge(yT_read, 2 * t + 2)
                dst = y_prompt[0] if t == 0 else y_sample[0, (t - 1) * P:t * P, :]
                sp.dma_start(dst, xin[:, t, :]).then_inc(y_out, 16)
            sp.wait_ge(y_out, 16 * NT)

        @block.gpsimd
        def _(pool):
            ck = cache_k.rearrange("b l p h s d -> p (b l) (h s d)")
            cv = cache_v.rearrange("b l p h e -> p (b l) (h e)")
            nk = new_k.rearrange("b l p h s d -> p (b l) (h s d)")
            nv = new_v.rearrange("b l p h e -> p (b l) (h e)")
            with pool.Fori(0, DEPTH) as l:
                pool.wait_ge(stat_full, 3 * l + 1)
                pool.dma_start(kc[:, :], ck[:, ds(l, 1), :].rearrange("p a n -> p (a n)")).then_inc(kv_in, 16)
                pool.dma_start(v[:, 1, :], cv[:, ds(l, 1), :].rearrange("p a n -> p (a n)")).then_inc(kv_in, 16)
                pool.wait_ge(qk_ready, 2 * NT * l + NT + 1)
                apart(pool)
                pool.dma_start(nk[:, ds(l, 1), :].rearrange("p a n -> p (a n)"), qn[:, 0, :]).then_inc(nk_out, 16)
                pool.wait_ge(v_ready, NT * l + 1)
                apart(pool)
                pool.dma_start(nv[:, ds(l, 1), :].rearrange("p a n -> p (a n)"), v[:, 0, :]).then_inc(out_done, 16)
            pool.wait_ge(out_done, 16 * DEPTH)
            pool.wait_ge(nk_out, 16 * DEPTH)

        @block.tensor
        def _(pe):
            mm = nc.tensor.matmul

            def gemm(out, b, kt, width, col, mov_hi, mov_lo, first=True, last=True):
                wh = w_hi[:, b, 0:kt * width].rearrange("p (t n) -> p t n", n=width)
                wl = w_lo[:, b, 0:kt * width].rearrange("p (t n) -> p t n", n=width)
                for k in range(kt):
                    mm(out, wh[:, k, col:col + P], mov_hi(k), start=first and k == 0, stop=False)
                    mm(out, wh[:, k, col:col + P], mov_lo(k), start=False, stop=False)
                    ins = mm(out, wl[:, k, col:col + P], mov_hi(k), start=False, stop=last and k == kt - 1)
                return ins

            def mod_group(l, k, raw_at):
                for u in range(4):
                    b = u % 2
                    if l is None:
                        pe.wait_ge(raw_full[b], 32 * ((k + u) // 2 + 1))
                    else:
                        pe.wait_ge(raw_full[b], landed(l, raw_at + u))
                    if u == 0 and (l is not None or k):
                        pe.wait_ge(mod_ready, (k // 4) if l is None else 6 * l + (2 + k // 4))
                    wu = raw[:, b, :].rearrange("p (t n) -> p t n", n=UC)
                    for t in range(KT):
                        ins = mm(ps[0:2, 5 + u // 2, b * UC:(b + 1) * UC], cT[:, t, :], wu[:, t, :],
                                 start=t == 0, stop=t == KT - 1)
                    ins.then_inc(mod_used, 1)
                pe.wait_ge(row_read, (2 * (k // 4) + 2) if l is None else 12 * l + (6 + 2 * (k // 4)))
                apart(pe)
                for t in range(KT):
                    ins = nc.tensor.transpose(ps[:, 7, 2 * t:2 * t + 2], mod_row[0:2, t * P:(t + 1) * P],
                                              ident[0:2, 0:2])
                ins.then_inc(modT_full, 1)

            def stat(l, which):
                pe.wait_ge(ssq_ready, 3 * l + (1 + which))
                for h in range(2):
                    ins = mm(ps[:, h, 0:HALF], ones[:, :], ssq[:, h * HALF:(h + 1) * HALF], start=True, stop=True)
                ins.then_inc(stat_full, 1)

            pe.sem_inc(unit_done[0], 1)
            pe.sem_inc(unit_done[1], 1)
            pe.wait_ge(small_in, 16 * N_SMALL)
            pe.wait_ge(const_ready, 1)
            pe.wait_ge(silu_c, 1)
            nc.tensor.transpose(ps[:, 0, 0:P], crow[:, :], ident[:, :]).then_inc(setup_full, 1)
            pe.wait_ge(ffn_in, 64)
            for l in range(DEPTH):
                for r in range(3):
                    ins = nc.tensor.transpose(ps[:, 1 + l, r * P:(r + 1) * P], vrow[:, l, r, :], ident[:, :])
                ins.then_inc(setup_full, 1)
            mm(ps[:, 3, :], ones[0:1, :], brow[0:1, 0:512], start=True, stop=True).then_inc(setup_full, 1)
            mm(ps[:, 4, 0:256], ones[0:1, :], brow[0:1, 512:768], start=True, stop=True).then_inc(setup_full, 1)
            pe.wait_ge(x_in, 32)
            pe.wait_ge(setup_read, 5)
            for j in range(2):
                for t in range(4):
                    ins = nc.tensor.transpose(ps[:, j, t * P:(t + 1) * P],
                                              xin[:, 0, (4 * j + t) * P:(4 * j + t + 1) * P], ident[:, :])
                ins.then_inc(xT_full, 1)
            for k in range(KT):
                bank = (2 + k) % 5
                if k >= 3:
                    pe.wait_ge(xT_read, k - 2)
                for t in range(4):
                    ins = nc.tensor.transpose(ps[:, bank, t * P:(t + 1) * P], xin[:, 1 + t, k * P:(k + 1) * P],
                                              ident[:, :])
                ins.then_inc(xT_full, 1)
            pe.wait_ge(cT_ready, 1)
            mod_group(None, 0, 0)
            mod_group(None, 4, 0)

            with pe.Fori(0, DEPTH) as l:
                stat(l, 0)
                mod_group(l, 0, M1_RAW)
                mod_group(l, 4, M1_RAW + 4)

                def qkv_unit(b, t, c0, signal):
                    col = TOK_TILES[t]
                    wh = w_hi[:, b, :].rearrange("p (t n) -> p t n", n=UC)
                    wl = w_lo[:, b, :].rearrange("p (t n) -> p t n", n=UC)
                    out = ps[:, t, c0:c0 + UC]
                    for k in range(KT):
                        mm(out, h_hi[:, k, col:col + P], wh[:, k, :], start=k == 0, stop=False)
                        mm(out, h_hi[:, k, col:col + P], wl[:, k, :], start=False, stop=False)
                        ins = mm(out, h_lo[:, k, col:col + P], wh[:, k, :], start=False, stop=k == KT - 1)
                    if t == NT - 1:
                        ins.then_inc(unit_done[b], 1)
                    elif signal:
                        ins.then_inc(qkv_full, 1)

                pe.wait_ge(h_ready, 2 * l + 1)
                pe.wait_ge(rms_ready, 3 * l + 1)
                pe.wait_ge(kv_in, 32 * l + 32)
                for s in range(4):
                    ins = nc.tensor.transpose(ps[:, 5, s * P:(s + 1) * P], kc[:, s * P:(s + 1) * P], ident[:, :])
                ins.then_inc(qkT_full, 1)
                for b in range(2):
                    pe.wait_ge(split_full[b], usable(l, b))
                    for t in range(NT):
                        qkv_unit(b, t, b * UC, b == 1)
                with pe.Fori(1, 3) as p:
                    pe.wait_ge(split_full[0], l * SPLIT_SLOT + 2 + p)
                    for t in range(NT):
                        pe.wait_ge(qkv_read, 2 * NT * l + NT * p + (t + 1 - NT))
                        qkv_unit(0, t, 0, False)
                        pe.wait_ge(qk_ready, 2 * NT * l + NT * p + (t + 1 - NT))
                        if t != 1:
                            pe.wait_ge(qkT_read, 11 * l + NT * p + (t - NT + (t == 0)))
                        for s in range(4):
                            ins = nc.tensor.transpose(ps[:, 5 + t % 2, s * P:(s + 1) * P],
                                                      qn[:, t, s * P:(s + 1) * P], ident[:, :])
                        ins.then_inc(qkT_full, 1)
                    pe.wait_ge(split_full[1], l * SPLIT_SLOT + 2 + p)
                    for t in range(NT):
                        qkv_unit(1, t, UC, True)

                def conv_half(i):
                    n = C_U + i // 4
                    b, tile, h = n % 2, (i % 4) // 2, i % 2
                    if i % 4 == 0:
                        pe.wait_ge(split_full[b], usable(l, n))
                    if i >= 2:
                        j = i - 2
                        if (j // 4) % 3 == 0:
                            pe.wait_ge(cg_read, 8 * l + (4 * (j // 12) + j % 4 + 1))
                        else:
                            pe.wait_ge(xb_read, 16 * l + (8 * (j // 12) + (j % 12) - 4 + 1))
                    ins = gemm(ps[:, h, 0:HALF], b, KT, UC, tile * P,
                               lambda k: h_hi[:, k, h * HALF:(h + 1) * HALF],
                               lambda k: h_lo[:, k, h * HALF:(h + 1) * HALF])
                    ins.then_inc(unit_done[b] if i % 4 == 3 else conv_full, 1)

                def qk_scores(i):
                    hd, t = divmod(i, NT)
                    if i:
                        pe.wait_ge(exp_done, ROUNDS * l + i)
                    else:
                        pe.wait_ge(qkT_read, 11 * l + 11)
                    for s in range(2):
                        if t == 0:
                            parts, k0 = [(0, SEQ)], K_PROMPT
                        else:
                            parts, k0 = ([(512, N_KEY), (0, 512)], [(384, N_KEY), (0, 384)])[s], K_PAST
                        for j, (a, e) in enumerate(parts):
                            if s and j:
                                pe.wait_ge(bank3_first, (ROUNDS - NH) * l + (hd * (NT - 1) + t))
                            ins = mm(scores[:, s * N_KEY + a:s * N_KEY + e],
                                     qT[s * HD:(s + 1) * HD, hd, t * P:(t + 1) * P],
                                     kT[s * HD:(s + 1) * HD, hd, k0 + a:k0 + e], start=True, stop=True)
                            if s == 0 and j == 0 and t:
                                ins.then_inc(bank3_first, 1)
                    ins.then_inc(qk_full, 1)

                def key_tiles(i):
                    return [0] if i % NT == 0 else [1, 2, 3, 4, 5]

                def transposes(i):
                    pe.wait_ge(a_ready, ROUNDS * l + (i + 1))
                    if i:
                        pe.wait_ge(aT_ready, ROUNDS * l + i)
                    for j in range(len(key_tiles(i))):
                        ins = nc.tensor.transpose(probsT[:, j * P:(j + 1) * P], probs[:, i % 2, 0, j * P:(j + 1) * P],
                                                  ident[:, :])
                    ins.then_inc(aT_full, 1)

                def pv(i):
                    pe.wait_ge(aT_ready, ROUNDS * l + (i + 1))
                    if i:
                        pe.wait_ge(o_read, ROUNDS * l + i)
                    else:
                        pe.wait_ge(mod_ready, 6 * l + 4)
                    tiles, hd = key_tiles(i), i // NT
                    for j, kt in enumerate(tiles):
                        ins = mm(ps[:, 7, 0:VD], aT[:, j * P:(j + 1) * P], v[:, kt, hd * VD:(hd + 1) * VD],
                                 start=j == 0, stop=j == len(tiles) - 1)
                    ins.then_inc(pv_full, 1)

                pe.wait_ge(v_ready, NT * l + NT)
                for i in range(HALVES):
                    conv_half(i)
                    if i < ROUNDS:
                        qk_scores(i)
                    if 2 <= i < ROUNDS + 2:
                        pv(i - 2)
                    if 1 <= i < ROUNDS + 1:
                        transposes(i - 1)

                pe.wait_ge(o_read, ROUNDS * l + ROUNDS)
                mod_group(l, 8, M2_RAW)
                stat(l, 1)
                pe.wait_ge(on_ready, l + 1)
                for t in range(NT):
                    if t >= 3:
                        pe.wait_ge(oT_read, NT * l + (t - 2))
                    for hd in range(NH):
                        ins = nc.tensor.transpose(ps[:, 2 + t % 3, hd * P:(hd + 1) * P], o[:, hd * NT + t, :],
                                                  ident[:, :])
                    ins.then_inc(oT_full, 1)
                mod_group(l, 12, M2_RAW + 4)

                pe.wait_ge(mix_ready, l + 1)
                pe.wait_ge(mod_ready, 6 * l + 6)
                apart(pe)
                with pe.Fori(0, 2) as i:
                    for j in range(4):
                        b = j // 2
                        if j % 2 == 0:
                            pe.wait_ge(split_full[b], l * SPLIT_SLOT + (O_U // 2 + 2) + i)
                        pe.wait_ge(x_ready, 16 * l + 4 * i + (j + 5))
                        for h in range(2):
                            ins = gemm(ps[:, 2 * j + h, 0:HALF], b, KT, UC, (j % 2) * P,
                                       lambda k: h_hi[:, k, h * HALF:(h + 1) * HALF],
                                       lambda k: h_lo[:, k, h * HALF:(h + 1) * HALF])
                        ins.then_inc(unit_done[b] if j % 2 else out_full, 1)
                stat(l, 2)
                mod_group(l, 16, M3_RAW)
                mod_group(l, 20, M3_RAW + 4)

                pe.wait_ge(h_ready, 2 * l + 2)
                pe.wait_ge(rms_ready, 3 * l + 3)
                pe.wait_ge(mod_ready, 6 * l + 8)
                for c in range(2):
                    if c:
                        pe.wait_ge(dn_read, 8 * l + (2 + 8))
                    apart(pe)
                    with pe.Fori(0, CHUNKS[c] // 2) as i:
                        for b in range(2):
                            pe.wait_ge(split_full[b], l * SPLIT_SLOT + (UP_U[c] // 2 + 2) + i)
                            pe.wait_ge(up_read, 22 * l + 2 * i + (CH0[c] + b + 1))
                            for s in range(2):
                                wh = w_hi[:, b, s * KT * P:(s + 1) * KT * P].rearrange("p (t n) -> p t n", n=P)
                                wl = w_lo[:, b, s * KT * P:(s + 1) * KT * P].rearrange("p (t n) -> p t n", n=P)
                                for h in range(2):
                                    out = ps[:, 4 * b + 2 * s + h, 0:HALF]
                                    for k in range(KT):
                                        hh = h_hi[:, k, h * HALF:(h + 1) * HALF]
                                        mm(out, wh[:, k, :], hh, start=k == 0, stop=False)
                                        mm(out, wh[:, k, :], h_lo[:, k, h * HALF:(h + 1) * HALF],
                                           start=False, stop=False)
                                        ins = mm(out, wl[:, k, :], hh, start=False, stop=k == KT - 1)
                            ins.then_inc(unit_done[b], 1)
                    pe.wait_ge(g_ready, 22 * l + (CH0[c] + CHUNKS[c]))
                    apart(pe)
                    with pe.Fori(0, 4) as i:
                        for b in range(2):
                            pe.wait_ge(split_full[b], l * SPLIT_SLOT + (DN_U[c] // 2 + 2) + i)
                            if c == 0:
                                pe.wait_ge(dn_read, 8 * l + 2 * i + (b + 1))
                            else:
                                pe.wait_ge(x_ready, 16 * l + 2 * i + (b + 15))
                            for h in range(2):
                                ins = gemm(ps[:, 2 * b + h, 0:HALF], b, CHUNKS[c], P, 0,
                                           lambda k: g_hi[:, k * T + h * HALF:k * T + (h + 1) * HALF],
                                           lambda k: g_lo[:, k * T + h * HALF:k * T + (h + 1) * HALF])
                            ins.then_inc(unit_done[b], 1)

            pe.wait_ge(ssq_ready, 3 * DEPTH + 1)
            for j in range(2 * NT):
                t, kh = j // 2, j % 2
                if j >= 8:
                    pe.wait_ge(yT_read, j - 7)
                for s in range(4):
                    k = 4 * kh + s
                    ins = nc.tensor.transpose(ps[:, j % 8, s * P:(s + 1) * P],
                                              x[:, k, TOK_TILES[t]:TOK_TILES[t] + P], ident[:, :])
                ins.then_inc(yT_full, 1)

        def at(expr, i, by=1):
            return expr if i is None else expr + i * by

        @block.scalar
        def _(act):
            A = nc.scalar.activation

            def rows(l, g, half):
                if half == 0 and (l is not None or g):
                    act.wait_ge(modT_full, g if l is None else 6 * l + (2 + g))
                act.wait_ge(mod_used, 4 * g + 2 * half + 2 if l is None
                            else MOD_LAYER * l + (MOD_PRE + 4 * g + 2 * half + 2))
                A(mod_row[0:2, half * 512:(half + 1) * 512], ps[0:2, 5 + half, :], ACT.Copy).then_inc(row_read, 1)

            act.wait_ge(const_ready, 1)
            act.dma_start(crow[0:KT, :], c_ctx.rearrange("(t n) -> t n", n=P)).then_inc(c_in, 16)
            act.dma_start(crow[KT:2 * KT, :], c_sample.rearrange("b (t n) -> (b t) n", n=P)).then_inc(c_in, 16)
            small = [(ident[:, :], ident_in), (rope[:, :, :, :], rope_in)]
            for src, r0, n in ((b_mod, V_BMOD, 48), (norm1_g, V_N1, KT), (norm2_g, V_N2, KT),
                               (conv_norm_g, V_CNG, 4), (subln_g, V_SUB, 1)):
                small.append((vrow[r0:r0 + n, :, 0, :], src.rearrange("l (t n) -> t l n", n=P)))
            for j in range(3):
                small.append((vrow[V_CONV + 4 * j:V_CONV + 4 * j + 4, :, 0, :],
                              conv_w[:, j, :].rearrange("l (t n) -> t l n", n=P)))
            for i, src in enumerate((lambda_q1, lambda_k1, lambda_q2, lambda_k2, q_norm_g, k_norm_g)):
                small.append((brow[0:1, i * P:(i + 1) * P], src.rearrange("(a l) n -> a (l n)", a=1)))
            assert len(small) == N_SMALL
            for dst, src in small:
                act.dma_start(dst, src).then_inc(small_in, 16)
            for l in range(DEPTH):
                fr = ffn_conv_w[l].rearrange("w (t n) -> (w t) n", n=P)
                act.dma_start(vrow[:, l, 1, :], fr[0:P, :]).then_inc(ffn_in, 16)
                act.dma_start(vrow[0:3 * V_FT - P, l, 2, :], fr[P:3 * V_FT, :]).then_inc(ffn_in, 16)
            act.dma_start(xin[:, 0, :], x_prompt[0]).then_inc(x_in, 16)
            act.dma_start(xin[:, 1:NT, :], x_sample[0].rearrange("(t p) n -> p t n", p=P)).then_inc(x_in, 16)
            act.wait_ge(c_in, 32)
            A(crow[:, :], crow[:, :], ACT.Silu).then_inc(silu_c, 1)
            act.wait_ge(lam_ready, 1)
            A(lam_s[:, :], lam_s[:, :], ACT.Exp).then_inc(lam_exp, 1)
            for k in range(KT):
                act.wait_ge(xT_read, k + 3)
                if k:
                    act.wait_ge(sq_added, k)
                A(sq[:, :], x[:, k, :], ACT.Square).then_inc(sq_ready, 1)
            for g in range(2):
                rows(None, g, 0)
                rows(None, g, 1)

            with act.Fori(0, DEPTH) as l:
                def split_hi(n, i=None, size=SLOT):
                    b = n % 2
                    act.wait_ge(raw_full[b], at(landed(l, raw_of(n)), i, 32))
                    act.wait_ge(unit_done[b], at(l * SPLIT_SLOT + (n // 2 + 1), i))
                    A(w_hi[:, b, 0:size], raw[:, b, 0:size], ACT.Copy).then_inc(hi_done[b], 1)

                def rms(which, scale):
                    act.wait_ge(stat_full, 3 * l + (1 + which))
                    A(rb[:, :].rearrange("p (h n) -> p h n", h=2), ps[:, 0:2, 0:HALF], ACT.Sqrt,
                      bias=eps[:, :], scale=scale).then_inc(rms_ready, 1)

                def norm_hi(k, vec, base):
                    act.wait_ge(tmp_ready, 20 * l + (base + k + 1))
                    for c0, n, s in SEQS:
                        ins = A(h_hi[:, k, c0:c0 + n], tmp[:, k % 2, c0:c0 + n], ACT.Identity,
                                bias=modv[:, vec, k, s:s + 1])
                    ins.then_inc(hh_ready, 1)

                def norm(which, vec, base, g):
                    rms(which, 1.0 / D)
                    rows(l, g, 0)
                    for k in range(4):
                        norm_hi(k, vec, base)
                    rows(l, g, 1)
                    for k in range(4, KT):
                        norm_hi(k, vec, base)
                    rows(l, g + 1, 0)
                    rows(l, g + 1, 1)

                split_hi(0)
                split_hi(1)
                norm(0, 0, 0, 0)

                def qk_copy(n):
                    bank = 5 if n == 0 else 5 + (n - 1) % NT % 2
                    if n == 0:
                        dst = kT[:, :, K_PAST:K_PAST + P]
                    elif n <= NT:
                        dst = qT[:, :, (n - 1) * P:n * P]
                    else:
                        t = n - 1 - NT
                        c0 = K_PROMPT if t == 0 else K_SAMPLE + (t - 1) * P
                        dst = kT[:, :, c0:c0 + P]
                    act.wait_ge(qkT_full, 11 * l + (n + 1))
                    A(dst, ps[:, bank, :].rearrange("p (s n) -> p s n", n=P), ACT.Copy).then_inc(qkT_read, 1)

                qk_copy(0)
                for p in range(3):
                    if p:
                        for t in range(NT):
                            qk_copy(1 + (p - 1) * NT + t)
                    split_hi(2 * p + 2)
                    for t in range(NT):
                        if t < NT - 1:
                            act.wait_ge(qkv_full, 12 * l + (4 * p + t + 1))
                        else:
                            act.wait_ge(unit_done[1], done(l, 2 * p + 1))
                        if p == 2:
                            A(v[:, t + (t > 0), :], ps[:, t, :], ACT.Copy).then_inc(v_ready, 1)
                            continue
                        n = NT * p + t
                        A(sq[:, 0:D_ATTN], ps[:, t, :], ACT.Square).then_inc(qsq_ready, 1)
                        if n >= 2:
                            act.wait_ge(qk_ready, 2 * NT * l + (n - 1))
                        A(qraw[:, n % 2, :], ps[:, t, :], ACT.Copy).then_inc(qkv_read, 1)
                        act.wait_ge(qsum_ready, 2 * NT * l + (n + 1))
                        A(st8[:, n % 2, :], st8[:, n % 2, :], ACT.Sqrt, bias=eps[:, :], scale=1.0 / HD
                          ).then_inc(qrms_ready, 1)
                    split_hi(2 * p + 3)

                for i in range(HALVES):
                    unit, tile, h = i // 4, (i % 4) // 2, i % 2
                    if i % 4 == 0 and unit:
                        split_hi(C_U + unit + 1)
                    if unit % 3 == 0:
                        if i == 12:
                            act.wait_ge(xb_read, 16 * l + 8)
                        if i % 4 == 3:
                            act.wait_ge(unit_done[unit % 2], done(l, C_U + unit))
                        else:
                            act.wait_ge(conv_full, 18 * l + (3 * unit + i % 4 + 1))
                        A(cgb[:, tile, h * HALF:(h + 1) * HALF], ps[:, h, 0:HALF], ACT.Copy).then_inc(cg_read, 1)
                    if 1 <= i < ROUNDS + 1:
                        w = P if (i - 1) % NT == 0 else N_KEY
                        act.wait_ge(aT_full, ROUNDS * l + i)
                        A(aT[:, 0:w], probsT[:, 0:w], ACT.Copy).then_inc(aT_ready, 1)
                    if i < ROUNDS:
                        w = P if i % NT == 0 else N_KEY
                        if i == 0:
                            act.wait_ge(nk_out, 16 * l + 16)
                            act.wait_ge(out_done, 16 * l + 16)
                        act.wait_ge(max_ready, ROUNDS * l + (i + 1))
                        for s in range(2):
                            ins = A(probs[:, i % 2, s, 0:w], scores[:, s * N_KEY:s * N_KEY + w], ACT.Exp,
                                    bias=nbias[:, i % 2, s:s + 1], scale=SCALE,
                                    accum_out=sums[:, i % 2, s:s + 1])
                        ins.then_inc(exp_done, 1)
                    if 2 <= i < ROUNDS + 2:
                        r = i - 2
                        act.wait_ge(pv_full, ROUNDS * l + (r + 1))
                        A(o[:, r, :], ps[:, 7, 0:VD], ACT.Copy)
                        A(junk[:, :], ps[:, 7, 0:VD], ACT.Square, accum_out=ssq_o[:, r:r + 1]
                          ).then_inc(o_read, 1)

                split_hi(C_U + 7)
                act.drain()
                A(ssq_o[:, :], ssq_o[:, :], ACT.Sqrt, bias=eps[:, :], scale=1.0 / VD).then_inc(orms_ready, 1)
                rows(l, 2, 0)
                rows(l, 2, 1)
                rms(1, 1.0 / D_CONV)
                for t in range(NT):
                    c0 = TOK_TILES[t]
                    act.wait_ge(oT_full, NT * l + (t + 1))
                    A(h_hi[:, 0:4, c0:c0 + P], ps[:, 2 + t % 3, :].rearrange("p (s n) -> p s n", n=P), ACT.Copy,
                      scale=vl[:, V_SUB:V_SUB + 1]).then_inc(oT_hi, 1)
                rows(l, 3, 0)
                for k in range(4):
                    act.wait_ge(tmp_ready, 20 * l + (KT + k + 1))
                    A(h_hi[:, 4 + k, :], tmp[:, k % 2, :], ACT.Copy).then_inc(hh_ready, 1)
                rows(l, 3, 1)

                def square(k, i=None):
                    act.wait_ge(x_ready, at(16 * l + (KT + k + 1), i, 2))
                    kx = at(k % KT * T, i, 2 * T)
                    A(sq[:, :], xf[:, ds(kx, T)] if i is not None else xf[:, kx:kx + T], ACT.Square
                      ).then_inc(sq_ready, 1)

                for n in range(4):
                    square(2 * n)
                    square(2 * n + 1)
                    split_hi(O_U + n + 2)
                norm(2, 3, 12, 4)

                def up_post(c, b, i, j, nxt_size):
                    n = UP_U[c] + j
                    gate = CH0[c] + j
                    act.wait_ge(unit_done[b], at(done(l, n), i))
                    both = ps[:, 4 * b:4 * b + 4, 0:HALF]
                    A(ub[:, :, :].rearrange("p s (h n) -> p (s h) n", h=2), both, ACT.Copy)
                    for s in range(2):
                        w = V_FFN + V_FT + s * (V_FT // 2) + gate
                        ins = A(cen[:, s, :].rearrange("p (h n) -> p h n", h=2), both[:, 2 * s:2 * s + 2, :],
                                ACT.Copy, scale=vl[:, w:w + 1] if i is None else vl[:, ds(i * 2 + w, 1)])
                    ins.then_inc(up_read, 1)
                    split_hi(n + 2, i, nxt_size)
                    act.wait_ge(taps_ready, at(22 * l + (gate + 1), i, 2))
                    A(cen[:, 0, :], cen[:, 0, :], ACT.Silu).then_inc(silu_ready, 1)
                    act.wait_ge(gm_ready, at(22 * l + (gate + 1), i, 2))
                    A(g_hi[:, j * T:(j + 1) * T] if i is None else g_hi[:, ds(i * (2 * T) + j * T, T)],
                      gt[:, :], ACT.Copy).then_inc(gh_ready, 1)

                for c in range(2):
                    pairs = CHUNKS[c] // 2
                    with act.Fori(0, pairs - 1) as i:
                        for b in range(2):
                            up_post(c, b, i, b, SLOT)
                    for b in range(2):
                        up_post(c, b, None, 2 * (pairs - 1) + b, CHUNKS[c] * P)
                    with act.Fori(0, 3) as i:
                        for b in range(2):
                            if c:
                                square(KT + b, i)
                            split_hi(DN_U[c] + b + 2, i, CHUNKS[c] * P)
                    for b in range(2):
                        if c:
                            square(KT + 6 + b)
                        else:
                            split_hi(DN_U[c] + 6 + b + 2)

            for j in range(2 * NT):
                act.wait_ge(yT_full, j + 1)
                A(xin[:, j // 2, (j % 2) * 512:(j % 2) * 512 + 512], ps[:, j % 8, :], ACT.Copy).then_inc(yT_read, 1)

        @block.vector
        def _(dve):
            V = nc.vector

            def mod_post(l, g, vec, bias):
                dve.wait_ge(modT_full, g + 1 if l is None else 6 * l + (g + 3))
                apart(dve)
                V.tensor_tensor(modv[:, vec, :, :], ps[:, 7, 0:2 * KT].rearrange("p (t s) -> p t s", s=2),
                                bias.unsqueeze(2).broadcast_to([P, KT, 2]), ALU.add).then_inc(mod_ready, 1)

            V.memset(vrow[:, :, :, :], 0.0)
            V.memset(crow[:, :], 0.0)
            V.memset(ones[:, :], 1.0)
            V.memset(eps[:, :], EPS)
            dve.drain()
            dve.sem_inc(const_ready, 1)
            for b in range(2):
                dve.sem_inc(split_full[b], 1)
            dve.sem_inc(up_read, 2)
            dve.sem_inc(dn_read, 2)
            dve.sem_inc(x_ready, KT)
            for buf in (x, h_hi, h_lo):
                for a, e in ((0, 1), (C_SAMPLE - 1, C_SAMPLE), (T - 2, T)):
                    V.memset(buf[:, :, a:e] if buf is x else buf[:, :, a:e].bitcast(F32), 0.0)
            dve.wait_ge(setup_full, 1)
            V.tensor_copy(cT[:, :, :].rearrange("p t s -> p s t"),
                          ps[:, 0, 0:2 * KT].rearrange("p (s t) -> p s t", s=2)).then_inc(setup_read, 1)
            for l in range(DEPTH):
                dve.wait_ge(setup_full, 2 + l)
                V.tensor_copy(vecs[:, l, :], ps[:, 1 + l, 0:V_N]).then_inc(setup_read, 1)
            dve.wait_ge(setup_full, 4)
            V.tensor_copy(lamb[:, :, :, :].rearrange("p a l n -> p (a l n)"), ps[:, 3, :]).then_inc(setup_read, 1)
            dve.wait_ge(setup_full, 5)
            V.tensor_copy(qkg[:, :, :, :].rearrange("p a l n -> p (a l n)"), ps[:, 4, 0:256]
                          ).then_inc(setup_read, 1)
            dve.drain()
            for l in range(DEPTH):
                V.tensor_scalar(vecs[:, l, V_SUB:V_SUB + 1], vecs[:, l, V_SUB:V_SUB + 1], 1.0 - LAM_INIT[l], None,
                                ALU.mult)
            lv = lamb[:, :, :, :].rearrange("p (a c) l n -> p a c (l n)", c=2)
            V.tensor_tensor(lamp[:, :, :, :].rearrange("p a l n -> p a (l n)"), lv[:, :, 0, :], lv[:, :, 1, :],
                            ALU.mult)
            dve.drain()
            V.tensor_reduce(lam_s[:, :], lamp[:, :, :, :].rearrange("p a l n -> p (a l) n"), axis=AX.X, op=ALU.add
                            ).then_inc(lam_ready, 1)
            dve.wait_ge(lam_exp, 1)
            V.tensor_tensor(neglam[:, :], lam_s[:, DEPTH:2 * DEPTH], lam_s[:, 0:DEPTH], ALU.subtract)
            dve.drain()
            for l in range(DEPTH):
                V.tensor_scalar(neglam[:, l:l + 1], neglam[:, l:l + 1], -LAM_INIT[l], None, ALU.add)
            dve.drain()
            dve.sem_inc(cT_ready, 1)
            for j in range(2):
                dve.wait_ge(xT_full, j + 1)
                V.tensor_copy(x[:, 4 * j:4 * j + 4, C_PROMPT:C_PROMPT + SEQ],
                              ps[:, j, :].rearrange("p (t n) -> p t n", n=P)).then_inc(xT_read, 1)
            V.memset(ssq[:, :], 0.0)
            for k in range(KT):
                dve.wait_ge(xT_full, k + 3)
                V.tensor_copy(x[:, k, C_SAMPLE:C_SAMPLE + DEC], ps[:, (2 + k) % 5, :]).then_inc(xT_read, 1)
            for k in range(KT):
                dve.wait_ge(sq_ready, k + 1)
                dve.drain()
                V.tensor_tensor(ssq[:, :], ssq[:, :], sq[:, :], ALU.add).then_inc(
                    ssq_ready if k == KT - 1 else sq_added, 1)
            for g in range(2):
                mod_post(None, g, g, vecs[:, 0, V_BMOD + g * KT:V_BMOD + (g + 1) * KT])

            with dve.Fori(0, DEPTH) as l:
                def split_lo(n, i=None, size=SLOT):
                    b = n % 2
                    dve.wait_ge(hi_done[b], at(l * SPLIT_SLOT + (n // 2 + 1), i))
                    V.tensor_tensor(w_lo[:, b, 0:size], raw[:, b, 0:size], w_hi[:, b, 0:size].bitcast(F32),
                                    ALU.subtract).then_inc(split_full[b], 1)

                def inverse_rms(which):
                    dve.wait_ge(rms_ready, 3 * l + (1 + which))
                    V.reciprocal(rb[:, :], rb[:, :])
                    dve.drain()

                def norm(which, vec, gain_col, base):
                    V.scalar_tensor_tensor(out=gain[:, :, :], in0=modv[:, vec + 1, :, :], scalar=1.0,
                                           in1=vl[:, gain_col:gain_col + KT].unsqueeze(2).broadcast_to([P, KT, 2]),
                                           op0=ALU.add, op1=ALU.mult)
                    inverse_rms(which)
                    for k in range(KT + 1):
                        if k < KT:
                            if k > 1:
                                dve.drain()
                            for c0, n, s in SEQS:
                                ins = V.scalar_tensor_tensor(
                                    out=tmp[:, k % 2, c0:c0 + n], in0=x[:, k, c0:c0 + n],
                                    scalar=gain[:, k, s:s + 1], in1=rb[:, c0:c0 + n], op0=ALU.mult, op1=ALU.mult)
                            ins.then_inc(tmp_ready, 1)
                        if k:
                            j = k - 1
                            dve.wait_ge(hh_ready, 20 * l + (base + j + 1))
                            for c0, n, s in SEQS:
                                ins = V.scalar_tensor_tensor(
                                    out=h_lo[:, j, c0:c0 + n], in0=tmp[:, j % 2, c0:c0 + n],
                                    scalar=modv[:, vec, j, s:s + 1], in1=h_hi[:, j, c0:c0 + n].bitcast(F32),
                                    op0=ALU.add, op1=ALU.subtract)
                            if k == KT:
                                ins.then_inc(h_ready, 1)

                V.tensor_copy(vl[:, :], vecs[:, :, :].rearrange("p l n -> p (l n)")[:, ds(l * V_N, V_N)])
                V.tensor_copy(qkg_l[:, :, :], qkg[:, :, ds(l, 1), :].rearrange("p a l n -> p a (l n)"))
                V.tensor_copy(neglam_l[:, :], neglam[:, ds(l, 1)])
                dve.drain()
                split_lo(0)
                split_lo(1)
                norm(0, 0, V_N1, 0)
                mod_post(l, 0, 2, vl[:, V_BMOD + 2 * KT:V_BMOD + 3 * KT])
                mod_post(l, 1, 3, vl[:, V_BMOD + 3 * KT:V_BMOD + 4 * KT])
                for a in range(2):
                    g4 = qkg_l[:, a, :].unsqueeze(1).broadcast_to([P, 4, HD])
                    V.tensor_tensor(rope_q[:, a, 0, :, :], rope[:, 0, :, :], g4, ALU.mult)
                    for m in range(2):
                        def member(ap, m):
                            return ap.rearrange("p (a m n) -> p a m n", m=2, n=16)[:, :, m, :]
                        V.tensor_tensor(member(rope_q[:, a, 1, :, :].rearrange("p t n -> p (t n)"), m),
                                        member(rope[:, 1, :, :].rearrange("p t n -> p (t n)"), m),
                                        g4.rearrange("p t (a m n) -> p t a m n", m=2, n=16)[:, :, :, 1 - m, :],
                                        ALU.mult)

                def groups(ap):
                    return ap.rearrange("p (g n) -> p g n", n=HD)

                for p in range(3):
                    split_lo(2 * p + 2)
                    for t in range(NT if p < 2 else 0):
                        n = NT * p + t
                        q = qraw[:, n % 2, :]
                        dve.wait_ge(qsq_ready, 2 * NT * l + (n + 1))
                        V.tensor_reduce(st8[:, n % 2, :], groups(sq[:, 0:D_ATTN]), axis=AX.X, op=ALU.add
                                        ).then_inc(qsum_ready, 1)
                        dve.wait_ge(qrms_ready, 2 * NT * l + (n + 1))
                        V.reciprocal(st8[:, n % 2, :], st8[:, n % 2, :])
                        dve.drain()
                        V.tensor_tensor(groups(q), groups(q),
                                        st8[:, n % 2, :].unsqueeze(2).broadcast_to([P, 8, HD]), ALU.mult)
                        dve.drain()
                        if t == 0:
                            V.tensor_tensor(groups(qn[:, 0, :]), groups(q),
                                            qkg_l[:, p, :].unsqueeze(1).broadcast_to([P, 8, HD]), ALU.mult
                                            ).then_inc(qk_ready, 1)
                            continue
                        V.tensor_tensor(groups(rt[:, 0, :]), groups(q),
                                        rope_q[:, p, 0, t - 1, :].unsqueeze(1).broadcast_to([P, 8, HD]), ALU.mult)
                        for m in range(2):
                            def member(ap, m):
                                return ap.rearrange("p (a m n) -> p a m n", m=2, n=16)[:, :, m, :]
                            sn = member(rope_q[:, p, 1, t - 1, :], m).unsqueeze(1).broadcast_to([P, 8, 2, 16])
                            V.tensor_tensor(member(rt[:, 1, :], m).rearrange("p (g a) n -> p g a n", a=2),
                                            member(q, 1 - m).rearrange("p (g a) n -> p g a n", a=2), sn, ALU.mult)
                        dve.drain()
                        V.tensor_tensor(qn[:, t, :], rt[:, 0, :], rt[:, 1, :], ALU.add).then_inc(qk_ready, 1)
                    split_lo(2 * p + 3)

                for i in range(HALVES):
                    unit, tile, h = i // 4, (i % 4) // 2, i % 2
                    pair, kind = divmod(unit, 3)
                    if 1 <= i < ROUNDS + 1:
                        r = (i - 1) % 2
                        w = P if (i - 1) % NT == 0 else N_KEY
                        dve.wait_ge(exp_done, ROUNDS * l + i)
                        V.reciprocal(rec[:, r, :], sums[:, r, :])
                        dve.drain()
                        V.tensor_tensor(rec[:, r, 1:2], rec[:, r, 1:2], neglam_l[:, :], ALU.mult)
                        V.tensor_scalar(probs[:, r, 0, 0:w], probs[:, r, 0, 0:w], rec[:, r, 0:1], None, ALU.mult)
                        dve.drain()
                        V.scalar_tensor_tensor(out=probs[:, r, 0, 0:w], in0=probs[:, r, 1, 0:w],
                                               scalar=rec[:, r, 1:2], in1=probs[:, r, 0, 0:w], op0=ALU.mult,
                                               op1=ALU.add).then_inc(a_ready, 1)
                    if kind:
                        if i % 4 == 3:
                            dve.wait_ge(unit_done[unit % 2], done(l, C_U + unit))
                        else:
                            dve.wait_ge(conv_full, 18 * l + (3 * unit + i % 4 + 1))
                        cols = slice(h * HALF, (h + 1) * HALF)
                    z = cgb[:, tile, :]
                    if kind == 1:
                        dve.wait_ge(cg_read, 8 * l + (4 * pair + i % 4 + 1))
                        V.tensor_tensor(z[:, cols], ps[:, h, 0:HALF], z[:, cols], ALU.mult).then_inc(xb_read, 1)
                        if h:
                            def cw(j):
                                w = V_CONV + 4 * j + 2 * pair + tile
                                return vl[:, w:w + 1]
                            dve.drain()
                            V.tensor_scalar(tap[:, tile, :], z, cw(1), None, ALU.mult)
                            for j, off in ((0, 0), (2, 2)):
                                dve.drain()
                                V.scalar_tensor_tensor(out=tap[:, tile, 1:T - 1], in0=z[:, off:off + T - 2],
                                                       scalar=cw(j), in1=tap[:, tile, 1:T - 1], op0=ALU.mult,
                                                       op1=ALU.add)
                            dve.drain()
                    elif kind == 2:
                        k = 2 * pair + tile
                        V.tensor_tensor(y[:, k, cols], ps[:, h, 0:HALF], tap[:, tile, cols], ALU.mult
                                        ).then_inc(xb_read, 1)
                        if h:
                            dve.drain()
                            if k == 0:
                                V.tensor_tensor(ssq[:, :], y[:, k, :], y[:, k, :], ALU.mult)
                            else:
                                V.tensor_tensor(sq[:, :], y[:, k, :], y[:, k, :], ALU.mult)
                                dve.drain()
                                ins = V.tensor_tensor(ssq[:, :], ssq[:, :], sq[:, :], ALU.add)
                                if k == 3:
                                    ins.then_inc(ssq_ready, 1)
                    if i < ROUNDS:
                        w = P if i % NT == 0 else N_KEY
                        dve.wait_ge(qk_full, ROUNDS * l + (i + 1))
                        V.reduce_max(mx[:, i % 2, :],
                                     scores[:, 0:2 * N_KEY].rearrange("p (s n) -> p s n", s=2)[:, :, 0:w], AX.X)
                        dve.drain()
                        V.tensor_scalar(nbias[:, i % 2, :], mx[:, i % 2, :], -SCALE, None, ALU.mult
                                        ).then_inc(max_ready, 1)
                    if i % 4 == 0 and unit:
                        split_lo(C_U + unit + 1)

                split_lo(C_U + 7)
                dve.wait_ge(orms_ready, l + 1)
                V.reciprocal(ssq_o[:, :], ssq_o[:, :])
                dve.drain()
                V.tensor_tensor(o[:, :, :], o[:, :, :], ssq_o[:, :].unsqueeze(2).broadcast_to([P, ROUNDS, VD]),
                                ALU.mult).then_inc(on_ready, 1)
                mod_post(l, 2, 4, vl[:, V_BMOD + 4 * KT:V_BMOD + 5 * KT])
                inverse_rms(1)
                for a, e in ((0, 1), (C_SAMPLE - 1, C_SAMPLE), (T - 2, T)):
                    V.memset(rb[:, a:e], 0.0)
                for t in range(NT):
                    c0 = TOK_TILES[t]
                    dve.wait_ge(oT_hi, NT * l + (t + 1))
                    V.scalar_tensor_tensor(out=h_lo[:, 0:4, c0:c0 + P],
                                           in0=ps[:, 2 + t % 3, :].rearrange("p (s n) -> p s n", n=P),
                                           scalar=vl[:, V_SUB:V_SUB + 1],
                                           in1=h_hi[:, 0:4, c0:c0 + P].bitcast(F32),
                                           op0=ALU.mult, op1=ALU.subtract).then_inc(oT_read, 1)
                dve.drain()
                for k in range(5):
                    if k < 4:
                        dve.drain()
                        V.scalar_tensor_tensor(out=tmp[:, k % 2, :], in0=y[:, k, :],
                                               scalar=vl[:, V_CNG + k:V_CNG + k + 1], in1=rb[:, :],
                                               op0=ALU.mult, op1=ALU.mult).then_inc(tmp_ready, 1)
                    if k:
                        dve.wait_ge(hh_ready, 20 * l + (KT + k))
                        ins = V.tensor_tensor(h_lo[:, 3 + k, :], tmp[:, (k - 1) % 2, :],
                                              h_hi[:, 3 + k, :].bitcast(F32), ALU.subtract)
                ins.then_inc(mix_ready, 1)
                mod_post(l, 3, 5, vl[:, V_BMOD + 5 * KT:V_BMOD + 6 * KT])

                def add_to_x(bank, vec, k, i, signal):
                    for c0, n, h, p0, s in PIECES:
                        g0 = (vec * KT + k) * 2 + s
                        gate = mf[:, g0:g0 + 1] if i is None else mf[:, ds(i * 4 + g0, 1)]
                        a = k * T + c0
                        xs = xf[:, a:a + n] if i is None else xf[:, ds(i * (2 * T) + a, n)]
                        ins = V.scalar_tensor_tensor(out=xs, in0=ps[:, bank + h, p0:p0 + n], scalar=gate, in1=xs,
                                                     op0=ALU.mult, op1=ALU.add)
                    ins.then_inc(signal, 1)

                def add_square(k, i, last):
                    dve.wait_ge(sq_ready, at(16 * l + (KT + k + 1), i, 2))
                    ins = V.tensor_tensor(ssq[:, :], ssq[:, :], sq[:, :], ALU.add)
                    if last:
                        ins.then_inc(ssq_ready, 1)
                    else:
                        dve.drain()

                V.memset(ssq[:, :], 0.0)
                for k in range(KT):
                    n = O_U + k // 2
                    if k % 2:
                        dve.wait_ge(unit_done[n % 2], done(l, n))
                    else:
                        dve.wait_ge(out_full, 4 * l + (k // 2 + 1))
                    add_to_x(2 * (k % 4), 2, k, None, x_ready)
                    add_square(k, None, k == KT - 1)
                    if k % 2:
                        split_lo(n + 2)
                norm(2, 3, V_N2, 12)
                nxt = (DEPTH - 1) - l
                for g in range(2):
                    mod_post(l, 4 + g, g, vecs[:, :, :].rearrange("p l n -> p (l n)")[
                        :, ds(nxt * V_N + (V_BMOD + g * KT), KT)])

                def up_post(c, b, i, j, nxt_size):
                    n, gate = UP_U[c] + j, CH0[c] + j
                    dve.wait_ge(up_read, at(22 * l + (gate + 3), i, 2))
                    for tap_i, off in ((0, 0), (2, 2)):
                        for s in range(2):
                            w = V_FFN + tap_i * V_FT + s * (V_FT // 2) + gate
                            ins = V.scalar_tensor_tensor(
                                out=cen[:, s, 1:T - 1], in0=ub[:, s, off:off + T - 2],
                                scalar=vl[:, w:w + 1] if i is None else vl[:, ds(i * 2 + w, 1)],
                                in1=cen[:, s, 1:T - 1], op0=ALU.mult, op1=ALU.add)
                        if tap_i == 0:
                            dve.drain()
                    ins.then_inc(taps_ready, 1)
                    split_lo(n + 2, i, nxt_size)
                    dve.wait_ge(silu_ready, at(22 * l + (gate + 1), i, 2))
                    V.tensor_tensor(gt[:, :], cen[:, 0, :], cen[:, 1, :], ALU.mult).then_inc(gm_ready, 1)
                    dve.wait_ge(gh_ready, at(22 * l + (gate + 1), i, 2))
                    dst, hi = ((g_lo[:, j * T:(j + 1) * T], g_hi[:, j * T:(j + 1) * T]) if i is None else
                               (g_lo[:, ds(i * (2 * T) + j * T, T)], g_hi[:, ds(i * (2 * T) + j * T, T)]))
                    V.tensor_tensor(dst, gt[:, :], hi.bitcast(F32), ALU.subtract).then_inc(g_ready, 1)

                for c in range(2):
                    pairs = CHUNKS[c] // 2
                    with dve.Fori(0, pairs - 1) as i:
                        for b in range(2):
                            up_post(c, b, i, b, SLOT)
                    for b in range(2):
                        up_post(c, b, None, 2 * (pairs - 1) + b, CHUNKS[c] * P)
                    if c:
                        V.memset(ssq[:, :], 0.0)
                        dve.drain()

                    def down_post(b, i, j):
                        dve.wait_ge(unit_done[b], at(done(l, DN_U[c] + j), i))
                        add_to_x(2 * b, 5, j, i, x_ready if c else dn_read)
                        if c:
                            add_square(KT + j, i, j == KT - 1)

                    with dve.Fori(0, 3) as i:
                        for b in range(2):
                            down_post(b, i, b)
                            split_lo(DN_U[c] + b + 2, i, CHUNKS[c] * P)
                    for b in range(2):
                        down_post(b, None, 6 + b)
                        if not c:
                            split_lo(DN_U[c] + 6 + b + 2)


def _tables():
    half = HD // 2
    nf = HD // 4
    inv = (10000.0 ** (-np.arange(nf, dtype=np.float32) / nf)).astype(np.float32)
    tok = np.arange(DEC)
    ang = np.concatenate([np.tile(pos.astype(np.float32)[:, None] * inv[None], (1, 2))
                          for pos in (tok // GRID_W, tok % GRID_W)], axis=1)
    sign = np.tile(np.repeat(np.float32([-1, 1]), nf), 2)
    both = np.stack([np.cos(ang), np.sin(ang) * sign]).astype(np.float32)
    assert both.shape == (2, DEC, 2 * half)
    return {"ident": np.eye(P, dtype=np.float32),
            "rope": np.ascontiguousarray(both.reshape(2, DEC // P, P, HD).transpose(2, 0, 1, 3))}


_INS = ['x_prompt', 'x_sample', 'cache_k', 'cache_v', 'c', 'c_ctx', 'w_mod', 'b_mod', 'norm1_g', 'w_in', 'q_norm_g',
        'k_norm_g', 'lambda_q1', 'lambda_k1', 'lambda_q2', 'lambda_k2', 'subln_g', 'conv_w', 'conv_norm_g', 'w_out',
        'norm2_g', 'w_up', 'ffn_conv_w', 'w_down']
_OUTS = [(1, SEQ, D), (1, DEC, D), (1, DEPTH, SEQ, NH, 2, HD), (1, DEPTH, SEQ, NH, VD)]


def kernel(**inputs):
    import concourse.bacc as _bacc
    from concourse.bass_utils import run_bass_kernel_spmd as _run

    nc = _bacc.Bacc("TRN2", target_bir_lowering=False, num_devices=1)
    tables = _tables()
    arrays, args = {}, []
    for name in _INS + ["ident", "rope"]:
        a = np.ascontiguousarray(inputs[name] if name in inputs else tables[name])
        arrays[f"in_{name}_dram"] = a
        args.append(nc.dram_tensor(f"in_{name}_dram", a.shape, mybir.dt.from_np(a.dtype), kind="ExternalInput").ap())
    for i, shape in enumerate(_OUTS):
        args.append(nc.dram_tensor(f"out_{i}_dram", shape, F32, kind="ExternalOutput").ap())
    hybrid_step(nc, *args)
    r = _run(nc, [arrays], core_ids=[0])
    return tuple(r.results[0][f"out_{i}_dram"] for i in range(len(_OUTS)))
```

```python
import math
from contextlib import ExitStack

import concourse.bass as bass
import numpy as np
from concourse import mybir

F32 = mybir.dt.float32
F32R = mybir.dt.float32r
ALU = mybir.AluOpType
ACT = mybir.ActivationFunctionType
AX = mybir.AxisListType
ds = bass.ds

P = 128
D = 1024
KT = D // P
DEPTH = 2
SEQ, DEC, PAST = 128, 512, 128
NH, HD, VD = 4, 64, 128
D_ATTN = D_CONV = 512
D_IN = 3 * D_ATTN + 3 * D_CONV
FF = 2816
NMOD = 6
GRID_W = 64
EPS = 1e-6
SCALE = HD ** -0.5

T = 644
HALF = T // 2
C_PROMPT, C_SAMPLE = 1, 130
TOK_TILES = [C_PROMPT] + [C_SAMPLE + P * i for i in range(DEC // P)]
NT = len(TOK_TILES)
SEQS = [(C_PROMPT, SEQ, 0), (C_SAMPLE, DEC, 1)]
PIECES = [(C_PROMPT, SEQ, 0, C_PROMPT, 0), (C_SAMPLE, HALF - C_SAMPLE, 0, C_SAMPLE, 1),
          (HALF, C_SAMPLE + DEC - HALF, 1, 0, 1)]
N_KEY = PAST + DEC
TILE_SEQ = [0] + [1] * (DEC // P)
K_PROMPT, K_PAST, K_SAMPLE = 0, SEQ, SEQ + PAST

UC = 256
SLOT = KT * UC
CHUNKS = [12, 10]
CH0 = [0, 12]
Q_U, C_U, O_U = 0, 6, 12
UP_U = [16, 36]
DN_U = [28, 46]
N_SPLIT = 54
SPLIT_SLOT = N_SPLIT // 2
MOD_PRE = 8
MOD_LAYER = 24
RAW_SLOT = (N_SPLIT + MOD_LAYER) // 2
RAW_PRE = MOD_PRE // 2
MOD_PRE_G, MOD_LAYER_G = MOD_PRE // 2, MOD_LAYER // 2
NORM1, MIXN, NORM2 = NT * KT, 2 * 4, 2 * KT
NORMED = NORM1 + MIXN + NORM2
LAG = 3
QUAD = 32


def load_order():
    mod = [("mod", j) for j in range(MOD_LAYER)]
    split = [("split", n) for n in range(UP_U[0] + 2)]
    order = split[0:2] + mod[0:4] + split[2:4]
    for h in range(2, 6):
        order += mod[2 * h:2 * h + 2] + split[h + 2:h + 3]
    order += split[8:14]
    for h in range(6, 10):
        order += mod[2 * h:2 * h + 2] + split[h + 8:h + 9]
    return order + mod[20:24]


ORDER = load_order()


def raw_of(n):
    return ORDER.index(("split", n)) if n < UP_U[0] + 2 else n + MOD_LAYER


def mod_raw(j):
    return ORDER.index(("mod", j))


V_BMOD, V_N1, V_N2, V_CONV, V_CNG, V_SUB, V_FFN = 0, 48, 56, 64, 76, 80, 128
V_ROWS0 = 81
V_FT = 2 * FF // P
V_N = V_FFN + 3 * V_FT
ROUNDS = NH * NT
HALVES = 24
N_SMALL = 15
LAM_INIT = [0.8 - 0.6 * math.exp(-0.3 * i) for i in range(DEPTH)]


def hybrid_step(nc, x_prompt, x_sample, cache_k, cache_v, c_sample, c_ctx, w_mod, b_mod, norm1_g, w_in, q_norm_g,
                k_norm_g, lambda_q1, lambda_k1, lambda_q2, lambda_k2, subln_g, conv_w, conv_norm_g, w_out,
                norm2_g, w_up, ffn_conv_w, w_down, ident_in, rope_in, y_prompt, y_sample, new_k, new_v):
    ctx = ExitStack()
    with ctx:
        def sb(name, shape, dt=F32, scope=None):
            return (scope or ctx).enter_context(nc.sbuf_tensor(name, shape, dt))

        def sem(name):
            return ctx.enter_context(nc.semaphore(name))

        x = sb("x", [P, KT, T])
        h_hi = sb("h_hi", [P, KT, T], F32R)
        h_lo = sb("h_lo", [P, KT, T], F32R)
        raw = sb("raw", [P, 2, SLOT])
        w_hi = sb("w_hi", [P, 2, SLOT], F32R)
        w_lo = sb("w_lo", [P, 2, SLOT], F32R)
        rb = sb("rb", [P, T])
        ssq = sb("ssq", [P, T])
        sq = sb("sq", [P, T])
        tmp = sb("tmp", [P, 2, T])
        ident = sb("ident", [P, P])
        ones = sb("ones", [P, P])
        junk = sb("junk", [P, VD])
        rope = sb("rope", [P, 2, 4, HD])
        rope_q = sb("rope_q", [P, 2, 2, 4, HD])
        vecs = sb("vecs", [P, DEPTH, V_N])
        vl = sb("vl", [P, V_N])
        modv = sb("modv", [P, NMOD, KT, 2])
        gain = sb("gain", [P, KT, 2])
        cT = sb("cT", [P, KT, QUAD])
        sel = sb("sel", [P, 2])
        mod_row = sb("mod_row", [P, 2 * UC])
        qkg = sb("qkg", [P, 2, DEPTH, HD])
        qkg_l = sb("qkg_l", [P, 2, HD])
        neglam = sb("neglam", [P, DEPTH])
        neglam_l = sb("neglam_l", [P, 1])
        lam_s = sb("lam_s", [P, 4])
        eps = sb("eps", [P, 1])
        st8 = sb("st8", [P, 2, 8])
        mx = sb("mx", [P, 2, 2])
        nbias = sb("nbias", [P, 2, 2])
        sums = sb("sums", [P, 2, 2])
        rec = sb("rec", [P, 2, 2])
        ssq_o = sb("ssq_o", [P, ROUNDS])

        mix = ExitStack()
        qT = sb("qT", [P, NH, NT * P], scope=mix)
        kT = sb("kT", [P, NH, K_SAMPLE + DEC], scope=mix)
        v = sb("v", [P, 6, D_ATTN], scope=mix)
        cgb = sb("cgb", [P, 2, T], scope=mix)
        tap = tmp
        y = sb("y", [P, 4, T], scope=mix)
        prep = ExitStack()
        qraw = sb("qraw", [P, 2, D_ATTN], scope=prep)
        qn = sb("qn", [P, NT, D_ATTN], scope=prep)
        rt = sb("rt", [P, 2, D_ATTN], scope=prep)
        kc = sb("kc", [P, D_ATTN], scope=prep)
        prep.close()
        stage = ExitStack()
        xin = sb("xin", [P, NT, D], scope=stage)
        stage.close()
        setup = ExitStack()
        att = ExitStack()
        probs = sb("probs", [P, 2, 2, N_KEY], scope=att)
        aT = rb
        o = sb("o", [P, ROUNDS, VD], scope=att)
        att.close()
        mix.close()
        mlp = ExitStack()
        g_hi = sb("g_hi", [P, CHUNKS[0] * T], F32R, scope=mlp)
        g_lo = sb("g_lo", [P, CHUNKS[0] * T], F32R, scope=mlp)
        ub = sb("ub", [P, 2, T], scope=mlp)
        cen = tmp
        gt = sb("gt", [P, T], scope=mlp)
        mlp.close()
        vrow = sb("vrow", [P, DEPTH, 3, P], scope=setup)
        crow = sb("crow", [P, P], scope=setup)
        brow = sb("brow", [1, 768], scope=setup)
        lamb = sb("lamb", [P, 4, DEPTH, HD], scope=setup)
        lamp = sb("lamp", [P, 2, DEPTH, HD], scope=setup)
        setup.close()

        ps = ctx.enter_context(nc.psum_tensor("ps", [P, 8, 512], F32))
        scores = ps[:, 2:5, :].rearrange("p b n -> p (b n)")
        probsT = ps[:, 5:7, :].rearrange("p b n -> p (b n)")

        tmp_t = tmp[:, :, :].rearrange("p a n -> p (a n)")[:, 0:KT * P].rearrange("p (k n) -> p k n", n=P)
        tmp_h = tmp[:, :, :].rearrange("p a (b n) -> p (a b) n", n=HALF)
        xf = x[:, :, :].rearrange("p t n -> p (t n)")
        mf = modv[:, :, :, :].rearrange("p v t s -> p (v t s)")

        raw_full = [sem("raw_full0"), sem("raw_full1")]
        hi_done = [sem("hi_done0"), sem("hi_done1")]
        split_full = [sem("split_full0"), sem("split_full1")]
        unit_done = [sem("unit_done0"), sem("unit_done1")]
        mod_used = sem("mod_used")
        row_read, modT_full, mod_ready = sem("row_read"), sem("modT_full"), sem("mod_ready")
        c_in, small_in, ffn_in, x_in, kv_in, out_done = (
            sem(s) for s in ("c_in", "small_in", "ffn_in", "x_in", "kv_in", "out_done"))
        bank3_first = sem("bank3_first")
        spacer = sem("spacer")
        sq_added, y_out = sem("sq_added"), sem("y_out")
        const_ready, silu_c, setup_full, setup_read = (sem("const_ready"), sem("silu_c"), sem("setup_full"),
                                                       sem("setup_read"))
        lam_ready, lam_exp, cT_ready = sem("lam_ready"), sem("lam_exp"), sem("cT_ready")
        xT_full, xT_read = sem("xT_full"), sem("xT_read")
        x_ready, sq_ready, ssq_ready = sem("x_ready"), sem("sq_ready"), sem("ssq_ready")
        stat_full, rms_ready = sem("stat_full"), sem("rms_ready")
        tmp_ready, hh_ready, h_ready = sem("tmp_ready"), sem("hh_ready"), sem("h_ready")
        qkv_full, qkv_read, qsq_ready, qsum_ready, qrms_ready, qk_ready, qkT_full, qkT_read, v_ready = (
            sem(s) for s in ("qkv_full", "qkv_read", "qsq_ready", "qsum_ready", "qrms_ready", "qk_ready",
                             "qkT_full", "qkT_read", "v_ready"))
        nk_out = sem("nk_out")
        conv_full, cg_read, xb_read = sem("conv_full"), sem("cg_read"), sem("xb_read")
        qk_full, max_ready, exp_done, a_ready, aT_full, aT_ready, pv_full, o_read = (
            sem(s) for s in ("qk_full", "max_ready", "exp_done", "a_ready", "aT_full", "aT_ready", "pv_full",
                             "o_read"))
        orms_ready, on_ready, oT_full, oT_hi, oT_read, mix_ready = (
            sem(s) for s in ("orms_ready", "on_ready", "oT_full", "oT_hi", "oT_read", "mix_ready"))
        out_full = sem("out_full")
        up_read, taps_ready, silu_ready, gm_ready, gh_ready, g_ready = (
            sem(s) for s in ("up_read", "taps_ready", "silu_ready", "gm_ready", "gh_ready", "g_ready"))
        dn_read = sem("dn_read")
        yT_full, yT_read = sem("yT_full"), sem("yT_read")

        block = ctx.enter_context(nc.Block())

        def done(l, n):
            return 1 + l * SPLIT_SLOT + n // 2 + 1

        def usable(l, n):
            return l * SPLIT_SLOT + n // 2 + 2

        def landed(l, r):
            return 32 * (RAW_PRE + 1) + l * (32 * RAW_SLOT) + 32 * (r // 2)

        def apart(eng):
            eng.sem_inc(spacer, 1)

        w_in_v = w_in.rearrange("l (t p) n -> p (l t) n", p=P)
        w_out_v = w_out.rearrange("l (t p) n -> p (l t) n", p=P)
        w_up_v = w_up.rearrange("l (t p) n -> p (l t) n", p=P)
        w_down_v = w_down.rearrange("l (t p) n -> p (l t) n", p=P)
        w_mod_v = w_mod.rearrange("l (t p) n -> p (l t) n", p=P)

        @block.sync
        def _(sp):
            def load(b, src, t0, tiles, cols, width):
                hf = tiles // 2
                dst = raw[:, b, 0:tiles * width].rearrange("p (t n) -> p t n", n=width)
                for s in range(2):
                    sp.dma_start(dst[:, s * hf:(s + 1) * hf, :],
                                 src[:, ds(t0 + s * hf, hf), ds(cols, width)]).then_inc(raw_full[b], 16)

            for u in range(MOD_PRE):
                if u >= 2:
                    sp.wait_ge(mod_used, u - 1)
                load(u % 2, w_mod_v, 0, KT, u * UC, UC)

            with sp.Fori(0, DEPTH) as l:
                def free_of_split(n):
                    sp.wait_ge(split_full[n % 2], usable(l, n))

                def free_of_mod(k):
                    sp.wait_ge(mod_used, l * MOD_LAYER + (MOD_PRE + k))

                def split_unit(n):
                    if n < C_U + 6:
                        if n < C_U:
                            col = n * UC
                        else:
                            pair, kind = divmod(n - C_U, 3)
                            col = 3 * D_ATTN + D_CONV * (1, 2, 0)[kind] + pair * UC
                        load(n % 2, w_in_v, l * KT, KT, col, UC)
                    else:
                        load(n % 2, w_out_v, l * KT, KT, (n - O_U) * UC, UC)

                def up_unit(b, j):
                    dst = raw[:, b, :].rearrange("p (s t n) -> p s t n", s=2, n=P)
                    for s in range(2):
                        sp.dma_start(dst[:, s, :, :], w_up_v[:, ds(l * KT, KT), ds(s * FF + j * P, P)]
                                     ).then_inc(raw_full[b], 16)

                def mod_unit(j, slot):
                    layer, unit = (l, j + 8) if j < 16 else ((DEPTH - 1) - l, j - 16)
                    load(slot, w_mod_v, layer * KT, KT, unit * UC, UC)

                for n in range(2):
                    sp.wait_ge(mod_used, l * MOD_LAYER + MOD_PRE)
                    sp.wait_ge(split_full[n], l * SPLIT_SLOT + 1)
                    split_unit(n)
                for r in range(2, len(ORDER)):
                    before, j = ORDER[r - 2]
                    free_of_split(j) if before == "split" else free_of_mod(j + 1)
                    kind, n = ORDER[r]
                    if kind == "mod":
                        apart(sp)
                        mod_unit(n, r % 2)
                    elif n < UP_U[0]:
                        split_unit(n)
                    else:
                        up_unit(n % 2, n - UP_U[0])
                for b in range(2):
                    free_of_mod(24 - 1 + b)
                    up_unit(b, 2 + b)
                with sp.Fori(0, CHUNKS[0] // 2 - 2) as i:
                    for b in range(2):
                        sp.wait_ge(split_full[b], l * SPLIT_SLOT + ((UP_U[0] + 2) // 2 + 2) + i)
                        up_unit(b, 2 * i + (4 + b))
                for c in range(2):
                    if c == 1:
                        with sp.Fori(0, CHUNKS[1] // 2) as i:
                            for b in range(2):
                                sp.wait_ge(split_full[b], l * SPLIT_SLOT + (UP_U[1] // 2 + 1) + i)
                                up_unit(b, 2 * i + (CH0[1] + b))
                    with sp.Fori(0, 4) as i:
                        for b in range(2):
                            sp.wait_ge(split_full[b], l * SPLIT_SLOT + (DN_U[c] // 2 + 1) + i)
                            load(b, w_down_v, l * (FF // P) + CH0[c], CHUNKS[c], (2 * i + b) * P, P)

            for t in range(NT):
                sp.wait_ge(yT_read, 2 * t + 2)
                dst = y_prompt[0] if t == 0 else y_sample[0, (t - 1) * P:t * P, :]
                sp.dma_start(dst, xin[:, t, :]).then_inc(y_out, 16)
            sp.wait_ge(y_out, 16 * NT)

        @block.gpsimd
        def _(pool):
            ck = cache_k.rearrange("b l p h s d -> p (b l) (h s d)")
            cv = cache_v.rearrange("b l p h e -> p (b l) (h e)")
            nk = new_k.rearrange("b l p h s d -> p (b l) (h s d)")
            nv = new_v.rearrange("b l p h e -> p (b l) (h e)")
            with pool.Fori(0, DEPTH) as l:
                pool.wait_ge(stat_full, 3 * l + 1)
                pool.dma_start(kc[:, :], ck[:, ds(l, 1), :].rearrange("p a n -> p (a n)")).then_inc(kv_in, 16)
                pool.dma_start(v[:, 1, :], cv[:, ds(l, 1), :].rearrange("p a n -> p (a n)")).then_inc(kv_in, 16)
                pool.wait_ge(qk_ready, 2 * NT * l + NT + 1)
                apart(pool)
                pool.dma_start(nk[:, ds(l, 1), :].rearrange("p a n -> p (a n)"), qn[:, 0, :]).then_inc(nk_out, 16)
                pool.wait_ge(v_ready, NT * l + 1)
                apart(pool)
                pool.dma_start(nv[:, ds(l, 1), :].rearrange("p a n -> p (a n)"), v[:, 0, :]).then_inc(out_done, 16)
            pool.wait_ge(out_done, 16 * DEPTH)
            pool.wait_ge(nk_out, 16 * DEPTH)

        @block.tensor
        def _(pe):
            mm = nc.tensor.matmul

            def gemm(out, b, kt, width, col, mov_hi, mov_lo, first=True, last=True):
                wh = w_hi[:, b, 0:kt * width].rearrange("p (t n) -> p t n", n=width)
                wl = w_lo[:, b, 0:kt * width].rearrange("p (t n) -> p t n", n=width)
                for k in range(kt):
                    mm(out, wh[:, k, col:col + P], mov_hi(k), start=first and k == 0, stop=False)
                    mm(out, wh[:, k, col:col + P], mov_lo(k), start=False, stop=False)
                    ins = mm(out, wl[:, k, col:col + P], mov_hi(k), start=False, stop=last and k == kt - 1)
                return ins

            def mod_sum(l, h, u, b, landed_at):
                pe.wait_ge(raw_full[b], landed_at)
                if u == 0:
                    if l is not None:
                        pe.wait_ge(mod_ready, MOD_LAYER_G * l + h + MOD_PRE_G)
                    elif h:
                        pe.wait_ge(mod_ready, h)
                wu = raw[:, b, :].rearrange("p (t n) -> p t n", n=UC)
                for part in range(2):
                    for q in range(4):
                        k = 4 * part + q
                        ins = mm(ps[QUAD * q:QUAD * (q + 1), 7, u * UC:(u + 1) * UC], cT[:, k, :], wu[:, k, :],
                                 start=part == 0, stop=part == 1)
                ins.then_inc(mod_used, 1)

            def mod_turn(l, h):
                if l is None:
                    pe.wait_ge(row_read, h + 1)
                else:
                    pe.wait_ge(row_read, MOD_LAYER_G * l + h + (MOD_PRE_G + 1))
                    apart(pe)
                for t in range(4):
                    ins = mm(ps[:, 7, 2 * t:2 * t + 2], mod_row[:, t * P:(t + 1) * P], sel[:, :],
                             start=True, stop=True)
                ins.then_inc(modT_full, 1)

            def stat(l, which):
                pe.wait_ge(ssq_ready, 3 * l + (1 + which))
                for h in range(2):
                    ins = mm(ps[:, h, 0:HALF], ones[:, :], ssq[:, h * HALF:(h + 1) * HALF], start=True, stop=True)
                ins.then_inc(stat_full, 1)

            pe.sem_inc(unit_done[0], 1)
            pe.sem_inc(unit_done[1], 1)
            def pre_sum(h):
                for u in range(2):
                    mod_sum(None, h, u, u, 32 * (h + 1))

            def x_sample(ks):
                for k in ks:
                    bank = (2 + k) % 5
                    if k >= 3:
                        pe.wait_ge(xT_read, k - 2)
                    for t in range(4):
                        ins = nc.tensor.transpose(ps[:, bank, t * P:(t + 1) * P], xin[:, 1 + t, k * P:(k + 1) * P],
                                                  ident[:, :])
                    ins.then_inc(xT_full, 1)

            pe.wait_ge(c_in, 48)
            pe.wait_ge(silu_c, 1)
            nc.tensor.transpose(ps[:, 0, 0:P], crow[:, :], ident[:, :]).then_inc(setup_full, 1)
            pe.wait_ge(cT_ready, 1)
            pre_sum(0)
            pe.wait_ge(x_in, 32)
            pe.wait_ge(setup_read, 1)
            for j in range(2):
                for t in range(4):
                    ins = nc.tensor.transpose(ps[:, j, t * P:(t + 1) * P],
                                              xin[:, 0, (4 * j + t) * P:(4 * j + t + 1) * P], ident[:, :])
                ins.then_inc(xT_full, 1)
            mod_turn(None, 0)
            pe.wait_ge(small_in, 16 * N_SMALL)
            pe.wait_ge(ffn_in, 64)
            for l in range(DEPTH):
                for r in range(3):
                    ins = nc.tensor.transpose(ps[:, 2 + l, r * P:(r + 1) * P], vrow[:, l, r, :], ident[:, :])
                ins.then_inc(setup_full, 1)
            mm(ps[:, 4, :], ones[0:1, :], brow[0:1, 0:512], start=True, stop=True).then_inc(setup_full, 1)
            mm(ps[:, 5, 0:256], ones[0:1, :], brow[0:1, 512:768], start=True, stop=True).then_inc(setup_full, 1)
            pre_sum(1)
            pe.wait_ge(setup_read, 5)
            x_sample(range(0, 3))
            mod_turn(None, 1)
            x_sample(range(3, 5))
            pre_sum(2)
            x_sample(range(5, KT))
            mod_turn(None, 2)
            pre_sum(3)
            mod_turn(None, 3)

            with pe.Fori(0, DEPTH) as l:
                stat(l, 0)

                def qkv_unit(b, t, c0, signal, follow=False):
                    col = TOK_TILES[t]
                    wh = w_hi[:, b, :].rearrange("p (t n) -> p t n", n=UC)
                    wl = w_lo[:, b, :].rearrange("p (t n) -> p t n", n=UC)
                    out = ps[:, t, c0:c0 + UC]
                    for k in range(KT):
                        if follow:
                            pe.wait_ge(h_ready, (NORM1 + NORM2) * l + (t * KT + k + 1))
                        mm(out, h_hi[:, k, col:col + P], wh[:, k, :], start=k == 0, stop=False)
                        mm(out, h_hi[:, k, col:col + P], wl[:, k, :], start=False, stop=False)
                        ins = mm(out, h_lo[:, k, col:col + P], wh[:, k, :], start=False, stop=k == KT - 1)
                    if t == NT - 1:
                        ins.then_inc(unit_done[b], 1)
                    elif signal:
                        ins.then_inc(qkv_full, 1)

                pe.wait_ge(rms_ready, 3 * l + 1)
                pe.wait_ge(kv_in, 32 * l + 32)
                for s in range(4):
                    ins = nc.tensor.transpose(ps[:, 5, s * P:(s + 1) * P], kc[:, s * P:(s + 1) * P], ident[:, :])
                ins.then_inc(qkT_full, 1)
                def pair_steps(h, b, t):
                    u = t // 2
                    if t == 0:
                        mod_turn(l, h - 1)
                    elif t % 2:
                        slot = b if u == 0 else 1 - b
                        r2 = mod_raw(4 + 2 * b + u) // 2
                        mod_sum(l, h, u, slot,
                                l * (32 * RAW_SLOT) + (h - b) * 48 + (32 * (RAW_PRE + 1 + r2) - 96))

                pe.wait_ge(split_full[0], usable(l, 0))
                for b, t in ((0, 0), (1, 0), (0, 1), (1, 1), (0, 2), (0, 3), (0, 4), (1, 2), (1, 3), (1, 4)):
                    if (b, t) == (1, 0):
                        pe.wait_ge(split_full[1], usable(l, 1))
                    qkv_unit(b, t, b * UC, b == 1, follow=b == 0)
                    if (b, t) == (1, 0):
                        mod_sum(l, 0, 0, 0, landed(l, mod_raw(0)))
                    elif (b, t) == (1, 1):
                        mod_sum(l, 0, 1, 1, landed(l, mod_raw(1)))
                    elif (b, t) == (0, 2):
                        mod_turn(l, 0)
                    elif (b, t) == (0, 3):
                        mod_sum(l, 1, 0, 0, landed(l, mod_raw(2)))
                    elif (b, t) == (0, 4):
                        mod_sum(l, 1, 1, 1, landed(l, mod_raw(3)))
                with pe.Fori(1, 3) as p:
                    pe.wait_ge(split_full[0], l * SPLIT_SLOT + 2 + p)
                    for t in range(NT):
                        pe.wait_ge(qkv_read, 2 * NT * l + NT * p + (t + 1 - NT))
                        qkv_unit(0, t, 0, False)
                        pair_steps(2 * p, 0, t)
                        pe.wait_ge(qk_ready, 2 * NT * l + NT * p + (t + 1 - NT))
                        if t != 1:
                            pe.wait_ge(qkT_read, 11 * l + NT * p + (t - NT + (t == 0)))
                        for s in range(4):
                            ins = nc.tensor.transpose(ps[:, 5 + t % 2, s * P:(s + 1) * P],
                                                      qn[:, t, s * P:(s + 1) * P], ident[:, :])
                        ins.then_inc(qkT_full, 1)
                    pe.wait_ge(split_full[1], l * SPLIT_SLOT + 2 + p)
                    for t in range(NT):
                        qkv_unit(1, t, UC, True)
                        pair_steps(2 * p + 1, 1, t)

                def conv_half(i):
                    n = C_U + i // 4
                    b, tile, h = n % 2, (i % 4) // 2, i % 2
                    if i % 4 == 0:
                        pe.wait_ge(split_full[b], usable(l, n))
                    if i >= 2:
                        j = i - 2
                        if (j // 4) % 3 == 0:
                            pe.wait_ge(cg_read, 8 * l + (4 * (j // 12) + j % 4 + 1))
                        else:
                            pe.wait_ge(xb_read, 16 * l + (8 * (j // 12) + (j % 12) - 4 + 1))
                    ins = gemm(ps[:, h, 0:HALF], b, KT, UC, tile * P,
                               lambda k: h_hi[:, k, h * HALF:(h + 1) * HALF],
                               lambda k: h_lo[:, k, h * HALF:(h + 1) * HALF])
                    ins.then_inc(unit_done[b] if i % 4 == 3 else conv_full, 1)

                def qk_scores(i):
                    hd, t = divmod(i, NT)
                    if i:
                        pe.wait_ge(exp_done, ROUNDS * l + i)
                    else:
                        pe.wait_ge(qkT_read, 11 * l + 11)
                    for s in range(2):
                        if t == 0:
                            parts, k0 = [(0, SEQ)], K_PROMPT
                        else:
                            parts, k0 = ([(512, N_KEY), (0, 512)], [(384, N_KEY), (0, 384)])[s], K_PAST
                        for j, (a, e) in enumerate(parts):
                            if s and j:
                                pe.wait_ge(bank3_first, (ROUNDS - NH) * l + (hd * (NT - 1) + t))
                            ins = mm(scores[:, s * N_KEY + a:s * N_KEY + e],
                                     qT[s * HD:(s + 1) * HD, hd, t * P:(t + 1) * P],
                                     kT[s * HD:(s + 1) * HD, hd, k0 + a:k0 + e], start=True, stop=True)
                            if s == 0 and j == 0 and t:
                                ins.then_inc(bank3_first, 1)
                    ins.then_inc(qk_full, 1)

                def key_tiles(i):
                    return [0] if i % NT == 0 else [1, 2, 3, 4, 5]

                def transposes(i):
                    pe.wait_ge(a_ready, ROUNDS * l + (i + 1))
                    if i:
                        pe.wait_ge(aT_ready, ROUNDS * l + i)
                    for j in range(len(key_tiles(i))):
                        ins = nc.tensor.transpose(probsT[:, j * P:(j + 1) * P], probs[:, i % 2, 0, j * P:(j + 1) * P],
                                                  ident[:, :])
                    ins.then_inc(aT_full, 1)

                def pv(i):
                    pe.wait_ge(aT_ready, ROUNDS * l + (i + 1))
                    if i:
                        pe.wait_ge(o_read, ROUNDS * l + i)
                    else:
                        pe.wait_ge(mod_ready, MOD_LAYER_G * l + (MOD_PRE_G + 6))
                    tiles, hd = key_tiles(i), i // NT
                    for j, kt in enumerate(tiles):
                        ins = mm(ps[:, 7, 0:VD], aT[:, j * P:(j + 1) * P], v[:, kt, hd * VD:(hd + 1) * VD],
                                 start=j == 0, stop=j == len(tiles) - 1)
                    ins.then_inc(pv_full, 1)

                pe.wait_ge(v_ready, NT * l + NT)
                for i in range(HALVES):
                    conv_half(i)
                    if i == 0:
                        mod_turn(l, 5)
                    if i < ROUNDS:
                        qk_scores(i)
                    if 2 <= i < ROUNDS + 2:
                        pv(i - 2)
                    if 1 <= i < ROUNDS + 1:
                        transposes(i - 1)

                pe.wait_ge(on_ready, l + 1)
                for t in range(NT):
                    for hd in range(NH):
                        ins = nc.tensor.transpose(ps[:, 2 + t, hd * P:(hd + 1) * P], o[:, hd * NT + t, :],
                                                  ident[:, :])
                    ins.then_inc(oT_full, 1)
                stat(l, 1)

                def out_unit(n, b):
                    steps = [(0, 0), (1, 0), (0, 1), (1, 1)] if n == 0 else [(0, 0), (0, 1), (1, 0), (1, 1)]
                    for i, (j, h) in enumerate(steps):
                        if (i % 2 == 0) if n else h == 0:
                            pe.wait_ge(x_ready, 16 * l + (2 * n + j + 7))
                        wh = w_hi[:, b, :].rearrange("p (t n) -> p t n", n=UC)[:, :, j * P:(j + 1) * P]
                        wl = w_lo[:, b, :].rearrange("p (t n) -> p t n", n=UC)[:, :, j * P:(j + 1) * P]
                        out = ps[:, 2 * j + h, 0:HALF]
                        for k in range(KT):
                            if n == 0 and j == 0:
                                if k == 0:
                                    pe.wait_ge(oT_read, NT * l + (NT if h else 3))
                                elif k >= 4:
                                    pe.wait_ge(mix_ready, MIXN * l + (4 * h + k - 3))
                            hh = h_hi[:, k, h * HALF:(h + 1) * HALF]
                            mm(out, wh[:, k, :], hh, start=k == 0, stop=False)
                            mm(out, wh[:, k, :], h_lo[:, k, h * HALF:(h + 1) * HALF], start=False, stop=False)
                            ins = mm(out, wl[:, k, :], hh, start=False, stop=k == KT - 1)
                        if i == 3:
                            ins.then_inc(unit_done[b], 1)
                        elif (j, h) == (0, 1):
                            ins.then_inc(out_full, 1)
                        if i == 0 and n:
                            mod_turn(l, n + 5)
                        elif i in (1, 2):
                            mod_sum(l, n + 6, i - 1, (b + i - 1) % 2, landed(l, mod_raw(2 * n + 11 + i)))

                pe.wait_ge(rms_ready, 3 * l + 2)
                pe.wait_ge(o_read, ROUNDS * l + ROUNDS)
                for n in range(4):
                    pe.wait_ge(split_full[n % 2], usable(l, O_U + n))
                    out_unit(n, n % 2)
                mod_turn(l, 9)
                stat(l, 2)
                def up_half(b, h, ks=(0, KT), follow=False):
                    w = [[half[:, b, s * KT * P:(s + 1) * KT * P].rearrange("p (t n) -> p t n", n=P)
                          for s in range(2)] for half in (w_hi, w_lo)]
                    for k in range(*ks):
                        if follow:
                            pe.wait_ge(h_ready, (NORM1 + NORM2) * l + (NORM1 + KT * h + k + 1))
                        hh, hl = (part[:, k, h * HALF:(h + 1) * HALF] for part in (h_hi, h_lo))
                        for s in range(2):
                            out = ps[:, 4 * b + 2 * s + h, 0:HALF]
                            mm(out, w[0][s][:, k, :], hh, start=k == 0, stop=False)
                            mm(out, w[0][s][:, k, :], hl, start=False, stop=False)
                            ins = mm(out, w[1][s][:, k, :], hh, start=False, stop=k == KT - 1)
                    if h and ks[1] == KT:
                        ins.then_inc(unit_done[b], 1)

                def up_pair_sum(h, u):
                    mod_sum(l, h, u, u, landed(l, mod_raw(2 * h + u)))

                up_pair_sum(10, 0)
                pe.wait_ge(split_full[0], usable(l, UP_U[0]))
                pe.wait_ge(rms_ready, 3 * l + 3)
                pe.wait_ge(up_read, 22 * l + 1)
                up_half(0, 0, follow=True)
                up_pair_sum(10, 1)
                up_half(0, 1, (0, 4), follow=True)
                mod_turn(l, 10)
                up_half(0, 1, (4, KT), follow=True)
                for u in range(2):
                    up_pair_sum(11, u)
                pe.wait_ge(split_full[1], usable(l, UP_U[0] + 1))
                pe.wait_ge(up_read, 22 * l + 2)
                up_half(1, 0)
                mod_turn(l, 11)
                pe.wait_ge(mod_ready, MOD_LAYER_G * l + (MOD_PRE_G + MOD_LAYER_G))
                apart(pe)
                up_half(1, 1)

                for c in range(2):
                    if c:
                        pe.wait_ge(dn_read, 8 * l + (2 + 8))
                    apart(pe)
                    with pe.Fori(1 - c, CHUNKS[c] // 2) as i:
                        for b in range(2):
                            pe.wait_ge(split_full[b], l * SPLIT_SLOT + (UP_U[c] // 2 + 2) + i)
                            pe.wait_ge(up_read, 22 * l + 2 * i + (CH0[c] + b + 1))
                            for h in range(2):
                                up_half(b, h)

                    def down(b, k0, k1):
                        kf = CHUNKS[c]
                        wh, wl = (half[:, b, 0:kf * P].rearrange("p (t n) -> p t n", n=P) for half in (w_hi, w_lo))
                        for h in range(2):
                            out = ps[:, 2 * b + h, 0:HALF]
                            for k in range(k0, k1):
                                gh, gl = (g[:, k * T + h * HALF:k * T + (h + 1) * HALF] for g in (g_hi, g_lo))
                                mm(out, wh[:, k, :], gh, start=k == 0, stop=False)
                                mm(out, wh[:, k, :], gl, start=False, stop=False)
                                ins = mm(out, wl[:, k, :], gh, start=False, stop=k == kf - 1)
                        if k1 == kf:
                            ins.then_inc(unit_done[b], 1)

                    for part in range(2):
                        pe.wait_ge(g_ready, 22 * l + (CH0[c] + CHUNKS[c] - (0 if part else 2)))
                        apart(pe)
                        for b in range(2):
                            if part == 0:
                                pe.wait_ge(split_full[b], usable(l, DN_U[c] + b))
                                if c == 0:
                                    pe.wait_ge(dn_read, 8 * l + (b + 1))
                                else:
                                    pe.wait_ge(x_ready, 16 * l + (b + 15))
                                down(b, 0, CHUNKS[c] - 2)
                            else:
                                down(b, CHUNKS[c] - 2, CHUNKS[c])
                    with pe.Fori(1, 4) as i:
                        for b in range(2):
                            pe.wait_ge(split_full[b], l * SPLIT_SLOT + (DN_U[c] // 2 + 2) + i)
                            if c == 0:
                                pe.wait_ge(dn_read, 8 * l + 2 * i + (b + 1))
                            else:
                                pe.wait_ge(x_ready, 16 * l + 2 * i + (b + 15))
                            down(b, 0, CHUNKS[c])

            pe.wait_ge(ssq_ready, 3 * DEPTH + 1)
            for j in range(2 * NT):
                t, kh = j // 2, j % 2
                if j >= 8:
                    pe.wait_ge(yT_read, j - 7)
                for s in range(4):
                    k = 4 * kh + s
                    ins = nc.tensor.transpose(ps[:, j % 8, s * P:(s + 1) * P],
                                              x[:, k, TOK_TILES[t]:TOK_TILES[t] + P], ident[:, :])
                ins.then_inc(yT_full, 1)

        def at(expr, i, by=1):
            return expr if i is None else expr + i * by

        @block.scalar
        def _(act):
            A = nc.scalar.activation

            def rows(l, h):
                act.wait_ge(mod_used, 2 * h + 2 if l is None else MOD_LAYER * l + (MOD_PRE + 2 * h + 2))
                A(mod_row[:, :], ps[:, 7, :], ACT.Copy).then_inc(row_read, 1)

            act.wait_ge(const_ready, 1)
            act.dma_start(crow[0:KT, :], c_ctx.rearrange("(t n) -> t n", n=P)).then_inc(c_in, 16)
            act.dma_start(crow[KT:2 * KT, :], c_sample.rearrange("b (t n) -> (b t) n", n=P)).then_inc(c_in, 16)
            act.dma_start(ident[:, :], ident_in).then_inc(c_in, 16)
            act.dma_start(xin[:, 0, :], x_prompt[0]).then_inc(x_in, 16)
            act.dma_start(xin[:, 1:NT, :], x_sample[0].rearrange("(t p) n -> p t n", p=P)).then_inc(x_in, 16)
            act.wait_ge(c_in, 48)
            A(crow[:, :], crow[:, :], ACT.Silu).then_inc(silu_c, 1)
            act.wait_ge(const_ready, 2)
            small = [(rope[:, :, :, :], rope_in)]
            for src, r0, n in ((b_mod, V_BMOD, 48), (norm1_g, V_N1, KT), (norm2_g, V_N2, KT),
                               (conv_norm_g, V_CNG, 4), (subln_g, V_SUB, 1)):
                small.append((vrow[r0:r0 + n, :, 0, :], src.rearrange("l (t n) -> t l n", n=P)))
            for j in range(3):
                small.append((vrow[V_CONV + 4 * j:V_CONV + 4 * j + 4, :, 0, :],
                              conv_w[:, j, :].rearrange("l (t n) -> t l n", n=P)))
            for i, src in enumerate((lambda_q1, lambda_k1, lambda_q2, lambda_k2, q_norm_g, k_norm_g)):
                small.append((brow[0:1, i * P:(i + 1) * P], src.rearrange("(a l) n -> a (l n)", a=1)))
            assert len(small) == N_SMALL
            for dst, src in small:
                act.dma_start(dst, src).then_inc(small_in, 16)
            for l in range(DEPTH):
                fr = ffn_conv_w[l].rearrange("w (t n) -> (w t) n", n=P)
                act.dma_start(vrow[:, l, 1, :], fr[0:P, :]).then_inc(ffn_in, 16)
                act.dma_start(vrow[0:3 * V_FT - P, l, 2, :], fr[P:3 * V_FT, :]).then_inc(ffn_in, 16)
            rows(None, 0)
            act.wait_ge(lam_ready, 1)
            A(lam_s[:, :], lam_s[:, :], ACT.Exp).then_inc(lam_exp, 1)
            rows(None, 1)
            for k in range(KT):
                if k == 3:
                    rows(None, 2)
                act.wait_ge(xT_read, k + 3)
                if k:
                    act.wait_ge(sq_added, k)
                A(sq[:, :], x[:, k, :], ACT.Square).then_inc(sq_ready, 1)
            rows(None, 3)

            with act.Fori(0, DEPTH) as l:
                def split_hi(n, i=None, size=SLOT):
                    b = n % 2
                    act.wait_ge(raw_full[b], at(landed(l, raw_of(n)), i, 32))
                    act.wait_ge(unit_done[b], at(l * SPLIT_SLOT + (n // 2 + 1), i))
                    A(w_hi[:, b, 0:size], raw[:, b, 0:size], ACT.Copy).then_inc(hi_done[b], 1)

                def rms(which, scale):
                    act.wait_ge(stat_full, 3 * l + (1 + which))
                    A(rb[:, :].rearrange("p (h n) -> p h n", h=2), ps[:, 0:2, 0:HALF], ACT.Sqrt,
                      bias=eps[:, :], scale=scale).then_inc(rms_ready, 1)

                def norm_hi(base, k, dst_src, vec):
                    act.wait_ge(tmp_ready, NORMED * l + (base + k + 1))
                    for dst, src, s in dst_src:
                        ins = A(dst, src, ACT.Identity, bias=modv[:, vec, k, s:s + 1])
                    ins.then_inc(hh_ready, 1)

                split_hi(0)
                rms(0, 1.0 / D)
                for t in range(NT):
                    for k in range(KT):
                        norm_hi(t * KT, k, [(h_hi[:, k, TOK_TILES[t]:TOK_TILES[t] + P], tmp_t[:, k, :],
                                             TILE_SEQ[t])], 0)
                    if t == 0:
                        split_hi(1)
                    if t == 3:
                        rows(l, 0)

                def qk_copy(n):
                    bank = 5 if n == 0 else 5 + (n - 1) % NT % 2
                    if n == 0:
                        dst = kT[:, :, K_PAST:K_PAST + P]
                    elif n <= NT:
                        dst = qT[:, :, (n - 1) * P:n * P]
                    else:
                        t = n - 1 - NT
                        c0 = K_PROMPT if t == 0 else K_SAMPLE + (t - 1) * P
                        dst = kT[:, :, c0:c0 + P]
                    act.wait_ge(qkT_full, 11 * l + (n + 1))
                    A(dst, ps[:, bank, :].rearrange("p (s n) -> p s n", n=P), ACT.Copy).then_inc(qkT_read, 1)

                qk_copy(0)
                for p in range(3):
                    for t in range(NT):
                        if t == NT - 1 and p:
                            rows(l, 2 * p)
                        if p:
                            qk_copy(1 + (p - 1) * NT + t)
                    split_hi(2 * p + 2)
                    if p == 0:
                        rows(l, 1)
                    for t in range(NT):
                        if t == NT - 1 and p:
                            rows(l, 2 * p + 1)
                        if t < NT - 1:
                            act.wait_ge(qkv_full, 12 * l + (4 * p + t + 1))
                        else:
                            act.wait_ge(unit_done[1], done(l, 2 * p + 1))
                        if p == 2:
                            A(v[:, t + (t > 0), :], ps[:, t, :], ACT.Copy).then_inc(v_ready, 1)
                            continue
                        n = NT * p + t
                        A(sq[:, 0:D_ATTN], ps[:, t, :], ACT.Square).then_inc(qsq_ready, 1)
                        if n >= 2:
                            act.wait_ge(qk_ready, 2 * NT * l + (n - 1))
                        A(qraw[:, n % 2, :], ps[:, t, :], ACT.Copy).then_inc(qkv_read, 1)
                        act.wait_ge(qsum_ready, 2 * NT * l + (n + 1))
                        A(st8[:, n % 2, :], st8[:, n % 2, :], ACT.Sqrt, bias=eps[:, :], scale=1.0 / HD
                          ).then_inc(qrms_ready, 1)
                    split_hi(2 * p + 3)

                for i in range(HALVES):
                    unit, tile, h = i // 4, (i % 4) // 2, i % 2
                    if i % 4 == 0 and unit:
                        split_hi(C_U + unit + 1)
                    if unit % 3 == 0:
                        if i == 12:
                            act.wait_ge(xb_read, 16 * l + 8)
                        if i % 4 == 3:
                            act.wait_ge(unit_done[unit % 2], done(l, C_U + unit))
                        else:
                            act.wait_ge(conv_full, 18 * l + (3 * unit + i % 4 + 1))
                        A(cgb[:, tile, h * HALF:(h + 1) * HALF], ps[:, h, 0:HALF], ACT.Copy).then_inc(cg_read, 1)
                    if 1 <= i < ROUNDS + 1:
                        w = P if (i - 1) % NT == 0 else N_KEY
                        act.wait_ge(aT_full, ROUNDS * l + i)
                        A(aT[:, 0:w], probsT[:, 0:w], ACT.Copy).then_inc(aT_ready, 1)
                    if i < ROUNDS:
                        w = P if i % NT == 0 else N_KEY
                        if i == 0:
                            act.wait_ge(nk_out, 16 * l + 16)
                            act.wait_ge(out_done, 16 * l + 16)
                        act.wait_ge(max_ready, ROUNDS * l + (i + 1))
                        for s in range(2):
                            ins = A(probs[:, i % 2, s, 0:w], scores[:, s * N_KEY:s * N_KEY + w], ACT.Exp,
                                    bias=nbias[:, i % 2, s:s + 1], scale=SCALE,
                                    accum_out=sums[:, i % 2, s:s + 1])
                        ins.then_inc(exp_done, 1)
                    if 2 <= i < ROUNDS + 2:
                        r = i - 2
                        act.wait_ge(pv_full, ROUNDS * l + (r + 1))
                        A(o[:, r, :], ps[:, 7, 0:VD], ACT.Copy)
                        A(junk[:, :], ps[:, 7, 0:VD], ACT.Square, accum_out=ssq_o[:, r:r + 1]
                          ).then_inc(o_read, 1)
                        if r == ROUNDS - 1:
                            act.drain()
                            A(ssq_o[:, :], ssq_o[:, :], ACT.Sqrt, bias=eps[:, :], scale=1.0 / VD
                              ).then_inc(orms_ready, 1)

                for t in range(NT):
                    c0 = TOK_TILES[t]
                    act.wait_ge(oT_full, NT * l + (t + 1))
                    A(h_hi[:, 0:4, c0:c0 + P], ps[:, 2 + t, :].rearrange("p (s n) -> p s n", n=P), ACT.Copy,
                      scale=vl[:, V_SUB:V_SUB + 1]).then_inc(oT_hi, 1)
                    if t == 2:
                        rms(1, 1.0 / D_CONV)
                for h in range(2):
                    for k in range(4):
                        act.wait_ge(tmp_ready, NORMED * l + (NORM1 + 4 * h + k + 1))
                        A(h_hi[:, 4 + k, h * HALF:(h + 1) * HALF], tmp_h[:, k, :], ACT.Copy).then_inc(hh_ready, 1)
                split_hi(C_U + 7)

                def square(k, i=None):
                    act.wait_ge(x_ready, at(16 * l + (KT + k + 1), i, 2))
                    kx = at(k % KT * T, i, 2 * T)
                    A(sq[:, :], xf[:, ds(kx, T)] if i is not None else xf[:, kx:kx + T], ACT.Square
                      ).then_inc(sq_ready, 1)

                for n in range(4):
                    square(2 * n)
                    rows(l, 6 + n)
                    square(2 * n + 1)
                    split_hi(O_U + n + 2)
                rms(2, 1.0 / D)
                for h in range(2):
                    for k in range(KT):
                        norm_hi(NORM1 + MIXN + KT * h, k,
                                [(h_hi[:, k, c0:c0 + n], tmp_h[:, k % 4, p0:p0 + n], s)
                                 for c0, n, hf, p0, s in PIECES if hf == h], 3)
                        if h and k == 3:
                            rows(l, 10)
                rows(l, 11)

                def up_post(c, b, i, j, nxt_size):
                    n = UP_U[c] + j
                    gate = CH0[c] + j
                    act.wait_ge(unit_done[b], at(done(l, n), i))
                    both = ps[:, 4 * b:4 * b + 4, 0:HALF]
                    A(ub[:, :, :].rearrange("p s (h n) -> p (s h) n", h=2), both, ACT.Copy)
                    for s in range(2):
                        w = V_FFN + V_FT + s * (V_FT // 2) + gate
                        ins = A(cen[:, s, :].rearrange("p (h n) -> p h n", h=2), both[:, 2 * s:2 * s + 2, :],
                                ACT.Copy, scale=vl[:, w:w + 1] if i is None else vl[:, ds(i * 2 + w, 1)])
                    ins.then_inc(up_read, 1)
                    split_hi(n + 2, i, nxt_size)
                    act.wait_ge(taps_ready, at(22 * l + (gate + 1), i, 2))
                    A(cen[:, 0, :], cen[:, 0, :], ACT.Silu).then_inc(silu_ready, 1)
                    act.wait_ge(gm_ready, at(22 * l + (gate + 1), i, 2))
                    A(g_hi[:, j * T:(j + 1) * T] if i is None else g_hi[:, ds(i * (2 * T) + j * T, T)],
                      gt[:, :], ACT.Copy).then_inc(gh_ready, 1)

                for c in range(2):
                    pairs = CHUNKS[c] // 2
                    with act.Fori(0, pairs - 1) as i:
                        for b in range(2):
                            up_post(c, b, i, b, SLOT)
                    for b in range(2):
                        up_post(c, b, None, 2 * (pairs - 1) + b, CHUNKS[c] * P)
                    with act.Fori(0, 3) as i:
                        for b in range(2):
                            if c:
                                square(KT + b, i)
                            split_hi(DN_U[c] + b + 2, i, CHUNKS[c] * P)
                    for b in range(2):
                        if c:
                            square(KT + 6 + b)
                        else:
                            split_hi(DN_U[c] + 6 + b + 2)

            for j in range(2 * NT):
                act.wait_ge(yT_full, j + 1)
                A(xin[:, j // 2, (j % 2) * 512:(j % 2) * 512 + 512], ps[:, j % 8, :], ACT.Copy).then_inc(yT_read, 1)

        @block.vector
        def _(dve):
            V = nc.vector

            def mod_post(l, h):
                dve.wait_ge(modT_full, h + 1 if l is None else MOD_LAYER_G * l + (MOD_PRE_G + h + 1))
                if l is not None:
                    apart(dve)
                vec = h // 2 if l is None else (h // 2 + 2) % NMOD
                c0 = vec * KT + 4 * (h % 2)
                if l is None:
                    bias = vecs[:, 0, V_BMOD + c0:V_BMOD + c0 + 4]
                elif h < 8:
                    bias = vl[:, V_BMOD + c0:V_BMOD + c0 + 4]
                else:
                    bias = vecs[:, :, :].rearrange("p l n -> p (l n)")[
                        :, ds(((DEPTH - 1) - l) * V_N + (V_BMOD + c0), 4)]
                V.tensor_tensor(modv[:, vec, 4 * (h % 2):4 * (h % 2) + 4, :],
                                ps[:, 7, 0:8].rearrange("p (t s) -> p t s", s=2),
                                bias.unsqueeze(2).broadcast_to([P, 4, 2]), ALU.add).then_inc(mod_ready, 1)

            V.memset(crow[:, :], 0.0)
            dve.drain()
            dve.sem_inc(const_ready, 1)
            V.memset(cT[:, :, :], 0.0)
            V.memset(vrow[:, :, :, :], 0.0)
            V.memset(ones[:, :], 1.0)
            V.memset(eps[:, :], EPS)
            dve.drain()
            dve.sem_inc(const_ready, 1)
            for b in range(2):
                dve.sem_inc(split_full[b], 1)
            dve.sem_inc(up_read, 2)
            dve.sem_inc(dn_read, 2)
            dve.sem_inc(x_ready, KT)
            for buf in (x, h_hi, h_lo):
                for a, e in ((0, 1), (C_SAMPLE - 1, C_SAMPLE), (T - 2, T)):
                    V.memset(buf[:, :, a:e] if buf is x else buf[:, :, a:e].bitcast(F32), 0.0)
            dve.wait_ge(setup_full, 1)
            dve.wait_ge(c_in, 48)
            V.tensor_reduce(sel[:, :], ident[:, :].rearrange("p (q m) -> p m q", m=QUAD)[:, 0:2, :], axis=AX.X,
                            op=ALU.add)
            V.tensor_copy(cT[:, :, 0:2].rearrange("p t s -> p s t"),
                          ps[:, 0, 0:2 * KT].rearrange("p (s t) -> p s t", s=2)).then_inc(setup_read, 1)
            dve.drain()
            dve.sem_inc(cT_ready, 1)
            for j in range(2):
                dve.wait_ge(xT_full, j + 1)
                V.tensor_copy(x[:, 4 * j:4 * j + 4, C_PROMPT:C_PROMPT + SEQ],
                              ps[:, j, :].rearrange("p (t n) -> p t n", n=P)).then_inc(xT_read, 1)
            for l in range(DEPTH):
                dve.wait_ge(setup_full, 2 + l)
                V.tensor_copy(vecs[:, l, :], ps[:, 2 + l, 0:V_N]).then_inc(setup_read, 1)
            dve.wait_ge(setup_full, 4)
            V.tensor_copy(lamb[:, :, :, :].rearrange("p a l n -> p (a l n)"), ps[:, 4, :]).then_inc(setup_read, 1)
            dve.wait_ge(setup_full, 5)
            V.tensor_copy(qkg[:, :, :, :].rearrange("p a l n -> p (a l n)"), ps[:, 5, 0:256]
                          ).then_inc(setup_read, 1)
            dve.drain()
            for l in range(DEPTH):
                V.tensor_scalar(vecs[:, l, V_SUB:V_SUB + 1], vecs[:, l, V_SUB:V_SUB + 1], 1.0 - LAM_INIT[l], None,
                                ALU.mult)
            lv = lamb[:, :, :, :].rearrange("p (a c) l n -> p a c (l n)", c=2)
            V.tensor_tensor(lamp[:, :, :, :].rearrange("p a l n -> p a (l n)"), lv[:, :, 0, :], lv[:, :, 1, :],
                            ALU.mult)
            dve.drain()
            V.tensor_reduce(lam_s[:, :], lamp[:, :, :, :].rearrange("p a l n -> p (a l) n"), axis=AX.X, op=ALU.add
                            ).then_inc(lam_ready, 1)
            dve.wait_ge(lam_exp, 1)
            V.tensor_tensor(neglam[:, :], lam_s[:, DEPTH:2 * DEPTH], lam_s[:, 0:DEPTH], ALU.subtract)
            dve.drain()
            for l in range(DEPTH):
                V.tensor_scalar(neglam[:, l:l + 1], neglam[:, l:l + 1], -LAM_INIT[l], None, ALU.add)
            mod_post(None, 0)
            V.memset(ssq[:, :], 0.0)

            def x_copies(ks):
                for k in ks:
                    dve.wait_ge(xT_full, k + 3)
                    V.tensor_copy(x[:, k, C_SAMPLE:C_SAMPLE + DEC], ps[:, (2 + k) % 5, :]).then_inc(xT_read, 1)

            def x_squares(ks):
                for k in ks:
                    dve.wait_ge(sq_ready, k + 1)
                    dve.drain()
                    V.tensor_tensor(ssq[:, :], ssq[:, :], sq[:, :], ALU.add).then_inc(
                        ssq_ready if k == KT - 1 else sq_added, 1)

            x_copies(range(0, 3))
            mod_post(None, 1)
            x_copies(range(3, 5))
            x_squares(range(0, 3))
            x_copies(range(5, KT))
            mod_post(None, 2)
            x_squares(range(3, KT))
            mod_post(None, 3)

            with dve.Fori(0, DEPTH) as l:
                def split_lo(n, i=None, size=SLOT):
                    b = n % 2
                    dve.wait_ge(hi_done[b], at(l * SPLIT_SLOT + (n // 2 + 1), i))
                    V.tensor_tensor(w_lo[:, b, 0:size], raw[:, b, 0:size], w_hi[:, b, 0:size].bitcast(F32),
                                    ALU.subtract).then_inc(split_full[b], 1)

                def gains(vec, gain_col):
                    V.scalar_tensor_tensor(out=gain[:, :, :], in0=modv[:, vec + 1, :, :], scalar=1.0,
                                           in1=vl[:, gain_col:gain_col + KT].unsqueeze(2).broadcast_to([P, KT, 2]),
                                           op0=ALU.add, op1=ALU.mult)

                def norm_part(vec, base, c0, n, slots, segs):
                    V.reciprocal(rb[:, c0:c0 + n], rb[:, c0:c0 + n])
                    dve.drain()
                    count = slots.shape[1]
                    for i in range(KT + LAG):
                        if i < KT:
                            if i >= count:
                                dve.drain()
                            for c, m, p0, s in segs:
                                ins = V.scalar_tensor_tensor(
                                    out=slots[:, i % count, p0:p0 + m], in0=x[:, i, c:c + m],
                                    scalar=gain[:, i, s:s + 1], in1=rb[:, c:c + m], op0=ALU.mult, op1=ALU.mult)
                            ins.then_inc(tmp_ready, 1)
                        if i >= LAG:
                            k = i - LAG
                            dve.wait_ge(hh_ready, NORMED * l + (base + k + 1))
                            for c, m, p0, s in segs:
                                ins = V.scalar_tensor_tensor(
                                    out=h_lo[:, k, c:c + m], in0=slots[:, k % count, p0:p0 + m],
                                    scalar=modv[:, vec, k, s:s + 1], in1=h_hi[:, k, c:c + m].bitcast(F32),
                                    op0=ALU.add, op1=ALU.subtract)
                            ins.then_inc(h_ready, 1)

                V.tensor_copy(vl[:, :], vecs[:, :, :].rearrange("p l n -> p (l n)")[:, ds(l * V_N, V_N)])
                V.tensor_copy(qkg_l[:, :, :], qkg[:, :, ds(l, 1), :].rearrange("p a l n -> p a (l n)"))
                V.tensor_copy(neglam_l[:, :], neglam[:, ds(l, 1)])
                dve.drain()
                gains(0, V_N1)
                split_lo(0)
                dve.wait_ge(rms_ready, 3 * l + 1)
                for t in range(NT):
                    norm_part(0, t * KT, TOK_TILES[t], P, tmp_t, [(TOK_TILES[t], P, 0, TILE_SEQ[t])])
                    if t == 0:
                        split_lo(1)
                mod_post(l, 0)
                for a in range(2):
                    g4 = qkg_l[:, a, :].unsqueeze(1).broadcast_to([P, 4, HD])
                    V.tensor_tensor(rope_q[:, a, 0, :, :], rope[:, 0, :, :], g4, ALU.mult)
                    for m in range(2):
                        def member(ap, m):
                            return ap.rearrange("p (a m n) -> p a m n", m=2, n=16)[:, :, m, :]
                        V.tensor_tensor(member(rope_q[:, a, 1, :, :].rearrange("p t n -> p (t n)"), m),
                                        member(rope[:, 1, :, :].rearrange("p t n -> p (t n)"), m),
                                        g4.rearrange("p t (a m n) -> p t a m n", m=2, n=16)[:, :, :, 1 - m, :],
                                        ALU.mult)

                def groups(ap):
                    return ap.rearrange("p (g n) -> p g n", n=HD)

                for p in range(3):
                    split_lo(2 * p + 2)
                    if p:
                        mod_post(l, 2 * p)
                    for t in range(NT if p < 2 else 0):
                        n = NT * p + t
                        if t == 3 + p:
                            mod_post(l, 2 * p + 1)
                        q = qraw[:, n % 2, :]
                        dve.wait_ge(qsq_ready, 2 * NT * l + (n + 1))
                        V.tensor_reduce(st8[:, n % 2, :], groups(sq[:, 0:D_ATTN]), axis=AX.X, op=ALU.add
                                        ).then_inc(qsum_ready, 1)
                        dve.wait_ge(qrms_ready, 2 * NT * l + (n + 1))
                        V.reciprocal(st8[:, n % 2, :], st8[:, n % 2, :])
                        dve.drain()
                        V.tensor_tensor(groups(q), groups(q),
                                        st8[:, n % 2, :].unsqueeze(2).broadcast_to([P, 8, HD]), ALU.mult)
                        dve.drain()
                        if t == 0:
                            V.tensor_tensor(groups(qn[:, 0, :]), groups(q),
                                            qkg_l[:, p, :].unsqueeze(1).broadcast_to([P, 8, HD]), ALU.mult
                                            ).then_inc(qk_ready, 1)
                            continue
                        V.tensor_tensor(groups(rt[:, 0, :]), groups(q),
                                        rope_q[:, p, 0, t - 1, :].unsqueeze(1).broadcast_to([P, 8, HD]), ALU.mult)
                        for m in range(2):
                            def member(ap, m):
                                return ap.rearrange("p (a m n) -> p a m n", m=2, n=16)[:, :, m, :]
                            sn = member(rope_q[:, p, 1, t - 1, :], m).unsqueeze(1).broadcast_to([P, 8, 2, 16])
                            V.tensor_tensor(member(rt[:, 1, :], m).rearrange("p (g a) n -> p g a n", a=2),
                                            member(q, 1 - m).rearrange("p (g a) n -> p g a n", a=2), sn, ALU.mult)
                        dve.drain()
                        V.tensor_tensor(qn[:, t, :], rt[:, 0, :], rt[:, 1, :], ALU.add).then_inc(qk_ready, 1)
                    split_lo(2 * p + 3)

                mod_post(l, 5)
                for i in range(HALVES):
                    unit, tile, h = i // 4, (i % 4) // 2, i % 2
                    pair, kind = divmod(unit, 3)
                    if 1 <= i < ROUNDS + 1:
                        r = (i - 1) % 2
                        w = P if (i - 1) % NT == 0 else N_KEY
                        dve.wait_ge(exp_done, ROUNDS * l + i)
                        V.reciprocal(rec[:, r, :], sums[:, r, :])
                        dve.drain()
                        V.tensor_tensor(rec[:, r, 1:2], rec[:, r, 1:2], neglam_l[:, :], ALU.mult)
                        V.tensor_scalar(probs[:, r, 0, 0:w], probs[:, r, 0, 0:w], rec[:, r, 0:1], None, ALU.mult)
                        dve.drain()
                        V.scalar_tensor_tensor(out=probs[:, r, 0, 0:w], in0=probs[:, r, 1, 0:w],
                                               scalar=rec[:, r, 1:2], in1=probs[:, r, 0, 0:w], op0=ALU.mult,
                                               op1=ALU.add).then_inc(a_ready, 1)
                    if i == ROUNDS + 2:
                        dve.wait_ge(orms_ready, l + 1)
                        V.reciprocal(ssq_o[:, :], ssq_o[:, :])
                        dve.drain()
                        V.tensor_tensor(o[:, :, :], o[:, :, :],
                                        ssq_o[:, :].unsqueeze(2).broadcast_to([P, ROUNDS, VD]),
                                        ALU.mult).then_inc(on_ready, 1)
                    if kind:
                        if i % 4 == 3:
                            dve.wait_ge(unit_done[unit % 2], done(l, C_U + unit))
                        else:
                            dve.wait_ge(conv_full, 18 * l + (3 * unit + i % 4 + 1))
                        cols = slice(h * HALF, (h + 1) * HALF)
                    z = cgb[:, tile, :]
                    if kind == 1:
                        dve.wait_ge(cg_read, 8 * l + (4 * pair + i % 4 + 1))
                        V.tensor_tensor(z[:, cols], ps[:, h, 0:HALF], z[:, cols], ALU.mult).then_inc(xb_read, 1)
                        if h:
                            def cw(j):
                                w = V_CONV + 4 * j + 2 * pair + tile
                                return vl[:, w:w + 1]
                            dve.drain()
                            V.tensor_scalar(tap[:, tile, :], z, cw(1), None, ALU.mult)
                            for j, off in ((0, 0), (2, 2)):
                                dve.drain()
                                V.scalar_tensor_tensor(out=tap[:, tile, 1:T - 1], in0=z[:, off:off + T - 2],
                                                       scalar=cw(j), in1=tap[:, tile, 1:T - 1], op0=ALU.mult,
                                                       op1=ALU.add)
                            dve.drain()
                    elif kind == 2:
                        k = 2 * pair + tile
                        V.tensor_tensor(y[:, k, cols], ps[:, h, 0:HALF], tap[:, tile, cols], ALU.mult
                                        ).then_inc(xb_read, 1)
                        if h:
                            dve.drain()
                            if k == 0:
                                V.tensor_tensor(ssq[:, :], y[:, k, :], y[:, k, :], ALU.mult)
                            else:
                                V.tensor_tensor(sq[:, :], y[:, k, :], y[:, k, :], ALU.mult)
                                dve.drain()
                                ins = V.tensor_tensor(ssq[:, :], ssq[:, :], sq[:, :], ALU.add)
                                if k == 3:
                                    ins.then_inc(ssq_ready, 1)
                    if i < ROUNDS:
                        w = P if i % NT == 0 else N_KEY
                        dve.wait_ge(qk_full, ROUNDS * l + (i + 1))
                        V.reduce_max(mx[:, i % 2, :],
                                     scores[:, 0:2 * N_KEY].rearrange("p (s n) -> p s n", s=2)[:, :, 0:w], AX.X)
                        dve.drain()
                        V.tensor_scalar(nbias[:, i % 2, :], mx[:, i % 2, :], -SCALE, None, ALU.mult
                                        ).then_inc(max_ready, 1)
                    if i % 4 == 0 and unit:
                        split_lo(C_U + unit + 1)

                for t in range(NT):
                    c0 = TOK_TILES[t]
                    dve.wait_ge(oT_hi, NT * l + (t + 1))
                    V.scalar_tensor_tensor(out=h_lo[:, 0:4, c0:c0 + P],
                                           in0=ps[:, 2 + t, :].rearrange("p (s n) -> p s n", n=P),
                                           scalar=vl[:, V_SUB:V_SUB + 1],
                                           in1=h_hi[:, 0:4, c0:c0 + P].bitcast(F32),
                                           op0=ALU.mult, op1=ALU.subtract).then_inc(oT_read, 1)
                dve.wait_ge(rms_ready, 3 * l + 2)
                for h in range(2):
                    V.reciprocal(rb[:, h * HALF:(h + 1) * HALF], rb[:, h * HALF:(h + 1) * HALF])
                    dve.drain()
                    for a, e in (((0, 1), (C_SAMPLE - 1, C_SAMPLE)) if h == 0 else ((T - 2, T),)):
                        V.memset(rb[:, a:e], 0.0)
                    dve.drain()
                    for i in range(4 + LAG):
                        if i < 4:
                            V.scalar_tensor_tensor(out=tmp_h[:, i, :], in0=y[:, i, h * HALF:(h + 1) * HALF],
                                                   scalar=vl[:, V_CNG + i:V_CNG + i + 1],
                                                   in1=rb[:, h * HALF:(h + 1) * HALF],
                                                   op0=ALU.mult, op1=ALU.mult).then_inc(tmp_ready, 1)
                        if i >= LAG:
                            k = i - LAG
                            dve.wait_ge(hh_ready, NORMED * l + (NORM1 + 4 * h + k + 1))
                            V.tensor_tensor(h_lo[:, 4 + k, h * HALF:(h + 1) * HALF], tmp_h[:, k, :],
                                            h_hi[:, 4 + k, h * HALF:(h + 1) * HALF].bitcast(F32), ALU.subtract
                                            ).then_inc(mix_ready, 1)
                split_lo(C_U + 7)

                def add_to_x(bank, vec, k, i, signal):
                    for c0, n, h, p0, s in PIECES:
                        g0 = (vec * KT + k) * 2 + s
                        gate = mf[:, g0:g0 + 1] if i is None else mf[:, ds(i * 4 + g0, 1)]
                        a = k * T + c0
                        xs = xf[:, a:a + n] if i is None else xf[:, ds(i * (2 * T) + a, n)]
                        ins = V.scalar_tensor_tensor(out=xs, in0=ps[:, bank + h, p0:p0 + n], scalar=gate, in1=xs,
                                                     op0=ALU.mult, op1=ALU.add)
                    ins.then_inc(signal, 1)

                def add_square(k, i, last):
                    dve.wait_ge(sq_ready, at(16 * l + (KT + k + 1), i, 2))
                    ins = V.tensor_tensor(ssq[:, :], ssq[:, :], sq[:, :], ALU.add)
                    if last:
                        ins.then_inc(ssq_ready, 1)
                    else:
                        dve.drain()

                V.memset(ssq[:, :], 0.0)
                for k in range(KT):
                    n = O_U + k // 2
                    if k % 2 == 0 and k:
                        mod_post(l, 5 + k // 2)
                    if k % 2:
                        dve.wait_ge(unit_done[n % 2], done(l, n))
                    else:
                        dve.wait_ge(out_full, 4 * l + (k // 2 + 1))
                    add_to_x(2 * (k % 2), 2, k, None, x_ready)
                    add_square(k, None, k == KT - 1)
                    if k % 2:
                        split_lo(n + 2)
                mod_post(l, 9)
                gains(3, V_N2)
                dve.wait_ge(rms_ready, 3 * l + 3)
                for h in range(2):
                    norm_part(3, NORM1 + MIXN + KT * h, h * HALF, HALF, tmp_h,
                              [(c0, n, p0, s) for c0, n, hf, p0, s in PIECES if hf == h])
                mod_post(l, 10)
                mod_post(l, 11)

                def up_post(c, b, i, j, nxt_size):
                    n, gate = UP_U[c] + j, CH0[c] + j
                    dve.wait_ge(up_read, at(22 * l + (gate + 3), i, 2))
                    for tap_i, off in ((0, 0), (2, 2)):
                        for s in range(2):
                            w = V_FFN + tap_i * V_FT + s * (V_FT // 2) + gate
                            ins = V.scalar_tensor_tensor(
                                out=cen[:, s, 1:T - 1], in0=ub[:, s, off:off + T - 2],
                                scalar=vl[:, w:w + 1] if i is None else vl[:, ds(i * 2 + w, 1)],
                                in1=cen[:, s, 1:T - 1], op0=ALU.mult, op1=ALU.add)
                        if tap_i == 0:
                            dve.drain()
                    ins.then_inc(taps_ready, 1)
                    split_lo(n + 2, i, nxt_size)
                    dve.wait_ge(silu_ready, at(22 * l + (gate + 1), i, 2))
                    V.tensor_tensor(gt[:, :], cen[:, 0, :], cen[:, 1, :], ALU.mult).then_inc(gm_ready, 1)
                    dve.wait_ge(gh_ready, at(22 * l + (gate + 1), i, 2))
                    dst, hi = ((g_lo[:, j * T:(j + 1) * T], g_hi[:, j * T:(j + 1) * T]) if i is None else
                               (g_lo[:, ds(i * (2 * T) + j * T, T)], g_hi[:, ds(i * (2 * T) + j * T, T)]))
                    V.tensor_tensor(dst, gt[:, :], hi.bitcast(F32), ALU.subtract).then_inc(g_ready, 1)

                for c in range(2):
                    pairs = CHUNKS[c] // 2
                    with dve.Fori(0, pairs - 1) as i:
                        for b in range(2):
                            up_post(c, b, i, b, SLOT)
                    for b in range(2):
                        up_post(c, b, None, 2 * (pairs - 1) + b, CHUNKS[c] * P)
                    if c:
                        V.memset(ssq[:, :], 0.0)
                        dve.drain()

                    def down_post(b, i, j):
                        dve.wait_ge(unit_done[b], at(done(l, DN_U[c] + j), i))
                        add_to_x(2 * b, 5, j, i, x_ready if c else dn_read)
                        if c:
                            add_square(KT + j, i, j == KT - 1)

                    with dve.Fori(0, 3) as i:
                        for b in range(2):
                            down_post(b, i, b)
                            split_lo(DN_U[c] + b + 2, i, CHUNKS[c] * P)
                    for b in range(2):
                        down_post(b, None, 6 + b)
                        if not c:
                            split_lo(DN_U[c] + 6 + b + 2)


def _tables():
    half = HD // 2
    nf = HD // 4
    inv = (10000.0 ** (-np.arange(nf, dtype=np.float32) / nf)).astype(np.float32)
    tok = np.arange(DEC)
    ang = np.concatenate([np.tile(pos.astype(np.float32)[:, None] * inv[None], (1, 2))
                          for pos in (tok // GRID_W, tok % GRID_W)], axis=1)
    sign = np.tile(np.repeat(np.float32([-1, 1]), nf), 2)
    both = np.stack([np.cos(ang), np.sin(ang) * sign]).astype(np.float32)
    assert both.shape == (2, DEC, 2 * half)
    return {"ident": np.eye(P, dtype=np.float32),
            "rope": np.ascontiguousarray(both.reshape(2, DEC // P, P, HD).transpose(2, 0, 1, 3))}


_INS = ['x_prompt', 'x_sample', 'cache_k', 'cache_v', 'c', 'c_ctx', 'w_mod', 'b_mod', 'norm1_g', 'w_in', 'q_norm_g',
        'k_norm_g', 'lambda_q1', 'lambda_k1', 'lambda_q2', 'lambda_k2', 'subln_g', 'conv_w', 'conv_norm_g', 'w_out',
        'norm2_g', 'w_up', 'ffn_conv_w', 'w_down']
_OUTS = [(1, SEQ, D), (1, DEC, D), (1, DEPTH, SEQ, NH, 2, HD), (1, DEPTH, SEQ, NH, VD)]


def kernel(**inputs):
    import concourse.bacc as _bacc
    from concourse.bass_utils import run_bass_kernel_spmd as _run

    nc = _bacc.Bacc("TRN2", target_bir_lowering=False, num_devices=1)
    tables = _tables()
    arrays, args = {}, []
    for name in _INS + ["ident", "rope"]:
        a = np.ascontiguousarray(inputs[name] if name in inputs else tables[name])
        arrays[f"in_{name}_dram"] = a
        args.append(nc.dram_tensor(f"in_{name}_dram", a.shape, mybir.dt.from_np(a.dtype), kind="ExternalInput").ap())
    for i, shape in enumerate(_OUTS):
        args.append(nc.dram_tensor(f"out_{i}_dram", shape, F32, kind="ExternalOutput").ap())
    hybrid_step(nc, *args)
    r = _run(nc, [arrays], core_ids=[0])
    return tuple(r.results[0][f"out_{i}_dram"] for i in range(len(_OUTS)))
```

```python
import math
from contextlib import ExitStack

import concourse.bass as bass
import numpy as np
from concourse import mybir

F32 = mybir.dt.float32
F32R = mybir.dt.float32r
ALU = mybir.AluOpType
ACT = mybir.ActivationFunctionType
AX = mybir.AxisListType
ds = bass.ds

P = 128
D = 1024
KT = D // P
DEPTH = 2
SEQ, DEC, PAST = 128, 512, 128
NH, HD, VD = 4, 64, 128
D_ATTN = D_CONV = 512
FF = 2816
NMOD = 6
GRID_W = 64
EPS = 1e-6
SCALE = HD ** -0.5

T = 644
HALF = T // 2
C_PROMPT, C_SAMPLE = 1, 130
TOK_TILES = [C_PROMPT] + [C_SAMPLE + P * i for i in range(DEC // P)]
NT = len(TOK_TILES)
PIECES = [(C_PROMPT, SEQ, 0, C_PROMPT, 0), (C_SAMPLE, HALF - C_SAMPLE, 0, C_SAMPLE, 1),
          (HALF, C_SAMPLE + DEC - HALF, 1, 0, 1)]
TILE_CUTS = [(t, max(c0, h * HALF) - c0, min(c0 + P, (h + 1) * HALF) - max(c0, h * HALF), h, max(c0 - h * HALF, 0))
             for t, c0 in enumerate(TOK_TILES) for h in range(2) if max(c0, h * HALF) < min(c0 + P, (h + 1) * HALF)]
B_RMS = [(5, 6), (5, 6), (3, 5)]
B_SUM, C_SUM = 6, 400
N_KEY = PAST + DEC
TILE_SEQ = [0] + [1] * (DEC // P)
K_PROMPT, K_PAST, K_SAMPLE = 0, SEQ, SEQ + PAST

UC = 256
SLOT = KT * UC
CHUNKS = [12, 10]
CH0 = [0, 12]
C_U, O_U = 6, 12
UP_U = [16, 36]
DN_U = [28, 46]
N_SPLIT = 54
SPLIT_SLOT = N_SPLIT // 2
MOD_PRE = 8
MOD_LAYER = 24
RAW_SLOT = (N_SPLIT + MOD_LAYER) // 2
RAW_PRE = MOD_PRE // 2
MOD_PRE_G, MOD_LAYER_G = MOD_PRE // 2, MOD_LAYER // 2
NORM1, MIXN, NORM2 = NT * KT, 2 * 4, 2 * KT
NORMED = NORM1 + MIXN + NORM2
LAG = 3
QUAD = 32


def load_order():
    mod = [("mod", j) for j in range(MOD_LAYER)]
    split = [("split", n) for n in range(UP_U[0] + 2)]
    order = split[0:2] + mod[0:4] + split[2:4]
    for h in range(2, 6):
        order += mod[2 * h:2 * h + 2] + split[h + 2:h + 3]
    order += split[8:14]
    for h in range(6, 9):
        order += mod[2 * h:2 * h + 2] + split[h + 8:h + 9]
    return order + mod[18:22] + split[17:18]


ORDER = load_order()


def raw_of(n):
    return ORDER.index(("split", n)) if n < UP_U[0] + 2 else n + MOD_LAYER - (2 if n < DN_U[0] + 2 else 0)


def mod_raw(j):
    return ORDER.index(("mod", j)) if j < MOD_LAYER - 2 else raw_of(DN_U[0] + 1) + 1 + j - (MOD_LAYER - 2)


V_BMOD, V_N1, V_N2, V_CONV, V_CNG, V_SUB, V_FFN = 0, 48, 56, 64, 76, 80, 128
V_FT = 2 * FF // P
V_N = V_FFN + 3 * V_FT
ROUNDS = NH * NT
HALVES = 24
N_SMALL = 15
YT_BANKS = [2, 3, 6, 7, 0, 1, 4, 5, 2, 3]
YT_WAITS = {0: 4, 4: 7, NT: KT}
OT_BANKS = [2, 3, 4, 0, 1]
MOD_BANK = 7


def mod_bank(l, h):
    return MOD_BANK - (h % 2) if l is None else MOD_BANK


LAM_INIT = [0.8 - 0.6 * math.exp(-0.3 * i) for i in range(DEPTH)]


def hybrid_step(nc, x_prompt, x_sample, cache_k, cache_v, c_sample, c_ctx, w_mod, b_mod, norm1_g, w_in, q_norm_g,
                k_norm_g, lambda_q1, lambda_k1, lambda_q2, lambda_k2, subln_g, conv_w, conv_norm_g, w_out,
                norm2_g, w_up, ffn_conv_w, w_down, ident_in, rope_in, y_prompt, y_sample, new_k, new_v):
    ctx = ExitStack()
    with ctx:
        def sb(name, shape, dt=F32, scope=None):
            return (scope or ctx).enter_context(nc.sbuf_tensor(name, shape, dt))

        def sem(name):
            return ctx.enter_context(nc.semaphore(name))

        x = sb("x", [P, KT, T])
        h_hi = sb("h_hi", [P, KT, T], F32R)
        h_lo = sb("h_lo", [P, KT, T], F32R)
        raw = sb("raw", [P, 2, SLOT])
        w_hi = sb("w_hi", [P, 2, SLOT], F32R)
        w_lo = sb("w_lo", [P, 2, SLOT], F32R)
        aT = sb("aT", [P, N_KEY])
        rms5 = sb("rms5", [P, NT])
        ssq = sb("ssq", [P, T])
        sq = sb("sq", [P, T])
        diag = sq
        tmp = sb("tmp", [P, 2, T])
        ident = sb("ident", [P, P])
        ones = sb("ones", [P, P])
        junk = sb("junk", [P, VD])
        rope = sb("rope", [P, 2, 4, HD])
        rope_q = sb("rope_q", [P, 2, 2, 4, HD])
        vecs = sb("vecs", [P, DEPTH, V_N])
        vl = sb("vl", [P, V_N])
        modv = sb("modv", [P, NMOD, KT, 2])
        gain = sb("gain", [P, KT, 2])
        cT = sb("cT", [P, KT, QUAD])
        mod_row = sb("mod_row", [P, 2 * UC])
        qkg = sb("qkg", [P, 2, DEPTH, HD])
        qkg_l = sb("qkg_l", [P, 2, HD])
        neglam = sb("neglam", [P, DEPTH])
        neglam_l = sb("neglam_l", [P, 1])
        lam_s = sb("lam_s", [P, 4])
        eps = sb("eps", [P, 1])
        st8 = sb("st8", [P, 2, 8])
        mx = sb("mx", [P, 2, 2])
        nbias = sb("nbias", [P, 2, 2])
        sums = sb("sums", [P, 2, 2])
        rec = sb("rec", [P, 2, 2])
        ssq_o = sb("ssq_o", [P, ROUNDS])

        mix = ExitStack()
        qT = sb("qT", [P, NH, NT * P], scope=mix)
        kT = sb("kT", [P, NH, K_SAMPLE + DEC], scope=mix)
        v = sb("v", [P, 6, D_ATTN], scope=mix)
        cgb = sb("cgb", [P, 2, T], scope=mix)
        tap = tmp
        y = sb("y", [P, 4, T], scope=mix)
        prep = ExitStack()
        qraw = sb("qraw", [P, 2, D_ATTN], scope=prep)
        qn = sb("qn", [P, NT, D_ATTN], scope=prep)
        rt = sb("rt", [P, 2, D_ATTN], scope=prep)
        kc = sb("kc", [P, D_ATTN], scope=prep)
        prep.close()
        stage = ExitStack()
        xin = sb("xin", [P, NT, D], scope=stage)
        stage.close()
        setup = ExitStack()
        att = ExitStack()
        probs = sb("probs", [P, 2, 2, N_KEY], scope=att)
        o = sb("o", [P, ROUNDS, VD], scope=att)
        att.close()
        mix.close()
        mlp = ExitStack()
        g_hi = sb("g_hi", [P, CHUNKS[0] * T], F32R, scope=mlp)
        g_lo = sb("g_lo", [P, CHUNKS[0] * T], F32R, scope=mlp)
        ub = sb("ub", [P, 2, T], scope=mlp)
        cen = tmp
        gt = sb("gt", [P, T], scope=mlp)
        mlp.close()
        vrow = sb("vrow", [P, DEPTH, 3, P], scope=setup)
        crow = sb("crow", [P, P], scope=setup)
        brow = sb("brow", [1, 768], scope=setup)
        lamb = sb("lamb", [P, 4, DEPTH, HD], scope=setup)
        lamp = sb("lamp", [P, 2, DEPTH, HD], scope=setup)
        setup.close()

        ps = ctx.enter_context(nc.psum_tensor("ps", [P, 8, 512], F32))
        scores = ps[:, 2:5, :].rearrange("p b n -> p (b n)")
        probsT = ps[:, 5:7, :].rearrange("p b n -> p (b n)")

        tmp_t = tmp[:, :, :].rearrange("p a n -> p (a n)")[:, 0:KT * P].rearrange("p (k n) -> p k n", n=P)
        tmp_h = tmp[:, :, :].rearrange("p a (b n) -> p (a b) n", n=HALF)
        xf = x[:, :, :].rearrange("p t n -> p (t n)")
        mf = modv[:, :, :, :].rearrange("p v t s -> p (v t s)")

        raw_full = [sem("raw_full0"), sem("raw_full1")]
        hi_done = [sem("hi_done0"), sem("hi_done1")]
        split_full = [sem("split_full0"), sem("split_full1")]
        unit_done = [sem("unit_done0"), sem("unit_done1")]
        mod_used = sem("mod_used")
        row_read, modT_full, mod_ready = sem("row_read"), sem("modT_full"), sem("mod_ready")
        c_in, small_in, ffn_in, x_in, kv_in, out_done = (
            sem(s) for s in ("c_in", "small_in", "ffn_in", "x_in", "kv_in", "out_done"))
        bank3_first = sem("bank3_first")
        spacer = sem("spacer")
        sq_added, y_out = sem("sq_added"), sem("y_out")
        const_ready, silu_c, setup_full, setup_read = (sem("const_ready"), sem("silu_c"), sem("setup_full"),
                                                       sem("setup_read"))
        lam_ready, lam_exp, cT_ready = sem("lam_ready"), sem("lam_exp"), sem("cT_ready")
        xT_full, xT_read = sem("xT_full"), sem("xT_read")
        x_ready, sq_ready, ssq_ready = sem("x_ready"), sem("sq_ready"), sem("ssq_ready")
        stat_full, rms_ready = sem("stat_full"), sem("rms_ready")
        sum_ready = sem("sum_ready")
        diag_ready, rb_full = sem("diag_ready"), sem("rb_full")
        tmp_ready, hh_ready, h_ready = sem("tmp_ready"), sem("hh_ready"), sem("h_ready")
        qkv_full, qkv_read, qsq_ready, qsum_ready, qrms_ready, qk_ready, qkT_full, qkT_read, v_ready = (
            sem(s) for s in ("qkv_full", "qkv_read", "qsq_ready", "qsum_ready", "qrms_ready", "qk_ready",
                             "qkT_full", "qkT_read", "v_ready"))
        nk_out = sem("nk_out")
        conv_full, cg_read, xb_read = sem("conv_full"), sem("cg_read"), sem("xb_read")
        qk_full, max_ready, exp_done, a_ready, aT_full, aT_ready, pv_full, o_read = (
            sem(s) for s in ("qk_full", "max_ready", "exp_done", "a_ready", "aT_full", "aT_ready", "pv_full",
                             "o_read"))
        orms_ready, on_ready, oT_full, oT_hi, oT_read, mix_ready = (
            sem(s) for s in ("orms_ready", "on_ready", "oT_full", "oT_hi", "oT_read", "mix_ready"))
        out_full = sem("out_full")
        up_read, taps_ready, silu_ready, gm_ready, gh_ready, g_ready = (
            sem(s) for s in ("up_read", "taps_ready", "silu_ready", "gm_ready", "gh_ready", "g_ready"))
        dn_read = sem("dn_read")
        yT_full, yT_read = sem("yT_full"), sem("yT_read")

        block = ctx.enter_context(nc.Block())

        def done(l, n):
            return 1 + l * SPLIT_SLOT + n // 2 + 1

        def usable(l, n):
            return l * SPLIT_SLOT + n // 2 + 2

        def landed(l, r):
            return 32 * (RAW_PRE + 1) + l * (32 * RAW_SLOT) + 32 * (r // 2)

        def apart(eng):
            eng.sem_inc(spacer, 1)

        w_in_v = w_in.rearrange("l (t p) n -> p (l t) n", p=P)
        w_out_v = w_out.rearrange("l (t p) n -> p (l t) n", p=P)
        w_up_v = w_up.rearrange("l (t p) n -> p (l t) n", p=P)
        w_down_v = w_down.rearrange("l (t p) n -> p (l t) n", p=P)
        w_mod_v = w_mod.rearrange("l (t p) n -> p (l t) n", p=P)

        @block.sync
        def _(sp):
            def load(b, src, t0, tiles, cols, width):
                hf = tiles // 2
                dst = raw[:, b, 0:tiles * width].rearrange("p (t n) -> p t n", n=width)
                for s in range(2):
                    sp.dma_start(dst[:, s * hf:(s + 1) * hf, :],
                                 src[:, ds(t0 + s * hf, hf), ds(cols, width)]).then_inc(raw_full[b], 16)

            for u in range(MOD_PRE):
                if u >= 2:
                    sp.wait_ge(mod_used, u - 1)
                load(u % 2, w_mod_v, 0, KT, u * UC, UC)

            sp.wait_ge(mod_used, MOD_PRE - 1)
            load(0, w_in_v, 0, KT, 0, UC)

            with sp.Fori(0, DEPTH) as l:
                def free_of_split(n):
                    sp.wait_ge(split_full[n % 2], usable(l, n))

                def free_of_mod(k):
                    sp.wait_ge(mod_used, l * MOD_LAYER + (MOD_PRE + k))

                def split_unit(n):
                    if n < C_U + 6:
                        if n < C_U:
                            col = n * UC
                        else:
                            pair, kind = divmod(n - C_U, 3)
                            col = 3 * D_ATTN + D_CONV * (1, 2, 0)[kind] + pair * UC
                        load(n % 2, w_in_v, l * KT, KT, col, UC)
                    else:
                        load(n % 2, w_out_v, l * KT, KT, (n - O_U) * UC, UC)

                def up_unit(b, j):
                    dst = raw[:, b, :].rearrange("p (s t n) -> p s t n", s=2, n=P)
                    for s in range(2):
                        sp.dma_start(dst[:, s, :, :], w_up_v[:, ds(l * KT, KT), ds(s * FF + j * P, P)]
                                     ).then_inc(raw_full[b], 16)

                def mod_unit(j, slot):
                    layer, unit = (l, j + 8) if j < 16 else ((DEPTH - 1) - l, j - 16)
                    load(slot, w_mod_v, layer * KT, KT, unit * UC, UC)

                sp.wait_ge(mod_used, l * MOD_LAYER + MOD_PRE)
                sp.wait_ge(split_full[1], l * SPLIT_SLOT + 1)
                split_unit(1)
                for r in range(2, len(ORDER)):
                    before, j = ORDER[r - 2]
                    free_of_split(j) if before == "split" else free_of_mod(j + 1)
                    kind, n = ORDER[r]
                    if kind == "mod":
                        apart(sp)
                        mod_unit(n, r % 2)
                    elif n < UP_U[0]:
                        split_unit(n)
                    else:
                        up_unit(n % 2, n - UP_U[0])
                free_of_mod(MOD_LAYER - 2)
                apart(sp)
                up_unit(0, 2)
                free_of_split(UP_U[0] + 1)
                up_unit(1, 3)
                with sp.Fori(0, CHUNKS[0] // 2 - 2) as i:
                    for b in range(2):
                        sp.wait_ge(split_full[b], l * SPLIT_SLOT + ((UP_U[0] + 2) // 2 + 2) + i)
                        up_unit(b, 2 * i + (4 + b))
                for c in range(2):
                    if c == 1:
                        with sp.Fori(0, CHUNKS[1] // 2) as i:
                            for b in range(2):
                                sp.wait_ge(split_full[b], l * SPLIT_SLOT + (UP_U[1] // 2 + 1) + i)
                                up_unit(b, 2 * i + (CH0[1] + b))
                    if c == 0:
                        for i in range(2):
                            for b in range(2):
                                free_of_mod(MOD_LAYER - 1 + b) if i else free_of_split(DN_U[0] - 2 + b)
                                apart(sp)
                                load(b, w_down_v, l * (FF // P), CHUNKS[0], (2 * i + b) * P, P)
                            if i == 0:
                                for b in range(2):
                                    free_of_split(DN_U[0] + b)
                                    mod_unit(MOD_LAYER - 2 + b, b)
                    with sp.Fori(0 if c else 2, 4) as i:
                        for b in range(2):
                            sp.wait_ge(split_full[b], l * SPLIT_SLOT + (DN_U[c] // 2 + 1) + i)
                            load(b, w_down_v, l * (FF // P) + CH0[c], CHUNKS[c], (2 * i + b) * P, P)

                free_of_split(N_SPLIT - 2)
                load(0, w_in_v, ((DEPTH - 1) - l) * KT, KT, 0, UC)

            for j in range(2 * NT):
                kh, t = divmod(j, NT)
                sp.wait_ge(yT_read, j + 1)
                dst = y_prompt[0] if t == 0 else y_sample[0, (t - 1) * P:t * P, :]
                sp.dma_start(dst[:, kh * 512:(kh + 1) * 512], xin[:, t, kh * 512:(kh + 1) * 512]).then_inc(y_out, 16)
            sp.wait_ge(y_out, 16 * 2 * NT)

        @block.gpsimd
        def _(pool):
            ck = cache_k.rearrange("b l p h s d -> p (b l) (h s d)")
            cv = cache_v.rearrange("b l p h e -> p (b l) (h e)")
            nk = new_k.rearrange("b l p h s d -> p (b l) (h s d)")
            nv = new_v.rearrange("b l p h e -> p (b l) (h e)")
            with pool.Fori(0, DEPTH) as l:
                pool.wait_ge(stat_full, 3 * l + 1)
                pool.dma_start(kc[:, :], ck[:, ds(l, 1), :].rearrange("p a n -> p (a n)")).then_inc(kv_in, 16)
                pool.dma_start(v[:, 1, :], cv[:, ds(l, 1), :].rearrange("p a n -> p (a n)")).then_inc(kv_in, 16)
                pool.wait_ge(qk_ready, 2 * NT * l + NT + 1)
                apart(pool)
                pool.dma_start(nk[:, ds(l, 1), :].rearrange("p a n -> p (a n)"), qn[:, 0, :]).then_inc(nk_out, 16)
                pool.wait_ge(v_ready, NT * l + 1)
                apart(pool)
                pool.dma_start(nv[:, ds(l, 1), :].rearrange("p a n -> p (a n)"), v[:, 0, :]).then_inc(out_done, 16)
            pool.wait_ge(out_done, 16 * DEPTH)
            pool.wait_ge(nk_out, 16 * DEPTH)

        def at(expr, i, by=1):
            return expr if i is None else expr + i * by

        @block.tensor
        def _(pe):
            mm = nc.tensor.matmul

            def gemm(out, b, kt, width, col, mov_hi, mov_lo):
                wh = w_hi[:, b, 0:kt * width].rearrange("p (t n) -> p t n", n=width)
                wl = w_lo[:, b, 0:kt * width].rearrange("p (t n) -> p t n", n=width)
                for k in range(kt):
                    mm(out, wh[:, k, col:col + P], mov_hi(k), start=k == 0, stop=False)
                    mm(out, wh[:, k, col:col + P], mov_lo(k), start=False, stop=False)
                    ins = mm(out, wl[:, k, col:col + P], mov_hi(k), start=False, stop=k == kt - 1)
                return ins

            def mod_sum(l, h, u, b, landed_at):
                pe.wait_ge(raw_full[b], landed_at)
                if u == 0:
                    if l is not None:
                        pe.wait_ge(mod_ready, MOD_LAYER_G * l + h + MOD_PRE_G)
                    elif h > 1:
                        pe.wait_ge(mod_ready, h - 1)
                wu = raw[:, b, :].rearrange("p (t n) -> p t n", n=UC)
                for part in range(2):
                    for q in range(4):
                        k = 4 * part + q
                        ins = mm(ps[QUAD * q:QUAD * (q + 1), mod_bank(l, h), u * UC:(u + 1) * UC], cT[:, k, :],
                                 wu[:, k, :], start=part == 0, stop=part == 1)
                ins.then_inc(mod_used, 1)

            def mod_turn(l, h):
                if l is None:
                    pe.wait_ge(row_read, h + 1)
                else:
                    pe.wait_ge(row_read, MOD_LAYER_G * l + h + (MOD_PRE_G + 1))
                    apart(pe)
                for t in range(4):
                    ins = nc.tensor.transpose(ps[:, mod_bank(l, h), t * P:(t + 1) * P],
                                              mod_row[:, t * P:(t + 1) * P], ident[:, :])
                ins.then_inc(modT_full, 1)

            def stat(l, which):
                pe.wait_ge(ssq_ready, 3 * l + (1 + which))
                for last, part in enumerate((ssq, sq)):
                    if last and which != 1:
                        pe.wait_ge(sq_ready, 16 * l + KT * (1 + which // 2))
                    for t in range(NT):
                        c0 = C_SUM + NT * last + t
                        ins = mm(ps[:, B_SUM, c0:c0 + 1], part[:, TOK_TILES[t]:TOK_TILES[t] + P], ones[:, 0:1],
                                 start=True, stop=True)
                ins.then_inc(stat_full, 1)

            def spread(l, which):
                for t, off, n, h, p0 in TILE_CUTS:
                    if off == 0:
                        pe.wait_ge(diag_ready, 3 * NT * l + (NT * which + t + 1))
                    ins = mm(ps[:, B_RMS[which][h], p0:p0 + n], ones[:, :], diag[:, t * P + off:t * P + off + n],
                             start=True, stop=True)
                    if off + n == P:
                        ins.then_inc(rb_full, 1)

            pe.sem_inc(unit_done[0], 1)
            pe.sem_inc(unit_done[1], 1)
            def pre_sum(h):
                for u in range(2):
                    mod_sum(None, h, u, u, 32 * (h + 1))

            def x_sample(ks):
                for k in ks:
                    bank = (2 + k) % 5
                    if k >= 3:
                        pe.wait_ge(xT_read, k - 2)
                    for t in range(4):
                        ins = nc.tensor.transpose(ps[:, bank, t * P:(t + 1) * P], xin[:, 1 + t, k * P:(k + 1) * P],
                                                  ident[:, :])
                    ins.then_inc(xT_full, 1)

            pe.wait_ge(c_in, 48)
            pe.wait_ge(silu_c, 1)
            nc.tensor.transpose(ps[:, 0, 0:P], crow[:, :], ident[:, :]).then_inc(setup_full, 1)
            pe.wait_ge(cT_ready, 1)
            pre_sum(0)
            pe.wait_ge(x_in, 32)
            pe.wait_ge(setup_read, 1)
            for j in range(2):
                for t in range(4):
                    ins = nc.tensor.transpose(ps[:, j, t * P:(t + 1) * P],
                                              xin[:, 0, (4 * j + t) * P:(4 * j + t + 1) * P], ident[:, :])
                ins.then_inc(xT_full, 1)
            mod_turn(None, 0)
            pre_sum(1)
            pe.wait_ge(small_in, 16 * N_SMALL)
            pe.wait_ge(ffn_in, 64)
            for l in range(DEPTH):
                for r in range(3):
                    ins = nc.tensor.transpose(ps[:, 2 + l, r * P:(r + 1) * P], vrow[:, l, r, :], ident[:, :])
                ins.then_inc(setup_full, 1)
            mm(ps[:, 4, :], ones[0:1, :], brow[0:1, 0:512], start=True, stop=True).then_inc(setup_full, 1)
            mm(ps[:, 5, 0:256], ones[0:1, :], brow[0:1, 512:768], start=True, stop=True).then_inc(setup_full, 1)
            mod_turn(None, 1)
            pe.wait_ge(setup_read, 5)
            x_sample(range(0, 3))
            pre_sum(2)
            x_sample(range(3, 5))
            mod_turn(None, 2)
            x_sample(range(5, KT))
            pre_sum(3)
            mod_turn(None, 3)

            with pe.Fori(0, DEPTH) as l:
                stat(l, 0)
                spread(l, 0)

                def qkv_unit(b, t, c0, signal, follow=False):
                    col = TOK_TILES[t]
                    wh = w_hi[:, b, :].rearrange("p (t n) -> p t n", n=UC)
                    wl = w_lo[:, b, :].rearrange("p (t n) -> p t n", n=UC)
                    out = ps[:, t, c0:c0 + UC]
                    for k in range(KT):
                        if follow:
                            pe.wait_ge(h_ready, (NORM1 + NORM2) * l + (t * KT + k + 1))
                        mm(out, h_hi[:, k, col:col + P], wh[:, k, :], start=k == 0, stop=False)
                        mm(out, h_hi[:, k, col:col + P], wl[:, k, :], start=False, stop=False)
                        ins = mm(out, h_lo[:, k, col:col + P], wh[:, k, :], start=False, stop=k == KT - 1)
                    if t == NT - 1:
                        ins.then_inc(unit_done[b], 1)
                    elif signal:
                        ins.then_inc(qkv_full, 1)

                def pair_steps(h, b, t):
                    u = t // 2
                    if t == 0:
                        mod_turn(l, h - 1)
                    elif t % 2:
                        slot = b if u == 0 else 1 - b
                        r2 = mod_raw(4 + 2 * b + u) // 2
                        mod_sum(l, h, u, slot,
                                l * (32 * RAW_SLOT) + (h - b) * 48 + (32 * (RAW_PRE + 1 + r2) - 96))

                pe.wait_ge(split_full[0], usable(l, 0))
                for b, t in ((0, 0), (1, 0), (0, 1), (1, 1), (0, 2), (0, 3), (0, 4), (1, 2), (1, 3), (1, 4)):
                    if (b, t) == (1, 0):
                        pe.wait_ge(split_full[1], usable(l, 1))
                    qkv_unit(b, t, b * UC, b == 1, follow=b == 0)
                    if (b, t) == (1, 0):
                        mod_sum(l, 0, 0, 0, landed(l, mod_raw(0)))
                    elif (b, t) == (1, 1):
                        mod_sum(l, 0, 1, 1, landed(l, mod_raw(1)))
                    elif (b, t) == (0, 2):
                        mod_turn(l, 0)
                    elif (b, t) == (0, 3):
                        mod_sum(l, 1, 0, 0, landed(l, mod_raw(2)))
                    elif (b, t) == (0, 4):
                        mod_sum(l, 1, 1, 1, landed(l, mod_raw(3)))
                        pe.wait_ge(kv_in, 32 * l + 32)
                        for s in range(4):
                            ins = nc.tensor.transpose(ps[:, 5, s * P:(s + 1) * P], kc[:, s * P:(s + 1) * P],
                                                      ident[:, :])
                        ins.then_inc(qkT_full, 1)
                with pe.Fori(1, 3) as p:
                    pe.wait_ge(split_full[0], l * SPLIT_SLOT + 2 + p)
                    for t in range(NT):
                        pe.wait_ge(qkv_read, 2 * NT * l + NT * p + (t + 1 - NT))
                        qkv_unit(0, t, 0, False)
                        pair_steps(2 * p, 0, t)
                        pe.wait_ge(qk_ready, 2 * NT * l + NT * p + (t + 1 - NT))
                        if t != 1:
                            pe.wait_ge(qkT_read, 11 * l + NT * p + (t - NT + (t == 0)))
                        for s in range(4):
                            ins = nc.tensor.transpose(ps[:, 5 + t % 2, s * P:(s + 1) * P],
                                                      qn[:, t, s * P:(s + 1) * P], ident[:, :])
                        ins.then_inc(qkT_full, 1)
                    pe.wait_ge(split_full[1], l * SPLIT_SLOT + 2 + p)
                    for t in range(NT):
                        qkv_unit(1, t, UC, True)
                        pair_steps(2 * p + 1, 1, t)

                def conv_half(i):
                    n = C_U + i // 4
                    b, tile, h = n % 2, (i % 4) // 2, i % 2
                    if i % 4 == 0:
                        pe.wait_ge(split_full[b], usable(l, n))
                    if i >= 2:
                        j = i - 2
                        if (j // 4) % 3 == 0:
                            pe.wait_ge(cg_read, 8 * l + (4 * (j // 12) + j % 4 + 1))
                        else:
                            pe.wait_ge(xb_read, 16 * l + (8 * (j // 12) + (j % 12) - 4 + 1))
                    ins = gemm(ps[:, h, 0:HALF], b, KT, UC, tile * P,
                               lambda k: h_hi[:, k, h * HALF:(h + 1) * HALF],
                               lambda k: h_lo[:, k, h * HALF:(h + 1) * HALF])
                    ins.then_inc(unit_done[b] if i % 4 == 3 else conv_full, 1)

                def qk_scores(i):
                    hd, t = divmod(i, NT)
                    if i:
                        pe.wait_ge(exp_done, ROUNDS * l + i)
                    else:
                        pe.wait_ge(qkT_read, 11 * l + 11)
                    for s in range(2):
                        if t == 0:
                            parts, k0 = [(0, SEQ)], K_PROMPT
                        else:
                            parts, k0 = ([(512, N_KEY), (0, 512)], [(384, N_KEY), (0, 384)])[s], K_PAST
                        for j, (a, e) in enumerate(parts):
                            if s and j:
                                pe.wait_ge(bank3_first, (ROUNDS - NH) * l + (hd * (NT - 1) + t))
                            ins = mm(scores[:, s * N_KEY + a:s * N_KEY + e],
                                     qT[s * HD:(s + 1) * HD, hd, t * P:(t + 1) * P],
                                     kT[s * HD:(s + 1) * HD, hd, k0 + a:k0 + e], start=True, stop=True)
                            if s == 0 and j == 0 and t:
                                ins.then_inc(bank3_first, 1)
                    ins.then_inc(qk_full, 1)

                def key_tiles(i):
                    return [0] if i % NT == 0 else [1, 2, 3, 4, 5]

                def transposes(i):
                    pe.wait_ge(a_ready, ROUNDS * l + (i + 1))
                    if i:
                        pe.wait_ge(aT_ready, ROUNDS * l + i)
                    for j in range(len(key_tiles(i))):
                        ins = nc.tensor.transpose(probsT[:, j * P:(j + 1) * P], probs[:, i % 2, 0, j * P:(j + 1) * P],
                                                  ident[:, :])
                    ins.then_inc(aT_full, 1)

                def pv(i):
                    pe.wait_ge(aT_ready, ROUNDS * l + (i + 1))
                    if i:
                        pe.wait_ge(o_read, ROUNDS * l + i)
                    else:
                        pe.wait_ge(mod_ready, MOD_LAYER_G * l + (MOD_PRE_G + 6))
                    tiles, hd = key_tiles(i), i // NT
                    for j, kt in enumerate(tiles):
                        ins = mm(ps[:, 7, 0:VD], aT[:, j * P:(j + 1) * P], v[:, kt, hd * VD:(hd + 1) * VD],
                                 start=j == 0, stop=j == len(tiles) - 1)
                    ins.then_inc(pv_full, 1)

                pe.wait_ge(v_ready, NT * l + 2)
                for i in range(HALVES):
                    conv_half(i)
                    if i == 0:
                        mod_turn(l, 5)
                        pe.wait_ge(v_ready, NT * l + NT)
                        apart(pe)
                    if i < ROUNDS:
                        qk_scores(i)
                    if 2 <= i < ROUNDS + 2:
                        pv(i - 2)
                    if 1 <= i < ROUNDS + 1:
                        transposes(i - 1)

                pe.wait_ge(on_ready, l + 1)
                for t in range(NT):
                    if t == 3:
                        stat(l, 1)
                    for hd in range(NH):
                        ins = nc.tensor.transpose(ps[:, OT_BANKS[t], hd * P:(hd + 1) * P], o[:, hd * NT + t, :],
                                                  ident[:, :])
                    ins.then_inc(oT_full, 1)

                def out_unit(n, b):
                    def chain(j, h, k0=0, k1=KT):
                        wh, wl = (half[:, b, :].rearrange("p (t n) -> p t n", n=UC)[:, :, j * P:(j + 1) * P]
                                  for half in (w_hi, w_lo))
                        out = ps[:, 2 * j + h, 0:HALF]
                        for k in range(k0, k1):
                            if n == 0 and j == 0 and k >= 4:
                                pe.wait_ge(mix_ready, MIXN * l + (4 * h + k - 3))
                            hh, hl = (part[:, k, h * HALF:(h + 1) * HALF] for part in (h_hi, h_lo))
                            mm(out, wh[:, k, :], hh, start=k == 0, stop=False)
                            mm(out, wh[:, k, :], hl, start=False, stop=False)
                            ins = mm(out, wl[:, k, :], hh, start=False, stop=k == KT - 1)
                        if k1 == KT and h:
                            ins.then_inc(unit_done[b] if j else out_full, 1)

                    def pair_sum(u, h=n + 6):
                        r = mod_raw(2 * h + u)
                        mod_sum(l, h, u, r % 2, landed(l, r))

                    if n == 0:
                        pe.wait_ge(x_ready, 16 * l + 8)
                        pe.wait_ge(oT_read, NT * l + 3)
                        chain(1, 0, 0, 4)
                        spread(l, 1)
                        pe.wait_ge(oT_read, NT * l + NT)
                        chain(1, 1, 0, 4)
                        chain(0, 0, 0, 4)
                        chain(0, 1, 0, 4)
                        for h in range(2):
                            chain(0, h, 4)
                            chain(1, h, 4)
                        pair_sum(0)
                    else:
                        for j in range(2):
                            pe.wait_ge(x_ready, 16 * l + (2 * n + j + 7))
                            chain(j, 0)
                            if n == 1:
                                pair_sum(0) if j else pair_sum(1, 6)
                            elif j == 0:
                                mod_turn(l, n + 5)
                            else:
                                pair_sum(1)
                            chain(j, 1)
                            if n == 1:
                                pair_sum(1) if j else mod_turn(l, 6)
                            elif j == 0:
                                pair_sum(0)

                pe.wait_ge(o_read, ROUNDS * l + ROUNDS)
                for n in range(4):
                    pe.wait_ge(split_full[n % 2], usable(l, O_U + n))
                    out_unit(n, n % 2)
                mod_turn(l, 9)
                stat(l, 2)
                def up_half(b, h, follow=False):
                    w = [[half[:, b, s * KT * P:(s + 1) * KT * P].rearrange("p (t n) -> p t n", n=P)
                          for s in range(2)] for half in (w_hi, w_lo)]
                    for k in range(KT):
                        if follow:
                            pe.wait_ge(h_ready, (NORM1 + NORM2) * l + (NORM1 + KT * h + k + 1))
                        hh, hl = (part[:, k, h * HALF:(h + 1) * HALF] for part in (h_hi, h_lo))
                        for s in range(2):
                            out = ps[:, 4 * b + 2 * s + h, 0:HALF]
                            mm(out, w[0][s][:, k, :], hh, start=k == 0, stop=False)
                            mm(out, w[0][s][:, k, :], hl, start=False, stop=False)
                            ins = mm(out, w[1][s][:, k, :], hh, start=False, stop=k == KT - 1)
                    if h:
                        ins.then_inc(unit_done[b], 1)

                def up_pair_sum(h, u):
                    r = mod_raw(2 * h + u)
                    mod_sum(l, h, u, r % 2, landed(l, r))

                up_pair_sum(10, 0)
                up_pair_sum(10, 1)
                spread(l, 2)
                pe.wait_ge(split_full[0], usable(l, UP_U[0]))
                pe.wait_ge(up_read, 22 * l + 1)
                up_half(0, 0, follow=True)
                mod_turn(l, 10)
                pe.wait_ge(split_full[1], usable(l, UP_U[0] + 1))
                pe.wait_ge(up_read, 22 * l + 2)
                up_half(1, 0)
                up_half(0, 1, follow=True)
                pe.wait_ge(mod_ready, MOD_LAYER_G * l + (MOD_PRE_G + 11))
                apart(pe)
                up_half(1, 1)

                for c in range(2):
                    if c:
                        pe.wait_ge(mod_ready, MOD_LAYER_G * l + (MOD_PRE_G + MOD_LAYER_G))
                        pe.wait_ge(dn_read, 8 * l + (2 + 7))
                    apart(pe)
                    with pe.Fori(1 - c, CHUNKS[c] // 2) as i:
                        for b in range(2):
                            pe.wait_ge(split_full[b], l * SPLIT_SLOT + (UP_U[c] // 2 + 2) + i)
                            pe.wait_ge(up_read, 22 * l + 2 * i + (CH0[c] + b + 1))
                            if c and b:
                                pe.wait_ge(dn_read, 8 * l + (2 + 8))
                                apart(pe)
                            for h in range(2):
                                up_half(b, h)

                    def down(b, h, k0, k1):
                        kf = CHUNKS[c]
                        wh, wl = (half[:, b, 0:kf * P].rearrange("p (t n) -> p t n", n=P) for half in (w_hi, w_lo))
                        out = ps[:, 4 * b + h, 0:HALF]
                        for k in range(k0, k1):
                            gh, gl = (g[:, k * T + h * HALF:k * T + (h + 1) * HALF] for g in (g_hi, g_lo))
                            mm(out, wh[:, k, :], gh, start=k == 0, stop=False)
                            mm(out, wh[:, k, :], gl, start=False, stop=False)
                            ins = mm(out, wl[:, k, :], gh, start=False, stop=k == kf - 1)
                        if h and k1 == kf:
                            ins.then_inc(unit_done[b], 1)

                    def bank_read(b, i):
                        if c == 0:
                            pe.wait_ge(dn_read, at(8 * l + (b + 1), i, 2))
                        else:
                            pe.wait_ge(x_ready, at(16 * l + (b + 15), i, 2))

                    last = CHUNKS[c] - 2
                    pe.wait_ge(g_ready, 22 * l + (CH0[c] + last))
                    for b in range(2):
                        pe.wait_ge(split_full[b], usable(l, DN_U[c] + b))
                        bank_read(b, None)
                        down(b, 0, 0, last)
                        if b == 0:
                            down(b, 1, 0, last)
                        if c == 0:
                            if b == 0:
                                pe.wait_ge(up_read, 22 * l + (2 + CHUNKS[0]))
                            up_pair_sum(11, b)
                    pe.wait_ge(g_ready, 22 * l + (CH0[c] + CHUNKS[c]))
                    apart(pe)
                    down(0, 0, last, CHUNKS[c])
                    down(0, 1, last, CHUNKS[c])
                    down(1, 0, last, CHUNKS[c])
                    if c == 0:
                        mod_turn(l, 11)
                    down(1, 1, 0, CHUNKS[c])
                    with pe.Fori(1, 4) as i:
                        for b in range(2):
                            pe.wait_ge(split_full[b], l * SPLIT_SLOT + (DN_U[c] // 2 + 2) + i)
                            bank_read(b, i)
                            for h in range(2):
                                down(b, h, 0, CHUNKS[c])

            for j in range(2 * NT):
                kh, t = divmod(j, NT)
                if j in YT_WAITS:
                    pe.wait_ge(x_ready, 16 * DEPTH + YT_WAITS[j])
                if j >= 8:
                    pe.wait_ge(yT_read, j - 7)
                for s in range(4):
                    ins = nc.tensor.transpose(ps[:, YT_BANKS[j], s * P:(s + 1) * P],
                                              x[:, 4 * kh + s, TOK_TILES[t]:TOK_TILES[t] + P], ident[:, :])
                ins.then_inc(yT_full, 1)

        @block.scalar
        def _(act):
            A = nc.scalar.activation

            def rows(l, h):
                act.wait_ge(mod_used, 2 * h + 2 if l is None else MOD_LAYER * l + (MOD_PRE + 2 * h + 2))
                if l is None and h:
                    act.wait_ge(modT_full, h)
                A(mod_row[:, :], ps[:, mod_bank(l, h), :], ACT.Copy).then_inc(row_read, 1)

            act.wait_ge(const_ready, 1)
            act.dma_start(crow[0:KT, :], c_ctx.rearrange("(t n) -> t n", n=P)).then_inc(c_in, 16)
            act.dma_start(crow[KT:2 * KT, :], c_sample.rearrange("b (t n) -> (b t) n", n=P)).then_inc(c_in, 16)
            act.dma_start(ident[:, :], ident_in).then_inc(c_in, 16)
            act.dma_start(xin[:, 0, :], x_prompt[0]).then_inc(x_in, 16)
            act.dma_start(xin[:, 1:NT, :], x_sample[0].rearrange("(t p) n -> p t n", p=P)).then_inc(x_in, 16)
            act.wait_ge(c_in, 48)
            A(crow[:, :], crow[:, :], ACT.Silu).then_inc(silu_c, 1)
            act.wait_ge(const_ready, 2)
            small = [(rope[:, :, :, :], rope_in)]
            for src, r0, n in ((b_mod, V_BMOD, 48), (norm1_g, V_N1, KT), (norm2_g, V_N2, KT),
                               (conv_norm_g, V_CNG, 4), (subln_g, V_SUB, 1)):
                small.append((vrow[r0:r0 + n, :, 0, :], src.rearrange("l (t n) -> t l n", n=P)))
            for j in range(3):
                small.append((vrow[V_CONV + 4 * j:V_CONV + 4 * j + 4, :, 0, :],
                              conv_w[:, j, :].rearrange("l (t n) -> t l n", n=P)))
            for i, src in enumerate((lambda_q1, lambda_k1, lambda_q2, lambda_k2, q_norm_g, k_norm_g)):
                small.append((brow[0:1, i * P:(i + 1) * P], src.rearrange("(a l) n -> a (l n)", a=1)))
            assert len(small) == N_SMALL
            for dst, src in small:
                act.dma_start(dst, src).then_inc(small_in, 16)
            for l in range(DEPTH):
                fr = ffn_conv_w[l].rearrange("w (t n) -> (w t) n", n=P)
                act.dma_start(vrow[:, l, 1, :], fr[0:P, :]).then_inc(ffn_in, 16)
                act.dma_start(vrow[0:3 * V_FT - P, l, 2, :], fr[P:3 * V_FT, :]).then_inc(ffn_in, 16)
            for h in range(2):
                rows(None, h)
            act.wait_ge(lam_ready, 1)
            A(lam_s[:, :], lam_s[:, :], ACT.Exp).then_inc(lam_exp, 1)
            for k in range(KT):
                if k in (2, 5):
                    rows(None, 2 + k // 5)
                act.wait_ge(xT_read, k + 3)
                if 2 <= k < KT - 1:
                    act.wait_ge(sq_added, k - 1)
                A(sq[:, :] if k == KT - 1 else tmp[:, k % 2, :], x[:, k, :], ACT.Square).then_inc(sq_ready, 1)

            def split_hi_of(l, n, i=None, size=SLOT):
                b = n % 2
                act.wait_ge(raw_full[b], at(landed(l, raw_of(n)), i, 32))
                act.wait_ge(unit_done[b], at(l * SPLIT_SLOT + (n // 2 + 1), i))
                A(w_hi[:, b, 0:size], raw[:, b, 0:size], ACT.Copy).then_inc(hi_done[b], 1)

            split_hi_of(0, 0)
            with act.Fori(0, DEPTH) as l:
                def split_hi(n, i=None, size=SLOT):
                    split_hi_of(l, n, i, size)

                def rms(which, scale):
                    act.wait_ge(sum_ready, 3 * l + (1 + which))
                    A(rms5[:, :], rms5[:, :], ACT.Sqrt, bias=eps[:, :], scale=scale).then_inc(rms_ready, 1)

                def norm_hi(base, k, dst_src, vec):
                    act.wait_ge(tmp_ready, NORMED * l + (base + k + 1))
                    for dst, src, s in dst_src:
                        ins = A(dst, src, ACT.Identity, bias=modv[:, vec, k, s:s + 1])
                    ins.then_inc(hh_ready, 1)

                rms(0, 1.0 / D)
                split_hi(1)
                for t in range(NT):
                    for k in range(KT):
                        norm_hi(t * KT, k, [(h_hi[:, k, TOK_TILES[t]:TOK_TILES[t] + P], tmp_t[:, k, :],
                                             TILE_SEQ[t])], 0)
                        if t == 3 and k == 3:
                            rows(l, 0)

                def qk_copy(n):
                    bank = 5 if n == 0 else 5 + (n - 1) % NT % 2
                    if n == 0:
                        dst = kT[:, :, K_PAST:K_PAST + P]
                    elif n <= NT:
                        dst = qT[:, :, (n - 1) * P:n * P]
                    else:
                        t = n - 1 - NT
                        c0 = K_PROMPT if t == 0 else K_SAMPLE + (t - 1) * P
                        dst = kT[:, :, c0:c0 + P]
                    act.wait_ge(qkT_full, 11 * l + (n + 1))
                    A(dst, ps[:, bank, :].rearrange("p (s n) -> p s n", n=P), ACT.Copy).then_inc(qkT_read, 1)

                def item(p, t):
                    if t < NT - 1:
                        act.wait_ge(qkv_full, 12 * l + (4 * p + t + 1))
                    else:
                        act.wait_ge(unit_done[1], done(l, 2 * p + 1))
                    n = NT * p + t
                    A(sq[:, 0:D_ATTN], ps[:, t, :], ACT.Square).then_inc(qsq_ready, 1)
                    if n >= 2:
                        act.wait_ge(qk_ready, 2 * NT * l + (n - 1))
                    A(qraw[:, n % 2, :], ps[:, t, :], ACT.Copy).then_inc(qkv_read, 1)
                    act.wait_ge(qsum_ready, 2 * NT * l + (n + 1))
                    A(st8[:, n % 2, :], st8[:, n % 2, :], ACT.Sqrt, bias=eps[:, :], scale=1.0 / HD
                      ).then_inc(qrms_ready, 1)

                for t in range(2):
                    item(0, t)
                qk_copy(0)
                for p in range(3):
                    for t in range(NT):
                        if t == NT - 1 and p:
                            rows(l, 2 * p)
                        if p:
                            qk_copy(1 + (p - 1) * NT + t)
                    split_hi(2 * p + 2)
                    if p == 0:
                        rows(l, 1)
                    for t in range(2 if p == 0 else 0, NT):
                        if t == NT - 1 and p:
                            rows(l, 2 * p + 1)
                        if t == min(3 + p, NT - 1):
                            split_hi(2 * p + 3)
                        if p < 2:
                            item(p, t)
                            continue
                        if t < NT - 1:
                            act.wait_ge(qkv_full, 12 * l + (4 * p + t + 1))
                        else:
                            act.wait_ge(unit_done[1], done(l, 2 * p + 1))
                        A(v[:, t + (t > 0), :], ps[:, t, :], ACT.Copy).then_inc(v_ready, 1)

                for i in range(HALVES):
                    unit, tile, h = i // 4, (i % 4) // 2, i % 2
                    if i % 4 == 0 and unit:
                        split_hi(C_U + unit + 1)
                    if unit % 3 == 0:
                        if i == 12:
                            act.wait_ge(xb_read, 16 * l + 8)
                        if i % 4 == 3:
                            act.wait_ge(unit_done[unit % 2], done(l, C_U + unit))
                        else:
                            act.wait_ge(conv_full, 18 * l + (3 * unit + i % 4 + 1))
                        A(cgb[:, tile, h * HALF:(h + 1) * HALF], ps[:, h, 0:HALF], ACT.Copy).then_inc(cg_read, 1)
                    if 1 <= i < ROUNDS + 1:
                        w = P if (i - 1) % NT == 0 else N_KEY
                        act.wait_ge(aT_full, ROUNDS * l + i)
                        A(aT[:, 0:w], probsT[:, 0:w], ACT.Copy).then_inc(aT_ready, 1)
                    if i < ROUNDS:
                        w = P if i % NT == 0 else N_KEY
                        if i == 0:
                            act.wait_ge(nk_out, 16 * l + 16)
                            act.wait_ge(out_done, 16 * l + 16)
                        act.wait_ge(max_ready, ROUNDS * l + (i + 1))
                        for s in range(2):
                            ins = A(probs[:, i % 2, s, 0:w], scores[:, s * N_KEY:s * N_KEY + w], ACT.Exp,
                                    bias=nbias[:, i % 2, s:s + 1], scale=SCALE,
                                    accum_out=sums[:, i % 2, s:s + 1])
                        ins.then_inc(exp_done, 1)
                    if 2 <= i < ROUNDS + 2:
                        r = i - 2
                        act.wait_ge(pv_full, ROUNDS * l + (r + 1))
                        A(o[:, r, :], ps[:, 7, 0:VD], ACT.Copy)
                        A(junk[:, :], ps[:, 7, 0:VD], ACT.Square, accum_out=ssq_o[:, r:r + 1]
                          ).then_inc(o_read, 1)
                        if r == ROUNDS - 1:
                            act.drain()
                            A(ssq_o[:, :], ssq_o[:, :], ACT.Sqrt, bias=eps[:, :], scale=1.0 / VD
                              ).then_inc(orms_ready, 1)

                for t in range(NT):
                    c0 = TOK_TILES[t]
                    act.wait_ge(oT_full, NT * l + (t + 1))
                    A(h_hi[:, 0:4, c0:c0 + P], ps[:, OT_BANKS[t], :].rearrange("p (s n) -> p s n", n=P), ACT.Copy,
                      scale=vl[:, V_SUB:V_SUB + 1]).then_inc(oT_hi, 1)
                    if t == 2:
                        rms(1, 1.0 / D_CONV)
                split_hi(C_U + 7)
                for h in range(2):
                    for k in range(4):
                        act.wait_ge(tmp_ready, NORMED * l + (NORM1 + 4 * h + k + 1))
                        for c0, n, hf, p0, s in PIECES:
                            if hf == h:
                                ins = A(h_hi[:, 4 + k, c0:c0 + n], tmp_h[:, k, p0:p0 + n], ACT.Copy)
                        ins.then_inc(hh_ready, 1)

                def square(k, i=None):
                    act.wait_ge(x_ready, at(16 * l + (KT + k + 1), i, 2))
                    kx = at(k % KT * T, i, 2 * T)
                    A(sq[:, :], xf[:, ds(kx, T)] if i is not None else xf[:, kx:kx + T], ACT.Square
                      ).then_inc(sq_ready, 1)

                for n in range(4):
                    square(2 * n)
                    rows(l, 6 + n)
                    square(2 * n + 1)
                    if n < 3:
                        split_hi(O_U + n + 2)
                rms(2, 1.0 / D)
                rows(l, 10)
                for h in range(2):
                    for k in range(KT):
                        norm_hi(NORM1 + MIXN + KT * h, k,
                                [(h_hi[:, k, c0:c0 + n], tmp_h[:, k % 4, p0:p0 + n], s)
                                 for c0, n, hf, p0, s in PIECES if hf == h], 3)
                    if h == 0:
                        split_hi(UP_U[0] + 1)

                def up_post(c, b, i, j, nxt_size):
                    n = UP_U[c] + j
                    gate = CH0[c] + j
                    if i is not None:
                        split_hi(n + 2, i, nxt_size)
                    act.wait_ge(unit_done[b], at(done(l, n), i))
                    both = ps[:, 4 * b:4 * b + 4, 0:HALF]
                    A(ub[:, :, :].rearrange("p s (h n) -> p (s h) n", h=2), both, ACT.Copy)
                    for s in range(2):
                        w = V_FFN + V_FT + s * (V_FT // 2) + gate
                        ins = A(cen[:, s, :].rearrange("p (h n) -> p h n", h=2), both[:, 2 * s:2 * s + 2, :],
                                ACT.Copy, scale=vl[:, w:w + 1] if i is None else vl[:, ds(i * 2 + w, 1)])
                    ins.then_inc(up_read, 1)
                    if i is None:
                        split_hi(n + 2, i, nxt_size)
                    act.wait_ge(taps_ready, at(22 * l + (gate + 1), i, 2))
                    A(cen[:, 0, :], cen[:, 0, :], ACT.Silu).then_inc(silu_ready, 1)
                    act.wait_ge(gm_ready, at(22 * l + (gate + 1), i, 2))
                    A(g_hi[:, j * T:(j + 1) * T] if i is None else g_hi[:, ds(i * (2 * T) + j * T, T)],
                      gt[:, :], ACT.Copy).then_inc(gh_ready, 1)

                for c in range(2):
                    pairs = CHUNKS[c] // 2
                    with act.Fori(0, pairs - 1) as i:
                        for b in range(2):
                            up_post(c, b, i, b, SLOT)
                    for b in range(2):
                        up_post(c, b, None, 2 * (pairs - 1) + b, CHUNKS[c] * P)
                    if c == 0:
                        rows(l, 11)
                    with act.Fori(0, 3) as i:
                        for b in range(2):
                            split_hi(DN_U[c] + b + 2, i, CHUNKS[c] * P)
                            if c:
                                square(KT + b, i)
                    if c:
                        A(junk[:, 0:1], eps[:, :], ACT.Sqrt)
                    for b in range(2):
                        if c:
                            square(KT + 6 + b)
                            if b == 0:
                                split_hi_of(l + 1, 0)
                        else:
                            split_hi(DN_U[c] + 6 + b + 2)

            for j in range(2 * NT):
                act.wait_ge(yT_full, j + 1)
                kh, t = divmod(j, NT)
                A(xin[:, t, kh * 512:(kh + 1) * 512], ps[:, YT_BANKS[j], :], ACT.Copy).then_inc(yT_read, 1)

        @block.vector
        def _(dve):
            V = nc.vector

            def mod_post(l, h):
                dve.wait_ge(modT_full, h + 1 if l is None else MOD_LAYER_G * l + (MOD_PRE_G + h + 1))
                if l is not None:
                    apart(dve)
                vec = h // 2 if l is None else (h // 2 + 2) % NMOD
                c0 = vec * KT + 4 * (h % 2)
                if l is None:
                    bias = vecs[:, 0, V_BMOD + c0:V_BMOD + c0 + 4]
                elif h < 8:
                    bias = vl[:, V_BMOD + c0:V_BMOD + c0 + 4]
                else:
                    bias = vecs[:, :, :].rearrange("p l n -> p (l n)")[
                        :, ds(((DEPTH - 1) - l) * V_N + (V_BMOD + c0), 4)]
                half = modv[:, vec, 4 * (h % 2):4 * (h % 2) + 4, :]
                V.tensor_reduce(half, ps[:, mod_bank(l, h), :].rearrange("p (t q m) -> p t m q", q=4, m=QUAD)[
                    :, :, 0:2, :], axis=AX.X, op=ALU.add)
                dve.drain()
                V.tensor_tensor(half, half, bias.unsqueeze(2).broadcast_to([P, 4, 2]), ALU.add
                                ).then_inc(mod_ready, 1)

            V.memset(crow[:, :], 0.0)
            dve.drain()
            dve.sem_inc(const_ready, 1)
            V.memset(cT[:, :, :], 0.0)
            V.memset(vrow[:, :, :, :], 0.0)
            V.memset(ones[:, :], 1.0)
            V.memset(eps[:, :], EPS)
            dve.drain()
            dve.sem_inc(const_ready, 1)
            for b in range(2):
                dve.sem_inc(split_full[b], 1)
            dve.sem_inc(up_read, 2)
            dve.sem_inc(dn_read, 2)
            dve.sem_inc(x_ready, KT)
            for buf in (x, h_hi, h_lo):
                for a, e in ((0, 1), (C_SAMPLE - 1, C_SAMPLE), (T - 2, T)):
                    V.memset(buf[:, :, a:e] if buf is x else buf[:, :, a:e].bitcast(F32), 0.0)
            dve.wait_ge(setup_full, 1)
            V.tensor_copy(cT[:, :, 0:2].rearrange("p t s -> p s t"),
                          ps[:, 0, 0:2 * KT].rearrange("p (s t) -> p s t", s=2)).then_inc(setup_read, 1)
            dve.drain()
            dve.sem_inc(cT_ready, 1)
            for j in range(2):
                dve.wait_ge(xT_full, j + 1)
                V.tensor_copy(x[:, 4 * j:4 * j + 4, C_PROMPT:C_PROMPT + SEQ],
                              ps[:, j, :].rearrange("p (t n) -> p t n", n=P)).then_inc(xT_read, 1)
            for l in range(DEPTH):
                dve.wait_ge(setup_full, 2 + l)
                V.tensor_copy(vecs[:, l, :], ps[:, 2 + l, 0:V_N]).then_inc(setup_read, 1)
            dve.wait_ge(setup_full, 4)
            V.tensor_copy(lamb[:, :, :, :].rearrange("p a l n -> p (a l n)"), ps[:, 4, :]).then_inc(setup_read, 1)
            dve.wait_ge(setup_full, 5)
            V.tensor_copy(qkg[:, :, :, :].rearrange("p a l n -> p (a l n)"), ps[:, 5, 0:256]
                          ).then_inc(setup_read, 1)
            dve.drain()
            for l in range(DEPTH):
                V.tensor_scalar(vecs[:, l, V_SUB:V_SUB + 1], vecs[:, l, V_SUB:V_SUB + 1], 1.0 - LAM_INIT[l], None,
                                ALU.mult)
            lv = lamb[:, :, :, :].rearrange("p (a c) l n -> p a c (l n)", c=2)
            V.tensor_tensor(lamp[:, :, :, :].rearrange("p a l n -> p a (l n)"), lv[:, :, 0, :], lv[:, :, 1, :],
                            ALU.mult)
            dve.drain()
            V.tensor_reduce(lam_s[:, :], lamp[:, :, :, :].rearrange("p a l n -> p (a l) n"), axis=AX.X, op=ALU.add
                            ).then_inc(lam_ready, 1)
            dve.wait_ge(lam_exp, 1)
            V.tensor_tensor(neglam[:, :], lam_s[:, DEPTH:2 * DEPTH], lam_s[:, 0:DEPTH], ALU.subtract)
            dve.drain()
            for l in range(DEPTH):
                V.tensor_scalar(neglam[:, l:l + 1], neglam[:, l:l + 1], -LAM_INIT[l], None, ALU.add)
            for h in range(2):
                mod_post(None, h)
            V.memset(ssq[:, :], 0.0)

            def x_copies(ks):
                for k in ks:
                    dve.wait_ge(xT_full, k + 3)
                    V.tensor_copy(x[:, k, C_SAMPLE:C_SAMPLE + DEC], ps[:, (2 + k) % 5, :]).then_inc(xT_read, 1)

            def x_squares(ks):
                for k in ks:
                    dve.wait_ge(sq_ready, k + 1)
                    dve.drain()
                    V.tensor_tensor(ssq[:, :], ssq[:, :], tmp[:, k % 2, :], ALU.add).then_inc(
                        ssq_ready if k == KT - 2 else sq_added, 1)

            x_copies(range(0, 5))
            mod_post(None, 2)
            x_copies(range(5, KT))
            x_squares(range(0, 3))
            x_squares(range(3, 5))
            mod_post(None, 3)
            x_squares(range(5, KT - 1))

            def split_lo_of(l, n, i=None, size=SLOT):
                b = n % 2
                dve.wait_ge(hi_done[b], at(l * SPLIT_SLOT + (n // 2 + 1), i))
                V.tensor_tensor(w_lo[:, b, 0:size], raw[:, b, 0:size], w_hi[:, b, 0:size].bitcast(F32),
                                ALU.subtract).then_inc(split_full[b], 1)

            split_lo_of(0, 0)
            with dve.Fori(0, DEPTH) as l:
                def split_lo(n, i=None, size=SLOT):
                    split_lo_of(l, n, i, size)

                def gains(vec, gain_col):
                    V.scalar_tensor_tensor(out=gain[:, :, :], in0=modv[:, vec + 1, :, :], scalar=1.0,
                                           in1=vl[:, gain_col:gain_col + KT].unsqueeze(2).broadcast_to([P, KT, 2]),
                                           op0=ALU.add, op1=ALU.mult)

                def reciprocals(which):
                    dve.wait_ge(stat_full, 3 * l + (1 + which))
                    V.tensor_reduce(rms5[:, :], ps[:, B_SUM, C_SUM:C_SUM + 2 * NT].rearrange(
                        "p (a t) -> p t a", a=2), axis=AX.X, op=ALU.add).then_inc(sum_ready, 1)
                    dve.wait_ge(rms_ready, 3 * l + (1 + which))
                    V.reciprocal(rms5[:, :], rms5[:, :])
                    dve.drain()
                    for t in range(NT):
                        V.tensor_scalar(diag[:, t * P:(t + 1) * P], ident[:, :], rms5[:, t:t + 1], None, ALU.mult
                                        ).then_inc(diag_ready, 1)

                def norm_part(which, vec, base, t, slots, segs):
                    dve.wait_ge(rb_full, 3 * NT * l + (NT * which + t + 1))
                    apart(dve)
                    count = slots.shape[1]
                    for i in range(KT + LAG):
                        if i < KT:
                            if i >= count:
                                dve.drain()
                            for c, m, p0, s, h, ph in segs:
                                ins = V.scalar_tensor_tensor(
                                    out=slots[:, i % count, p0:p0 + m], in0=x[:, i, c:c + m],
                                    scalar=gain[:, i, s:s + 1], in1=ps[:, B_RMS[which][h], ph:ph + m], op0=ALU.mult,
                                    op1=ALU.mult)
                            ins.then_inc(tmp_ready, 1)
                        if i >= LAG:
                            k = i - LAG
                            dve.wait_ge(hh_ready, NORMED * l + (base + k + 1))
                            for c, m, p0, s, h, ph in segs:
                                ins = V.scalar_tensor_tensor(
                                    out=h_lo[:, k, c:c + m], in0=slots[:, k % count, p0:p0 + m],
                                    scalar=modv[:, vec, k, s:s + 1], in1=h_hi[:, k, c:c + m].bitcast(F32),
                                    op0=ALU.add, op1=ALU.subtract)
                            ins.then_inc(h_ready, 1)
                    dve.drain()

                V.tensor_copy(vl[:, :], vecs[:, :, :].rearrange("p l n -> p (l n)")[:, ds(l * V_N, V_N)])
                V.tensor_copy(qkg_l[:, :, :], qkg[:, :, ds(l, 1), :].rearrange("p a l n -> p a (l n)"))
                V.tensor_copy(neglam_l[:, :], neglam[:, ds(l, 1)])
                dve.drain()
                gains(0, V_N1)
                reciprocals(0)
                split_lo(1)
                for t in range(NT):
                    norm_part(0, 0, t * KT, 2 if t < 2 else 4, tmp_t, [(TOK_TILES[t] + off, n, off, TILE_SEQ[t], h, p0)
                                                       for tile, off, n, h, p0 in TILE_CUTS if tile == t])
                    if t == 3:
                        mod_post(l, 0)
                for a in range(2):
                    g4 = qkg_l[:, a, :].unsqueeze(1).broadcast_to([P, 4, HD])
                    V.tensor_tensor(rope_q[:, a, 0, :, :], rope[:, 0, :, :], g4, ALU.mult)
                    for m in range(2):
                        def member(ap, m):
                            return ap.rearrange("p (a m n) -> p a m n", m=2, n=16)[:, :, m, :]
                        V.tensor_tensor(member(rope_q[:, a, 1, :, :].rearrange("p t n -> p (t n)"), m),
                                        member(rope[:, 1, :, :].rearrange("p t n -> p (t n)"), m),
                                        g4.rearrange("p t (a m n) -> p t a m n", m=2, n=16)[:, :, :, 1 - m, :],
                                        ALU.mult)

                def groups(ap):
                    return ap.rearrange("p (g n) -> p g n", n=HD)

                def group_sums(n):
                    dve.wait_ge(qsq_ready, 2 * NT * l + (n + 1))
                    V.tensor_reduce(st8[:, n % 2, :], groups(sq[:, 0:D_ATTN]), axis=AX.X, op=ALU.add
                                    ).then_inc(qsum_ready, 1)

                for p in range(3):
                    if p:
                        split_lo(2 * p + 2)
                        mod_post(l, 2 * p)
                    for t in range(NT if p < 2 else 0):
                        n = NT * p + t
                        if t == 1 and p == 0:
                            split_lo(2)
                        if t == 3 + p:
                            mod_post(l, 2 * p + 1)
                            split_lo(2 * p + 3)
                        q = qraw[:, n % 2, :]
                        if t == 0:
                            group_sums(n)
                        dve.wait_ge(qrms_ready, 2 * NT * l + (n + 1))
                        V.reciprocal(st8[:, n % 2, :], st8[:, n % 2, :])
                        dve.drain()
                        V.tensor_tensor(groups(q), groups(q),
                                        st8[:, n % 2, :].unsqueeze(2).broadcast_to([P, 8, HD]), ALU.mult)
                        dve.drain()
                        if t < NT - 1:
                            group_sums(n + 1)
                        if t == 0:
                            V.tensor_tensor(groups(qn[:, 0, :]), groups(q),
                                            qkg_l[:, p, :].unsqueeze(1).broadcast_to([P, 8, HD]), ALU.mult
                                            ).then_inc(qk_ready, 1)
                            continue
                        V.tensor_tensor(groups(rt[:, 0, :]), groups(q),
                                        rope_q[:, p, 0, t - 1, :].unsqueeze(1).broadcast_to([P, 8, HD]), ALU.mult)
                        for m in range(2):
                            def member(ap, m):
                                return ap.rearrange("p (a m n) -> p a m n", m=2, n=16)[:, :, m, :]
                            sn = member(rope_q[:, p, 1, t - 1, :], m).unsqueeze(1).broadcast_to([P, 8, 2, 16])
                            V.tensor_tensor(member(rt[:, 1, :], m).rearrange("p (g a) n -> p g a n", a=2),
                                            member(q, 1 - m).rearrange("p (g a) n -> p g a n", a=2), sn, ALU.mult)
                        dve.drain()
                        V.tensor_tensor(qn[:, t, :], rt[:, 0, :], rt[:, 1, :], ALU.add).then_inc(qk_ready, 1)
                    if p == 2:
                        split_lo(7)

                mod_post(l, 5)
                for i in range(HALVES):
                    unit, tile, h = i // 4, (i % 4) // 2, i % 2
                    pair, kind = divmod(unit, 3)
                    if 1 <= i < ROUNDS + 1:
                        r = (i - 1) % 2
                        w = P if (i - 1) % NT == 0 else N_KEY
                        dve.wait_ge(exp_done, ROUNDS * l + i)
                        V.reciprocal(rec[:, r, :], sums[:, r, :])
                        dve.drain()
                        V.tensor_tensor(rec[:, r, 1:2], rec[:, r, 1:2], neglam_l[:, :], ALU.mult)
                        V.tensor_scalar(probs[:, r, 0, 0:w], probs[:, r, 0, 0:w], rec[:, r, 0:1], None, ALU.mult)
                        dve.drain()
                        V.scalar_tensor_tensor(out=probs[:, r, 0, 0:w], in0=probs[:, r, 1, 0:w],
                                               scalar=rec[:, r, 1:2], in1=probs[:, r, 0, 0:w], op0=ALU.mult,
                                               op1=ALU.add).then_inc(a_ready, 1)
                    if i == ROUNDS + 2:
                        dve.wait_ge(orms_ready, l + 1)
                        V.reciprocal(ssq_o[:, :], ssq_o[:, :])
                        dve.drain()
                        V.tensor_tensor(o[:, :, :], o[:, :, :],
                                        ssq_o[:, :].unsqueeze(2).broadcast_to([P, ROUNDS, VD]),
                                        ALU.mult).then_inc(on_ready, 1)
                    if kind:
                        if i % 4 == 3:
                            dve.wait_ge(unit_done[unit % 2], done(l, C_U + unit))
                        else:
                            dve.wait_ge(conv_full, 18 * l + (3 * unit + i % 4 + 1))
                        cols = slice(h * HALF, (h + 1) * HALF)
                    z = cgb[:, tile, :]
                    if kind == 1:
                        dve.wait_ge(cg_read, 8 * l + (4 * pair + i % 4 + 1))
                        V.tensor_tensor(z[:, cols], ps[:, h, 0:HALF], z[:, cols], ALU.mult).then_inc(xb_read, 1)
                        if h:
                            def cw(j):
                                w = V_CONV + 4 * j + 2 * pair + tile
                                return vl[:, w:w + 1]
                            dve.drain()
                            V.tensor_scalar(tap[:, tile, :], z, cw(1), None, ALU.mult)
                            for j, off in ((0, 0), (2, 2)):
                                dve.drain()
                                V.scalar_tensor_tensor(out=tap[:, tile, 1:T - 1], in0=z[:, off:off + T - 2],
                                                       scalar=cw(j), in1=tap[:, tile, 1:T - 1], op0=ALU.mult,
                                                       op1=ALU.add)
                            dve.drain()
                    elif kind == 2:
                        k = 2 * pair + tile
                        V.tensor_tensor(y[:, k, cols], ps[:, h, 0:HALF], tap[:, tile, cols], ALU.mult
                                        ).then_inc(xb_read, 1)
                        if h:
                            dve.drain()
                            if k == 0:
                                V.tensor_tensor(ssq[:, :], y[:, k, :], y[:, k, :], ALU.mult)
                            else:
                                ins = V.tensor_tensor(sq[:, :], y[:, k, :], y[:, k, :], ALU.mult)
                                if k == 3:
                                    ins.then_inc(ssq_ready, 1)
                                dve.drain()
                                if k < 3:
                                    V.tensor_tensor(ssq[:, :], ssq[:, :], sq[:, :], ALU.add)
                                    dve.drain()
                    if i < ROUNDS:
                        w = P if i % NT == 0 else N_KEY
                        dve.wait_ge(qk_full, ROUNDS * l + (i + 1))
                        V.reduce_max(mx[:, i % 2, :],
                                     scores[:, 0:2 * N_KEY].rearrange("p (s n) -> p s n", s=2)[:, :, 0:w], AX.X)
                        dve.drain()
                        V.tensor_scalar(nbias[:, i % 2, :], mx[:, i % 2, :], -SCALE, None, ALU.mult
                                        ).then_inc(max_ready, 1)
                    if i % 4 == 0 and unit:
                        split_lo(C_U + unit + 1)

                for t in range(NT):
                    c0 = TOK_TILES[t]
                    dve.wait_ge(oT_hi, NT * l + (t + 1))
                    V.scalar_tensor_tensor(out=h_lo[:, 0:4, c0:c0 + P],
                                           in0=ps[:, OT_BANKS[t], :].rearrange("p (s n) -> p s n", n=P),
                                           scalar=vl[:, V_SUB:V_SUB + 1],
                                           in1=h_hi[:, 0:4, c0:c0 + P].bitcast(F32),
                                           op0=ALU.mult, op1=ALU.subtract).then_inc(oT_read, 1)
                    if t == 2:
                        reciprocals(1)
                split_lo(C_U + 7)
                for h in range(2):
                    dve.wait_ge(rb_full, 3 * NT * l + (NT + (NT if h else 3)))
                    apart(dve)
                    segs = [(c0, n, p0) for c0, n, hf, p0, s in PIECES if hf == h]
                    for i in range(4 + LAG):
                        if i < 4:
                            for c0, n, p0 in segs:
                                ins = V.scalar_tensor_tensor(out=tmp_h[:, i, p0:p0 + n], in0=y[:, i, c0:c0 + n],
                                                             scalar=vl[:, V_CNG + i:V_CNG + i + 1],
                                                             in1=ps[:, B_RMS[1][h], p0:p0 + n],
                                                             op0=ALU.mult, op1=ALU.mult)
                            ins.then_inc(tmp_ready, 1)
                        if i >= LAG:
                            k = i - LAG
                            dve.wait_ge(hh_ready, NORMED * l + (NORM1 + 4 * h + k + 1))
                            for c0, n, p0 in segs:
                                ins = V.tensor_tensor(h_lo[:, 4 + k, c0:c0 + n], tmp_h[:, k, p0:p0 + n],
                                                      h_hi[:, 4 + k, c0:c0 + n].bitcast(F32), ALU.subtract)
                            ins.then_inc(mix_ready, 1)
                    dve.drain()

                def add_to_x(bank, vec, k, i, signal):
                    for c0, n, h, p0, s in PIECES:
                        g0 = (vec * KT + k) * 2 + s
                        gate = mf[:, g0:g0 + 1] if i is None else mf[:, ds(i * 4 + g0, 1)]
                        a = k * T + c0
                        xs = xf[:, a:a + n] if i is None else xf[:, ds(i * (2 * T) + a, n)]
                        ins = V.scalar_tensor_tensor(out=xs, in0=ps[:, bank + h, p0:p0 + n], scalar=gate, in1=xs,
                                                     op0=ALU.mult, op1=ALU.add)
                    ins.then_inc(signal, 1)

                def add_square(k, i, last):
                    dve.wait_ge(sq_ready, at(16 * l + (KT + k + 1), i, 2))
                    ins = V.tensor_tensor(ssq[:, :], ssq[:, :], sq[:, :], ALU.add)
                    if last:
                        ins.then_inc(ssq_ready, 1)
                    else:
                        dve.drain()

                V.memset(ssq[:, :], 0.0)
                for k in range(KT):
                    n = O_U + k // 2
                    if k % 2 == 0 and k:
                        mod_post(l, 5 + k // 2)
                    if k % 2:
                        dve.wait_ge(unit_done[n % 2], done(l, n))
                    else:
                        dve.wait_ge(out_full, 4 * l + (k // 2 + 1))
                    add_to_x(2 * (k % 2), 2, k, None, x_ready)
                    if k < KT - 1:
                        add_square(k, None, k == KT - 2)
                    if k % 2 and k < KT - 1:
                        split_lo(n + 2)
                mod_post(l, 9)
                gains(3, V_N2)
                reciprocals(2)
                for h in range(2):
                    norm_part(2, 3, NORM1 + MIXN + KT * h, 2 + 2 * h, tmp_h,
                              [(c0, n, p0, s, h, p0) for c0, n, hf, p0, s in PIECES if hf == h])
                    if h == 0:
                        split_lo(UP_U[0] + 1)
                        mod_post(l, 10)

                def up_post(c, b, i, j, nxt_size):
                    n, gate = UP_U[c] + j, CH0[c] + j
                    if i is not None:
                        split_lo(n + 2, i, nxt_size)
                    dve.wait_ge(up_read, at(22 * l + (gate + 3), i, 2))
                    for tap_i, off in ((0, 0), (2, 2)):
                        for s in range(2):
                            w = V_FFN + tap_i * V_FT + s * (V_FT // 2) + gate
                            ins = V.scalar_tensor_tensor(
                                out=cen[:, s, 1:T - 1], in0=ub[:, s, off:off + T - 2],
                                scalar=vl[:, w:w + 1] if i is None else vl[:, ds(i * 2 + w, 1)],
                                in1=cen[:, s, 1:T - 1], op0=ALU.mult, op1=ALU.add)
                        if tap_i == 0:
                            dve.drain()
                    ins.then_inc(taps_ready, 1)
                    if i is None:
                        split_lo(n + 2, i, nxt_size)
                    dve.wait_ge(silu_ready, at(22 * l + (gate + 1), i, 2))
                    V.tensor_tensor(gt[:, :], cen[:, 0, :], cen[:, 1, :], ALU.mult).then_inc(gm_ready, 1)
                    dve.wait_ge(gh_ready, at(22 * l + (gate + 1), i, 2))
                    dst, hi = ((g_lo[:, j * T:(j + 1) * T], g_hi[:, j * T:(j + 1) * T]) if i is None else
                               (g_lo[:, ds(i * (2 * T) + j * T, T)], g_hi[:, ds(i * (2 * T) + j * T, T)]))
                    V.tensor_tensor(dst, gt[:, :], hi.bitcast(F32), ALU.subtract).then_inc(g_ready, 1)

                for c in range(2):
                    pairs = CHUNKS[c] // 2
                    with dve.Fori(0, pairs - 1) as i:
                        for b in range(2):
                            up_post(c, b, i, b, SLOT)
                    for b in range(2):
                        up_post(c, b, None, 2 * (pairs - 1) + b, CHUNKS[c] * P)
                    if c:
                        V.memset(ssq[:, :], 0.0)
                        dve.drain()

                    def down_post(b, i, j, meanwhile=None):
                        dve.wait_ge(unit_done[b], at(done(l, DN_U[c] + j), i))
                        add_to_x(4 * b, 5, j, i, x_ready if c else dn_read)
                        if meanwhile is not None:
                            split_lo(meanwhile, i, CHUNKS[c] * P)
                        if c and j < KT - 1:
                            add_square(KT + j, i, j == KT - 2)

                    if c == 0:
                        mod_post(l, 11)
                    with dve.Fori(0, 3) as i:
                        for b in range(2):
                            down_post(b, i, b, DN_U[c] + b + 2)
                    for b in range(2):
                        down_post(b, None, 6 + b)
                        if c and b == 0:
                            split_lo_of(l + 1, 0)
                        if not c:
                            split_lo(DN_U[c] + 6 + b + 2)


def _tables():
    half = HD // 2
    nf = HD // 4
    inv = (10000.0 ** (-np.arange(nf, dtype=np.float32) / nf)).astype(np.float32)
    tok = np.arange(DEC)
    ang = np.concatenate([np.tile(pos.astype(np.float32)[:, None] * inv[None], (1, 2))
                          for pos in (tok // GRID_W, tok % GRID_W)], axis=1)
    sign = np.tile(np.repeat(np.float32([-1, 1]), nf), 2)
    both = np.stack([np.cos(ang), np.sin(ang) * sign]).astype(np.float32)
    assert both.shape == (2, DEC, 2 * half)
    return {"ident": np.eye(P, dtype=np.float32),
            "rope": np.ascontiguousarray(both.reshape(2, DEC // P, P, HD).transpose(2, 0, 1, 3))}


_INS = ['x_prompt', 'x_sample', 'cache_k', 'cache_v', 'c', 'c_ctx', 'w_mod', 'b_mod', 'norm1_g', 'w_in', 'q_norm_g',
        'k_norm_g', 'lambda_q1', 'lambda_k1', 'lambda_q2', 'lambda_k2', 'subln_g', 'conv_w', 'conv_norm_g', 'w_out',
        'norm2_g', 'w_up', 'ffn_conv_w', 'w_down']
_OUTS = [(1, SEQ, D), (1, DEC, D), (1, DEPTH, SEQ, NH, 2, HD), (1, DEPTH, SEQ, NH, VD)]


def kernel(**inputs):
    import concourse.bacc as _bacc
    from concourse.bass_utils import run_bass_kernel_spmd as _run

    nc = _bacc.Bacc("TRN2", target_bir_lowering=False, num_devices=1)
    tables = _tables()
    arrays, args = {}, []
    for name in _INS + ["ident", "rope"]:
        a = np.ascontiguousarray(inputs[name] if name in inputs else tables[name])
        arrays[f"in_{name}_dram"] = a
        args.append(nc.dram_tensor(f"in_{name}_dram", a.shape, mybir.dt.from_np(a.dtype), kind="ExternalInput").ap())
    for i, shape in enumerate(_OUTS):
        args.append(nc.dram_tensor(f"out_{i}_dram", shape, F32, kind="ExternalOutput").ap())
    hybrid_step(nc, *args)
    r = _run(nc, [arrays], core_ids=[0])
    return tuple(r.results[0][f"out_{i}_dram"] for i in range(len(_OUTS)))
```
